# Optimizing a Trainium2 kernel written in Bass

```python
import math
import jax, jax.numpy as jnp
from jax import lax
import numpy as np

D_MODEL = 1024
BATCH = 1
SEQ = 512
DEPTH = 1

HEAD_DIM = 64
N_HEADS_A = 8
N_HEADS_B = 8
N_HEADS = N_HEADS_A + N_HEADS_B
D_A = N_HEADS_A * HEAD_DIM
D_B = N_HEADS_B * HEAD_DIM
D_MIX = D_A + D_B
N_IDX_HEADS = 4
IDX_DIM = 64
TOPK_MAX = 256
DIL_PATTERNS = ((128, 1), (512, 4), (2048, 16))
BLOCK = 128
N_BUCKETS = 32
MAX_DISTANCE = 128
EPS = 1e-6
SPLITS = (D_A, D_A, D_A, D_A, N_IDX_HEADS * IDX_DIM, IDX_DIM, N_IDX_HEADS, D_B, D_B, D_B, D_B)
D_IN = sum(SPLITS)


def rms_norm(x, g):
    xf = x.astype(jnp.float32)
    y = xf * lax.rsqrt(jnp.mean(xf * xf, axis=-1, keepdims=True) + EPS) * g.astype(jnp.float32)
    return y.astype(x.dtype)

def rel_bucket(dist):
    max_exact = N_BUCKETS // 2
    d = jnp.maximum(dist, 0)
    df = jnp.maximum(d, 1).astype(jnp.float32)
    large = max_exact + (jnp.log(df / max_exact) / math.log(MAX_DISTANCE / max_exact)
                         * (N_BUCKETS - max_exact)).astype(jnp.int32)
    large = jnp.minimum(large, N_BUCKETS - 1)
    return jnp.where(d < max_exact, d, large)

def dsa_attention(q, k, v, q_idx, k_idx, w_idx, bias_table):
    b, s, h, dh = q.shape
    topk = min(TOPK_MAX, s // 4)
    nblk = s // BLOCK
    scale = HEAD_DIM ** -0.5
    idx_scale = (N_IDX_HEADS * IDX_DIM) ** -0.5
    key_pos = jnp.arange(s)

    def to_blocks(a):
        return jnp.moveaxis(a.reshape(b, nblk, BLOCK, *a.shape[2:]), 1, 0)

    def block_fn(args):
        qb, qib, wb, start = args
        q_pos = start + jnp.arange(BLOCK)
        rel = jnp.einsum('bqhd,bsd->bqhs', qib, k_idx)
        score = jnp.einsum('bqhs,bqh->bqs', jax.nn.relu(rel).astype(jnp.float32),
                           wb.astype(jnp.float32)) * idx_scale
        causal = key_pos[None, :] <= q_pos[:, None]
        score = jnp.where(causal[None], score, -jnp.inf)
        top_val, top_idx = lax.top_k(score, topk)
        valid = jnp.isfinite(top_val)
        k_sel = jax.vmap(lambda kk, ii: kk[ii])(k, top_idx)
        v_sel = jax.vmap(lambda vv, ii: vv[ii])(v, top_idx)
        logits = jnp.einsum('bqhd,bqkhd->bqhk', qb, k_sel).astype(jnp.float32) * scale
        bucket = rel_bucket(q_pos[None, :, None] - top_idx)
        bias = jnp.moveaxis(bias_table[bucket], -1, -2).astype(jnp.float32)
        logits = jnp.where(valid[:, :, None, :], logits + bias, -jnp.inf)
        p = jax.nn.softmax(logits, axis=-1)
        return jnp.einsum('bqhk,bqkhd->bqhd', p.astype(v.dtype), v_sel)

    starts = jnp.arange(nblk) * BLOCK
    out = lax.map(block_fn, (to_blocks(q), to_blocks(q_idx), to_blocks(w_idx), starts))
    return jnp.moveaxis(out, 0, 1).reshape(b, s, h, dh)

def dilated_pattern(q, k, v, window, dilation, bias_table):
    b, s, h, dh = q.shape
    seg = dilation * BLOCK
    p_len = -(-s // seg) * seg
    pad = p_len - s
    n_sub = p_len // dilation
    nb = n_sub // BLOCK
    steps = window // dilation
    scale = HEAD_DIM ** -0.5

    def to_segments(a):
        a = jnp.pad(a, ((0, 0), (0, pad), (0, 0), (0, 0)))
        a = a.reshape(b, n_sub, dilation, h, dh).transpose(2, 0, 1, 3, 4)
        return a.reshape(dilation, b, nb, BLOCK, h, dh)

    def band(a):
        prev = jnp.pad(a, ((0, 0), (0, 0), (1, 0), (0, 0), (0, 0), (0, 0)))[:, :, :-1]
        return jnp.concatenate([prev, a], axis=3)

    def seg_major(a):
        return jnp.moveaxis(a, 2, 1).reshape(dilation * nb, b, *a.shape[3:])

    qs, ks, vs = to_segments(q), to_segments(k), to_segments(v)
    qs, kb, vb = seg_major(qs), seg_major(band(ks)), seg_major(band(vs))
    blk_ids = jnp.arange(dilation * nb) % nb

    a_idx = jnp.arange(BLOCK)[:, None]
    c_idx = jnp.arange(2 * BLOCK)[None, :]
    diff = a_idx - c_idx + BLOCK
    band_mask = (diff >= 0) & (diff <= steps)
    bias = jnp.transpose(bias_table[rel_bucket(diff * dilation)], (2, 0, 1)).astype(jnp.float32)

    def seg_fn(args):
        qq, kk, vv, blk = args
        key_ok = (blk * BLOCK - BLOCK + jnp.arange(2 * BLOCK)) >= 0
        mask = band_mask & key_ok[None, :]
        logits = jnp.einsum('bqhd,bkhd->bhqk', qq, kk).astype(jnp.float32) * scale + bias
        logits = jnp.where(mask, logits, -jnp.inf)
        m = jnp.max(logits, axis=-1)
        pexp = jnp.exp(logits - m[..., None])
        den = jnp.sum(pexp, axis=-1)
        num = jnp.einsum('bhqk,bkhd->bqhd', pexp, vv.astype(jnp.float32))
        return jnp.swapaxes(m, 1, 2), jnp.swapaxes(den, 1, 2), num

    m, den, num = lax.map(seg_fn, (qs, kb, vb, blk_ids))

    def unseg(a):
        rest = a.shape[3:]
        a = a.reshape(dilation, nb, b, BLOCK, *rest)
        a = jnp.moveaxis(jnp.moveaxis(a, 0, 3), 0, 1)
        return a.reshape(b, p_len, *rest)[:, :s]

    return unseg(m), unseg(den), unseg(num)

def dilated_attention(q, k, v, bias_table):
    stats = [dilated_pattern(q, k, v, w, d, bias_table) for (w, d) in DIL_PATTERNS]
    m_all = jnp.stack([st[0] for st in stats])
    wts = jnp.exp(m_all - jnp.max(m_all, axis=0))
    den = sum(wts[i] * stats[i][1] for i in range(len(stats)))
    num = sum(wts[i][..., None] * stats[i][2] for i in range(len(stats)))
    return (num / den[..., None]).astype(q.dtype)

def first_inputs(seed: int = 0) -> dict:
    key = jax.random.key(seed)
    ks = jax.random.split(key, 9)
    x = jax.random.normal(ks[0], (BATCH, SEQ, D_MODEL), jnp.float32)
    norm_gain = 1.0 + 0.02 * jax.random.normal(ks[1], (DEPTH, D_MODEL), jnp.float32)
    w_in = jax.random.normal(ks[2], (DEPTH, D_MODEL, D_IN), jnp.float32) * D_MODEL ** -0.5
    w_out = jax.random.normal(ks[3], (DEPTH, D_MIX, D_MODEL), jnp.float32) * D_MIX ** -0.5
    rel_bias = 0.1 * jax.random.normal(ks[4], (N_BUCKETS, N_HEADS), jnp.float32)
    q_norm_a = 1.0 + 0.02 * jax.random.normal(ks[5], (DEPTH, HEAD_DIM), jnp.float32)
    k_norm_a = 1.0 + 0.02 * jax.random.normal(ks[6], (DEPTH, HEAD_DIM), jnp.float32)
    q_norm_b = 1.0 + 0.02 * jax.random.normal(ks[7], (DEPTH, HEAD_DIM), jnp.float32)
    k_norm_b = 1.0 + 0.02 * jax.random.normal(ks[8], (DEPTH, HEAD_DIM), jnp.float32)
    return {"x": x, "norm_gain": norm_gain, "w_in": w_in, "w_out": w_out, "rel_bias": rel_bias,
            "q_norm_a": q_norm_a, "k_norm_a": k_norm_a, "q_norm_b": q_norm_b, "k_norm_b": k_norm_b}

def first_block(x, norm_gain, w_in, w_out, rel_bias, q_norm_a, k_norm_a, q_norm_b, k_norm_b):
    b, s, _ = x.shape
    split_points = np.cumsum(SPLITS)[:-1].tolist()
    bias_a = rel_bias[:, :N_HEADS_A]
    bias_b = rel_bias[:, N_HEADS_A:]
    for layer in range(DEPTH):
        xn = rms_norm(x, norm_gain[layer])
        proj = jnp.einsum('bsd,de->bse', xn, w_in[layer])
        qa, ka, va, za, qi, ki, wi, qb, kb, vb, zb = jnp.split(proj, split_points, axis=-1)
        qa = rms_norm(qa.reshape(b, s, N_HEADS_A, HEAD_DIM), q_norm_a[layer])
        ka = rms_norm(ka.reshape(b, s, N_HEADS_A, HEAD_DIM), k_norm_a[layer])
        va = va.reshape(b, s, N_HEADS_A, HEAD_DIM)
        qi = qi.reshape(b, s, N_IDX_HEADS, IDX_DIM)
        qb = rms_norm(qb.reshape(b, s, N_HEADS_B, HEAD_DIM), q_norm_b[layer])
        kb = rms_norm(kb.reshape(b, s, N_HEADS_B, HEAD_DIM), k_norm_b[layer])
        vb = vb.reshape(b, s, N_HEADS_B, HEAD_DIM)
        a_out = dsa_attention(qa, ka, va, qi, ki, wi, bias_a)
        b_out = dilated_attention(qb, kb, vb, bias_b)
        mixed = jnp.concatenate([a_out.reshape(b, s, D_A) * jax.nn.silu(za),
                                 b_out.reshape(b, s, D_B) * jax.nn.silu(zb)], axis=-1)
        x = x + jnp.einsum('bse,ed->bsd', mixed, w_out[layer])
    return x


N_HEADS_2 = 8
N_KV = 2
GROUP = N_HEADS_2 // N_KV
ROT_DIM = HEAD_DIM // 4
ROPE_THETA = 500000.0
CMP_BLOCK = 32
CMP_STRIDE = 16
CMP_HIDDEN = 4 * HEAD_DIM
SEL_BLOCK = 64
SEL_TOPK = 16
WINDOW = 512
Q_BLOCK = 128
N_NSA_BRANCHES = 3
ATTN_WIDTH = N_HEADS_2 * HEAD_DIM
KV_WIDTH = N_KV * HEAD_DIM
POOL_WIDTH = 512
POOL_WINDOWS = (2, 4, 8, 16)
POOL_GROUP = POOL_WIDTH // len(POOL_WINDOWS)
D_FF = 4 * D_MODEL
IN_SIZES = (ATTN_WIDTH, 6 * KV_WIDTH, N_NSA_BRANCHES * N_HEADS_2, POOL_WIDTH, 2 * D_MODEL)
IN_WIDTH = sum(IN_SIZES)
NEG_INF = -1e30
FORCE_SCORE = 1e4


def rms_norm_2(x, g):
    xf = x.astype(jnp.float32)
    y = xf * lax.rsqrt(jnp.mean(xf * xf, axis=-1, keepdims=True) + EPS)
    return (y * g.astype(jnp.float32)).astype(x.dtype)

def rope(x, pos):
    inv = ROPE_THETA ** (-jnp.arange(0, ROT_DIM, 2, dtype=jnp.float32) / ROT_DIM)
    ang = pos.astype(jnp.float32)[:, None] * inv
    cos, sin = jnp.cos(ang), jnp.sin(ang)
    xr = x[..., :ROT_DIM].astype(jnp.float32)
    x1, x2 = xr[..., :ROT_DIM // 2], xr[..., ROT_DIM // 2:]
    rot = jnp.concatenate([x1 * cos - x2 * sin, x2 * cos + x1 * sin], axis=-1)
    return jnp.concatenate([rot.astype(x.dtype), x[..., ROT_DIM:]], axis=-1)

def masked_softmax(s, mask):
    s = jnp.where(mask, s.astype(jnp.float32), NEG_INF)
    e = jnp.exp(s - jnp.max(s, axis=-1, keepdims=True)) * mask
    return e / jnp.maximum(jnp.sum(e, axis=-1, keepdims=True), 1e-30)

def cmp_to_sel_matrix(S):
    n_cmp = (S - CMP_BLOCK) // CMP_STRIDE + 1
    n_sel = S // SEL_BLOCK
    cs = np.arange(n_cmp)[:, None] * CMP_STRIDE
    js = np.arange(n_sel)[None, :] * SEL_BLOCK
    ov = np.clip(np.minimum(cs + CMP_BLOCK, js + SEL_BLOCK) - np.maximum(cs, js), 0, None)
    return jnp.asarray((ov / CMP_STRIDE).astype(np.float32))

def compress_blocks(k, pe, w1, w2):
    B, G, S, dh = k.shape
    ratio = CMP_BLOCK // CMP_STRIDE
    chunks = k.reshape(B, G, S // CMP_STRIDE, CMP_STRIDE, dh)
    n_cmp = S // CMP_STRIDE - ratio + 1
    blocks = jnp.concatenate([chunks[:, :, j:j + n_cmp] for j in range(ratio)], axis=3)
    flat = (blocks + pe).reshape(B, G, n_cmp, CMP_BLOCK * dh)
    return jax.nn.gelu(flat @ w1) @ w2

def nsa_attention(q_flat, kv_flat, gate_logits, pe_k, pe_v, ck_w1, ck_w2, cv_w1, cv_w2):
    B, S, _ = q_flat.shape
    dt = q_flat.dtype
    scale = HEAD_DIM ** -0.5
    t = jnp.arange(S)
    q = rope(q_flat.reshape(B, S, N_KV, GROUP, HEAD_DIM).transpose(0, 2, 3, 1, 4), t)

    def kv_heads(a):
        return a.reshape(B, S, N_KV, HEAD_DIM).transpose(0, 2, 1, 3)

    kc, vc, ks, vs, kw, vw = [kv_heads(a) for a in jnp.split(kv_flat, 6, axis=-1)]
    ks = rope(ks, t)
    kw = rope(kw, t)

    n_cmp = (S - CMP_BLOCK) // CMP_STRIDE + 1
    pos_c = jnp.arange(n_cmp) * CMP_STRIDE + CMP_BLOCK - 1
    k_cmp = rope(compress_blocks(kc, pe_k, ck_w1, ck_w2), pos_c)
    v_cmp = compress_blocks(vc, pe_v, cv_w1, cv_w2)
    s = jnp.einsum('bgrsd,bgcd->bgrsc', q, k_cmp) * scale
    p_cmp = masked_softmax(s, pos_c[None, :] <= t[:, None])
    o_cmp = jnp.einsum('bgrsc,bgcd->bgrsd', p_cmp.astype(dt), v_cmp)

    n_sel = S // SEL_BLOCK
    top = min(SEL_TOPK, n_sel)
    imp = jnp.einsum('bgrsc,cj->bgsj', p_cmp, cmp_to_sel_matrix(S))
    blk = jnp.arange(n_sel)[None, :]
    cur = (t // SEL_BLOCK)[:, None]
    imp = jnp.where(blk > cur, -FORCE_SCORE, imp)
    imp = jnp.where((blk == 0) | (blk == cur) | (blk == cur - 1), FORCE_SCORE, imp)
    _, sel_idx = lax.top_k(imp, top)

    nq = S // Q_BLOCK
    q_blocks = q.reshape(B, N_KV, GROUP, nq, Q_BLOCK, HEAD_DIM).transpose(3, 0, 1, 2, 4, 5)
    idx_blocks = sel_idx.reshape(B, N_KV, nq, Q_BLOCK, top).transpose(2, 0, 1, 3, 4)
    ks_blk = ks.reshape(B, N_KV, n_sel, SEL_BLOCK, HEAD_DIM)
    vs_blk = vs.reshape(B, N_KV, n_sel, SEL_BLOCK, HEAD_DIM)
    pad = ((0, 0), (0, 0), (WINDOW, 0), (0, 0))
    kw_pad = jnp.pad(kw, pad)
    vw_pad = jnp.pad(vw, pad)
    bi = jnp.arange(B)[:, None, None, None]
    gi = jnp.arange(N_KV)[None, :, None, None]
    offs = jnp.arange(SEL_BLOCK)
    band = WINDOW + Q_BLOCK

    def step(args):
        i, qb, ib = args
        qpos = i * Q_BLOCK + jnp.arange(Q_BLOCK)
        k_sel = ks_blk[bi, gi, ib].reshape(B, N_KV, Q_BLOCK, top * SEL_BLOCK, HEAD_DIM)
        v_sel = vs_blk[bi, gi, ib].reshape(B, N_KV, Q_BLOCK, top * SEL_BLOCK, HEAD_DIM)
        kpos = (ib[..., None] * SEL_BLOCK + offs).reshape(B, N_KV, Q_BLOCK, top * SEL_BLOCK)
        s_sel = jnp.einsum('bgrqd,bgqkd->bgrqk', qb, k_sel) * scale
        p_sel = masked_softmax(s_sel, (kpos <= qpos[:, None])[:, :, None])
        o_sel = jnp.einsum('bgrqk,bgqkd->bgrqd', p_sel.astype(dt), v_sel)
        k_win = lax.dynamic_slice_in_dim(kw_pad, i * Q_BLOCK, band, axis=2)
        v_win = lax.dynamic_slice_in_dim(vw_pad, i * Q_BLOCK, band, axis=2)
        wpos = i * Q_BLOCK - WINDOW + jnp.arange(band)
        dist = qpos[:, None] - wpos[None, :]
        wmask = (dist >= 0) & (dist < WINDOW) & (wpos >= 0)[None, :]
        s_win = jnp.einsum('bgrqd,bgkd->bgrqk', qb, k_win) * scale
        p_win = masked_softmax(s_win, wmask)
        o_win = jnp.einsum('bgrqk,bgkd->bgrqd', p_win.astype(dt), v_win)
        return o_sel, o_win

    o_sel, o_win = lax.map(step, (jnp.arange(nq), q_blocks, idx_blocks))
    o_sel = o_sel.transpose(1, 2, 3, 0, 4, 5).reshape(B, N_KV, GROUP, S, HEAD_DIM)
    o_win = o_win.transpose(1, 2, 3, 0, 4, 5).reshape(B, N_KV, GROUP, S, HEAD_DIM)

    g = jax.nn.sigmoid(gate_logits).reshape(B, S, N_NSA_BRANCHES, N_KV, GROUP).transpose(2, 0, 3, 4, 1)[..., None]
    o = g[0] * o_cmp + g[1] * o_sel + g[2] * o_win
    return o.transpose(0, 3, 1, 2, 4).reshape(B, S, ATTN_WIDTH)

def pool_mixer(u, w_pool, pool_scale):
    B, S, _ = u.shape
    uf = u.astype(jnp.float32)
    csp = jnp.concatenate([jnp.zeros((B, 1, POOL_WIDTH), jnp.float32), jnp.cumsum(uf, axis=1)], axis=1)
    t = jnp.arange(S)
    outs = []
    for gidx, w in enumerate(POOL_WINDOWS):
        lo, hi = gidx * POOL_GROUP, (gidx + 1) * POOL_GROUP
        c = csp[..., lo:hi]
        lower = jnp.concatenate([jnp.zeros((B, w - 1, POOL_GROUP), jnp.float32), c[:, :S - w + 1]], axis=1)
        cnt = jnp.minimum(t + 1, w).astype(jnp.float32)[:, None]
        outs.append((c[:, 1:] - lower) / cnt - uf[..., lo:hi])
    pooled = jnp.stack(outs, axis=2).astype(u.dtype)
    mixed = jnp.einsum('bsgc,gcd->bsgd', pooled, w_pool).reshape(B, S, POOL_WIDTH)
    return mixed * pool_scale

def hybrid_layer(x, norm_mix, w_in, cmp_pe_k, cmp_pe_v, cmp_k_w1, cmp_k_w2, cmp_v_w1, cmp_v_w2,
                 w_branch_attn, pool_w, pool_scale, w_branch_pool, w_out, norm_mlp, w_ff1, w_ff2):
    h = rms_norm_2(x, norm_mix)
    proj = h @ w_in
    q_flat, kv_flat, g_attn, u_pool, g_merge = jnp.split(proj, np.cumsum(IN_SIZES)[:-1].tolist(), axis=-1)
    a = nsa_attention(q_flat, kv_flat, g_attn, cmp_pe_k, cmp_pe_v, cmp_k_w1, cmp_k_w2, cmp_v_w1, cmp_v_w2) @ w_branch_attn
    b = pool_mixer(u_pool, pool_w, pool_scale) @ w_branch_pool
    ga, gb = jnp.split(jax.nn.sigmoid(g_merge), 2, axis=-1)
    x = x + (ga * a + gb * b) @ w_out
    h = rms_norm_2(x, norm_mlp)
    return x + jnp.square(jax.nn.relu(h @ w_ff1)) @ w_ff2

def second_inputs(seed: int = 0) -> dict:
    key = jax.random.key(seed)
    ks = jax.random.split(key, 20)
    f32 = jnp.float32

    def nrm(k, shape, fan_in):
        return jax.random.normal(k, shape, f32) * (fan_in ** -0.5)

    def gain(k, shape):
        return 1.0 + 0.05 * jax.random.normal(k, shape, f32)

    L = DEPTH
    return {
        "x": jax.random.normal(ks[0], (BATCH, SEQ, D_MODEL), f32),
        "norm_mix": gain(ks[1], (L, D_MODEL)),
        "w_in": nrm(ks[2], (L, D_MODEL, IN_WIDTH), D_MODEL),
        "cmp_pe_k": 0.02 * jax.random.normal(ks[3], (L, CMP_BLOCK, HEAD_DIM), f32),
        "cmp_pe_v": 0.02 * jax.random.normal(ks[4], (L, CMP_BLOCK, HEAD_DIM), f32),
        "cmp_k_w1": nrm(ks[5], (L, CMP_BLOCK * HEAD_DIM, CMP_HIDDEN), CMP_BLOCK * HEAD_DIM),
        "cmp_k_w2": nrm(ks[6], (L, CMP_HIDDEN, HEAD_DIM), CMP_HIDDEN),
        "cmp_v_w1": nrm(ks[7], (L, CMP_BLOCK * HEAD_DIM, CMP_HIDDEN), CMP_BLOCK * HEAD_DIM),
        "cmp_v_w2": nrm(ks[8], (L, CMP_HIDDEN, HEAD_DIM), CMP_HIDDEN),
        "w_branch_attn": nrm(ks[9], (L, ATTN_WIDTH, D_MODEL), ATTN_WIDTH),
        "pool_w": nrm(ks[10], (L, len(POOL_WINDOWS), POOL_GROUP, POOL_GROUP), POOL_GROUP),
        "pool_scale": 1.0 + 0.1 * jax.random.normal(ks[11], (L, POOL_WIDTH), f32),
        "w_branch_pool": nrm(ks[12], (L, POOL_WIDTH, D_MODEL), POOL_WIDTH),
        "w_out": nrm(ks[13], (L, D_MODEL, D_MODEL), D_MODEL),
        "norm_mlp": gain(ks[14], (L, D_MODEL)),
        "w_ff1": nrm(ks[15], (L, D_MODEL, D_FF), D_MODEL),
        "w_ff2": nrm(ks[16], (L, D_FF, D_MODEL), D_FF),
        "norm_final": gain(ks[17], (D_MODEL,)),
    }

def second_block(x, norm_mix, w_in, cmp_pe_k, cmp_pe_v, cmp_k_w1, cmp_k_w2, cmp_v_w1, cmp_v_w2,
              w_branch_attn, pool_w, pool_scale, w_branch_pool, w_out, norm_mlp, w_ff1, w_ff2,
              norm_final):
    for l in range(DEPTH):
        x = hybrid_layer(x, norm_mix[l], w_in[l], cmp_pe_k[l], cmp_pe_v[l], cmp_k_w1[l], cmp_k_w2[l],
                         cmp_v_w1[l], cmp_v_w2[l], w_branch_attn[l], pool_w[l], pool_scale[l],
                         w_branch_pool[l], w_out[l], norm_mlp[l], w_ff1[l], w_ff2[l])
    return rms_norm_2(x, norm_final)


def setup_inputs(seed=0):
    out = dict(first_inputs(seed))
    for name, value in second_inputs(seed + 1).items():
        if name != "x":
            out[name + "_2"] = value
    return out


def reference(
    x, norm_gain, w_in, w_out, rel_bias, q_norm_a, k_norm_a, q_norm_b, k_norm_b, norm_mix_2,
    w_in_2, cmp_pe_k_2, cmp_pe_v_2, cmp_k_w1_2, cmp_k_w2_2, cmp_v_w1_2, cmp_v_w2_2,
    w_branch_attn_2, pool_w_2, pool_scale_2, w_branch_pool_2, w_out_2, norm_mlp_2, w_ff1_2,
    w_ff2_2, norm_final_2,
):
    x = first_block(
        x, norm_gain, w_in, w_out, rel_bias, q_norm_a, k_norm_a, q_norm_b, k_norm_b,
    )
    return second_block(
        x, norm_mix_2, w_in_2, cmp_pe_k_2, cmp_pe_v_2, cmp_k_w1_2, cmp_k_w2_2, cmp_v_w1_2,
        cmp_v_w2_2, w_branch_attn_2, pool_w_2, pool_scale_2, w_branch_pool_2, w_out_2,
        norm_mlp_2, w_ff1_2, w_ff2_2, norm_final_2,
    )


_drawn_inputs = setup_inputs


def setup_inputs(seed=0):
    import zlib

    import numpy as np

    out = dict(_drawn_inputs(seed))
    spreads = {}
    factors = {'norm_gain': 5.57,
     'rel_bias': 6.114,
     'q_norm_a': 8.0,
     'k_norm_a': 8.0,
     'q_norm_b': 8.0,
     'k_norm_b': 8.0,
     'cmp_pe_k_2': 64.0,
     'cmp_pe_v_2': 64.0,
     'norm_mix_2': 8.0,
     'cmp_k_w1_2': 8.0,
     'cmp_k_w2_2': 8.0,
     'cmp_v_w1_2': 8.0,
     'cmp_v_w2_2': 8.0,
     'w_branch_attn_2': 8.0,
     'pool_scale_2': 25.301,
     'norm_mlp_2': 37.083}
    for name, (base, spread) in spreads.items():
        noise = np.random.default_rng([zlib.crc32(name.encode()), seed]).standard_normal(out[name].shape)
        drawn = base * np.exp(spread * noise) if base else spread * noise
        out[name] = __import__('jax').numpy.asarray(drawn.astype(out[name].dtype))
    for name, factor in factors.items():
        out[name] = (out[name] * factor).astype(out[name].dtype)
    return out
```

```python
from contextlib import ExitStack

import numpy as np

import concourse.bass as bass
from concourse import mybir

F32 = mybir.dt.float32
ALU = mybir.AluOpType
ACT = mybir.ActivationFunctionType
AX = mybir.AxisListType

P = 128
S = 512
D = 1024
NT = S // P
KC = D // P
HD = 64
NH = 8
EPS = 1e-6
SCALE = HD ** -0.5
TOPK = min(256, S // 4)
N_BUCKETS = 32
IDX_HEADS = 4
IDX_SCALE = (IDX_HEADS * HD) ** -0.5
NEG = -1e30
FUTURE = -3.0e38
TAKEN = -3.4e38
BIG = 3.0e38
DFF = 4 * D
VEC = S + P

QA, KA, VA, ZA, QI, KI, WI, QB, KB, VB, ZB = np.cumsum([0, 512, 512, 512, 512, 256, 64, 4, 512, 512, 512]).tolist()
Q2, KV2, KWVG, POOL, MERGE = 0, 512, 1024, 1304, 1816
GATES = 24
G2 = 2
GROUP = NH // G2
ROT = 8
CMP_BLOCK, CMP_STRIDE = 32, 16
NC = (S - CMP_BLOCK) // CMP_STRIDE + 1
NCP = NC + 1
POOL_WINDOWS = (2, 4, 8, 16)
THETA = 500000.0

C_ID, C_DIAG, C_STRIP, C_COS, C_SIN, C_CADD, C_C01, C_PCOS, C_PSIN, C_INV, C_END = np.cumsum(
    [0, P, P, S, NT * ROT, NT * ROT, NT * NCP, NT * NCP, ROT, ROT, 4 * 16]).tolist()
V_G1, V_G2, V_G3, V_QB, V_KB, V_QA, V_KA, V_PS, V_PEK, V_PEV, V_END = np.cumsum(
    [0, KC, KC, KC, 1, 1, 1, 1, 4, 16, 16]).tolist()

COPIES = 16
RING = 3
SLOT = 8 * 512


def shape_constants():
    c = np.zeros((P, C_END), np.float32)
    p = np.arange(P)[:, None]
    c[:, C_ID:C_ID + P] = np.eye(P)
    c[:, C_DIAG:C_DIAG + P] = np.where(np.arange(P)[None, :] > p, FUTURE, 0)
    c[:, C_STRIP:C_STRIP + S] = np.where((S - P) + p - np.arange(S)[None, :] < 0, NEG, 0)
    inv = THETA ** (-np.arange(0, 2 * ROT, 2, dtype=np.float32) / np.float32(2 * ROT))
    t = np.arange(S, dtype=np.float32)
    ang = (t[:, None] * inv.astype(np.float32)).astype(np.float32)
    tiled = lambda a: a.reshape(NT, P, -1).transpose(1, 0, 2).reshape(P, -1)
    c[:, C_COS:C_COS + NT * ROT] = tiled(np.cos(ang))
    c[:, C_SIN:C_SIN + NT * ROT] = tiled(np.sin(ang))
    pos = np.arange(NC) * CMP_STRIDE + CMP_BLOCK - 1
    seen = np.zeros((S, NCP), bool)
    seen[:, :NC] = pos[None, :] <= np.arange(S)[:, None]
    c[:, C_CADD:C_CADD + NT * NCP] = tiled(np.where(seen, 0, NEG))
    c[:, C_C01:C_C01 + NT * NCP] = tiled(seen.astype(np.float32))
    pang = (pos.astype(np.float32)[:, None] * inv.astype(np.float32)).astype(np.float32)
    c[:NC, C_PCOS:C_PCOS + ROT] = np.cos(pang)
    c[:NC, C_PSIN:C_PSIN + ROT] = np.sin(pang)
    for g, w in enumerate(POOL_WINDOWS):
        c[:, C_INV + 16 * g:C_INV + 16 * g + 16] = 1.0 / np.minimum(np.arange(16) + 1, w)
    d = (S - 1) - np.arange(VEC)
    df = np.maximum(d, 1).astype(np.float32)
    half = N_BUCKETS // 2
    large = half + (np.log(df / np.float32(half)) / np.float32(np.log(128 / half)) * np.float32(half)).astype(np.int32)
    bucket = np.where(d < half, np.maximum(d, 0), np.minimum(large, N_BUCKETS - 1))
    onehot = (bucket[None, :] == np.arange(N_BUCKETS)[:, None]).astype(np.float32)
    times = ((d <= 128).astype(int) + (d % 4 == 0) + (d % 16 == 0)) * (d >= 0)
    add = np.zeros((2 * NH, VEC), np.float32)
    add[:NH] = np.where(d >= 0, 0, NEG)
    add[NH:] = np.where(times > 0, np.log(np.maximum(times, 1)), NEG)
    return c, onehot, add


def weight_groups(w):
    def cols(a, c, n, at=0, width=512):
        return (at, n, width, a[:, c:c + n].rearrange("(k p) n -> p k n", p=P))

    def whole(a, k, n):
        return (0, n, n, a.rearrange("(k p) n -> p k n", p=P))

    w1, w2 = w["w_in"], w["w_in_2"]
    groups = [("idx", [cols(w1, QI, 320), cols(w1, KI, 64, 320), cols(w1, WI, IDX_HEADS, 384)])]
    groups += [(n, [cols(w1, c, 512)]) for n, c in
               (("zb", ZB), ("vb", VB), ("va", VA), ("kb", KB), ("qb", QB), ("ka", KA), ("qa", QA), ("za", ZA))]
    groups += [(f"wo{n}", [cols(w["w_out"], 512 * n, 512)]) for n in range(2)]
    groups += [("kv2", [cols(w2, KV2, 512)]), ("kwvg", [cols(w2, KWVG, 280)]), ("q2", [cols(w2, Q2, 512)])]
    groups += [("ck", None), ("cv", None)]
    groups += [("pool", [cols(w2, POOL, 512)])]
    groups += [(f"ga{n}", [cols(w2, MERGE + 512 * n, 512)]) for n in range(2)]
    groups += [(f"gb{n}", [cols(w2, MERGE + D + 512 * n, 512)]) for n in range(2)]
    groups += [("ba", [whole(w["w_branch_attn_2"], 4, D)]), ("bp", [whole(w["w_branch_pool_2"], 4, D)])]
    groups += [(f"w2o{n}", [cols(w["w_out_2"], 512 * n, 512)]) for n in range(2)]
    groups += [(f"f1_{n}", [cols(w["w_ff1_2"], 512 * n, 512)]) for n in range(8)]
    groups += [(f"f2_{n}_{k}", [cols(w["w_ff2_2"][k * D:(k + 1) * D, :], 512 * n, 512)]) for n in range(2) for k in range(4)]
    return groups


def build(nc, w, out):
    groups = weight_groups(w)
    number = {name: n for n, (name, _) in enumerate(groups)}
    copies = nc.dram_tensor("bias_copies", (COPIES, 2 * NH, VEC), F32).ap()

    A1 = [("qi", 0), ("qi", 1), ("ki", 0), ("wi", 0)]
    A1 += [("zb", i) for i in range(NT)]
    A1 += [("rel", i, h) for i in range(1, NT) for h in range(IDX_HEADS)]
    for g in ("vb", "va", "kb", "qb", "ka", "qa", "za"):
        A1 += [(g, i) for i in range(NT)]
    A2 = [(g, i) for g in ("kv2", "kwvg", "q2") for i in range(NT)]
    A2 += [("pool", g) for g in range(4)]
    A2 += [("hidk", 0), ("hidv", 0)]
    A2 += [("ga", e) for e in range(4)]
    A2 += [("kcmp", 0), ("vcmp", 0)]
    A2 += [("ga", e) for e in range(4, 8)] + [("gb", e) for e in range(8)]
    A2 += [("pm", g) for g in range(4)]
    A3 = [("ff", c) for c in range(DFF // P)]
    AT = {tile: n for n, tile in enumerate(A1 + A2 + A3)}
    A1_END, A2_END = len(A1), len(A1) + len(A2)

    T1 = [("h1", i, c) for i in range(NT) for c in range(2)]
    T1 += [(g, c) for g in ("kb", "qb", "ka", "qa") for c in range(4)]
    T2 = [("mx", i, c) for i in range(NT) for c in range(2)]
    T2 += [("h2", i, c) for i in range(NT) for c in range(2)]
    T2 += [("kv", n, g) for n in range(4) for g in range(G2)]
    T2 += [("q2", c) for c in range(4)]
    T2 += [("kcT", 0)] + [("ec", n) for n in range(2)]
    T3 = [("at", i) for i in range(NT)] + [("h3", i, c) for i in range(NT) for c in range(2)]
    TT = {tile: n for n, tile in enumerate(T1 + T2 + T3)}

    steps1 = [(i, br, h) for br in ("b", "a") for i in range(NT) for h in range(NH)]
    steps2 = [(i, br, h) for i in range(NT) for br in ("s", "w") for h in range(NH)]
    combos = [t for t, (i, br, h) in enumerate(steps1) if br == "a" and i > 0]
    NS = len(steps1)

    with ExitStack() as ctx:
        def sb(name, shape):
            return ctx.enter_context(nc.sbuf_tensor(name, shape, F32))

        def sem(name):
            return ctx.enter_context(nc.semaphore(name))

        bank = [ctx.enter_context(nc.psum_tensor(f"bank{b}", [P, 512], F32)) for b in range(8)]

        x = sb("x", [P, NT, D])
        hT = sb("hT", [P, KC * 512])
        wring = sb("wring", [P, RING, SLOT])
        consts = sb("consts", [P, C_END])
        small = sb("small", [P, V_END])
        junk = sb("junk", [P, D])
        stats = sb("stats", [P, 512])
        ARENA = 28900
        arena = sb("arena", [P, ARENA])
        used = [0]

        def region(n, at=None):
            if at is not None:
                return arena[:, at:at + n]
            used[0] += n
            return arena[:, used[0] - n:used[0]]

        hTk = hT[:, :].rearrange("p (k s) -> p k s", k=KC)
        qkT = {g: region(4 * S).rearrange("p (c s) -> p c s", c=4) for g in ("kb", "qb", "ka", "qa")}
        v1 = {g: region(NT * 512).rearrange("p (i n) -> p i n", i=NT) for g in ("vb", "va")}
        zz = region(NT * D).rearrange("p (i n) -> p i n", i=NT)
        raw_at = used[0]
        raw = [region(NT * 512).rearrange("p (i n) -> p i n", i=NT) for _ in range(2)]
        xn1 = region(NT * D, raw_at).rearrange("p (i n) -> p i n", i=NT)
        strips = region(2 * NH * S).rearrange("p (h u) -> p h u", h=2 * NH)
        scores = qkT["qa"].rearrange("p c s -> p (c s)")
        spans = {1: slice(0, 256), 2: slice(256, 640), 3: slice(640, 1152)}
        score_of = {i: scores[:, r] for i, r in spans.items()}
        mask_of = {i: raw[0].rearrange("p i n -> p (i n)")[:, r] for i, r in spans.items()}
        qiT = qkT["kb"][:, 0:2, :]
        kiT = qkT["kb"][:, 2, :]
        rels = [qkT["kb"][:, 3, :], qkT["qb"][:, 0, :]]
        vec = qkT["qb"][0:2 * NH, 1:3, :].rearrange("p a b -> p (a b)")[:, 0:VEC]
        bucket_sb = qkT["ka"][0:N_BUCKETS, 0:2, :].rearrange("p a b -> p (a b)")[:, 0:VEC]
        add_sb = qkT["ka"][0:2 * NH, 2:4, :].rearrange("p a b -> p (a b)")[:, 0:VEC]
        table_sb = qkT["qa"][0:N_BUCKETS, 3, 0:2 * NH]
        assert used[0] <= ARENA, used
        logits = [hT[:, 512 * n:512 * n + 512] for n in range(3)]
        probsT = [hT[:, 1536 + 512 * n:2048 + 512 * n] for n in range(2)]
        combo = [hT[:, 2560 + 512 * n:3072 + 512 * n] for n in range(2)]
        used[0] = 0
        q2 = region(NT * 512)
        dup = region(4 * NT * G2 * 2 * HD).rearrange("p (m i g r d) -> p m i g r d", m=4, i=NT, g=G2, r=2)
        xn2 = region(NT * D, 0).rearrange("p (i n) -> p i n", i=NT)
        v2 = {g: region(NT * G2 * HD).rearrange("p (i n) -> p i n", i=NT) for g in ("s", "w")}
        gates = region(NT * GATES).rearrange("p (i n) -> p i n", i=NT)
        q2T = region(4 * S).rearrange("p (c s) -> p c s", c=4)
        kT2 = {g: region(G2 * S).rearrange("p (g s) -> p g s", g=G2) for g in ("s", "w")}
        uT = region(4 * S).rearrange("p (g s) -> p g s", g=4)
        ptmp = [region(S) for _ in range(2)]
        gaT = region(KC * S).rearrange("p (e s) -> p e s", e=KC)
        gbT = region(KC * S).rearrange("p (e s) -> p e s", e=KC)
        blk = {m: region(G2 * NC * 16).rearrange("p (g c j) -> p g c j", g=G2, c=NC) for m in range(2)}
        hidk = region(2 * G2 * NCP).rearrange("p (m g c) -> p m g c", m=2, g=G2)
        hidv = region(2 * G2 * 4 * NCP).rearrange("p (m g r c) -> p m g r c", m=2, g=G2, r=4)
        kcn = region(G2 * 2 * HD).rearrange("p (g r d) -> p g r d", g=G2, r=2)
        kcT = region(G2 * NCP).rearrange("p (g c) -> p g c", g=G2)
        vdiag = region(G2 * 4 * HD).rearrange("p (g n) -> p g n", g=G2)
        pmT = uT
        attn = region(NT * 512).rearrange("p (i n) -> p i n", i=NT)
        ccw = region(2 * 2 * HD).rearrange("p (m k d) -> p m k d", m=2, k=2)
        poolw = region(4 * P).rearrange("p (g d) -> p g d", g=4)
        assert used[0] <= ARENA, used
        ec = dup[:, 0, :, :, :, :].rearrange("p i g r d -> p (i g r d)")
        ecT = dup[:, 1, :, :, :, :].rearrange("p i g r d -> p (i g r d)")
        ec_of = [ec.rearrange("p (m r c) -> p m r c", r=2, c=NCP)[:, :, n, :] for n in range(2)]
        aT = hT[:, 0:2048].rearrange("p (k s) -> p k s", k=4)
        ffT = region((DFF // P) * S, 0).rearrange("p (c s) -> p c s", c=DFF // P)
        xn3 = gbT.rearrange("p e s -> p (e s)").rearrange("p (i n) -> p i n", i=NT)
        gfin = region(D, ARENA - D)

        ident = consts[:, C_ID:C_ID + P]
        strip0 = consts[:, C_STRIP:C_STRIP + S]
        ss = stats[:, 0:12]
        rs = stats[:, 12:24]
        ssq = stats[:, 24:56]
        rsq = stats[:, 56:88]
        wi = stats[:, 88:104].rearrange("p (i h) -> p i h", i=NT)
        top8 = stats[:, 104:112]
        den = stats[:, 112:112 + NS]
        negm = stats[:, 176:176 + NS]
        gr = stats[:, 240:248]
        cm = stats[:, 248:280]
        cden = stats[:, 280:312]
        ssf = stats[:, 312:316]
        rsf = stats[:, 316:320]
        den2 = stats[:, 320:320 + NS]
        rope_tmp = [junk[:, 256 * n:256 * n + 256] for n in range(4)]

        x_in = sem("x_in")
        consts_in = sem("consts_in")
        table_in = sem("table_in")
        small2_in = sem("small2_in")
        gfin_in = sem("gfin_in")
        w_in = [sem(f"w_in{r}") for r in range(RING)]
        w_used = sem("w_used")
        vec_full = sem("vec_full")
        vec_done = sem("vec_done")
        vec_out = sem("vec_out")
        strips_in = sem("strips_in")
        ss_done = sem("ss_done")
        ms_done = sem("ms_done")
        sq_done = sem("sq_done")
        xn_done = sem("xn_done")
        a_full = sem("a_full")
        a_free = sem("a_free")
        t_full = sem("t_full")
        t_free = sem("t_free")
        r_full = sem("r_full")
        r_free = sem("r_free")
        rel_free = sem("rel_free")
        raw_ms = sem("raw_ms")
        raw_sq = sem("raw_sq")
        raw_done = sem("raw_done")
        masks_done = sem("masks_done")
        combo_done = sem("combo_done")
        s_full = sem("s_full")
        l_done = sem("l_done")
        e_done = sem("e_done")
        pt_full = sem("pt_full")
        pt_free = sem("pt_free")
        pv_done = sem("pv_done")
        o_free = sem("o_free")
        zeroed = sem("zeroed")
        rope_done = sem("rope_done")
        kcn_done = sem("kcn_done")
        pooled = sem("pooled")
        pool_chain = sem("pool_chain")
        cs_full = sem("cs_full")
        cl_done = sem("cl_done")
        ce_done = sem("ce_done")
        cp_done = sem("cp_done")
        co_full = sem("co_full")
        co_free = sem("co_free")
        mix_done = sem("mix_done")
        relu_done = sem("relu_done")
        dve_step = sem("dve_step")
        y_done = sem("y_done")
        out_done = sem("out_done")

        def slot(name, width=512):
            s = number[name] % RING
            return wring[:, s, :].rearrange("p (k n) -> p k n", n=width)

        R_BRANCH, R_OUT2, R_FF = 2 * NT, 2 * NT + 2 * KC, 4 * NT + 2 * KC

        def last_use(name):
            if name.startswith("f2_"):
                half, kg = int(name[3]), int(name[5])
                return (w_used, 3 * half + kg + 1) if kg < 3 else (r_full, R_FF + NT * (half + 1))
            if name[:2] in ("wo", "ba", "bp") or name.startswith("w2o"):
                return r_full, {"wo": R_BRANCH, "ba": R_OUT2, "bp": R_OUT2, "w2": R_FF}[name[:2]] - \
                    (1 if name in ("wo0", "w2o0", "ba") else 0)
            last = {"idx": ("wi", 0), "ck": ("hidk", 0), "cv": ("hidv", 0), "ga0": ("ga", 3), "ga1": ("ga", 7),
                    "gb0": ("gb", 3), "gb1": ("gb", 7)}.get(name, (name, NT - 1))
            if name.startswith("f1_"):
                last = ("ff", 4 * int(name[3:]) + 3)
            return a_full, AT[last] + 1

        block = ctx.enter_context(nc.Block())

        @block.sync
        def _(sp):
            for i in range(NT):
                sp.dma_start(x[:, i, :], w["x"][0, i * P:(i + 1) * P, :]).then_inc(x_in, 16)
            sp.dma_start(consts[:, :], w["consts"]).then_inc(consts_in, 16)
            sp.dma_start(small[:, :], w["small"]).then_inc(consts_in, 16)
            sp.dma_start(bucket_sb, w["onehot"]).then_inc(table_in, 16)
            sp.dma_start(add_sb, w["vec_add"]).then_inc(table_in, 16)
            sp.dma_start(table_sb, w["rel_bias"]).then_inc(table_in, 16)
            for n, (name, parts) in enumerate(groups):
                if n >= RING:
                    done, value = last_use(groups[n - RING][0])
                    sp.wait_ge(done, value)
                if parts is None:
                    src = w["cmp_k_w1_2" if name == "ck" else "cmp_v_w1_2"]
                    for half in range(2):
                        rows = src[half * D:(half + 1) * D, :].rearrange("(j d) n -> d j n", d=HD)
                        sp.dma_start(slot(name, 256)[half * HD:(half + 1) * HD, :, :], rows).then_inc(w_in[n % RING], 16)
                else:
                    for at, cols, width, view in parts:
                        sp.dma_start(slot(name, width)[:, :, at:at + cols], view).then_inc(w_in[n % RING], 16)
                if name == "kwvg":
                    sp.wait_ge(zeroed, 1)
                    for m, a in enumerate(("cmp_k_w2_2", "cmp_v_w2_2")):
                        sp.dma_start(ccw[:, m, :, :], w[a].rearrange("(k p) d -> p k d", p=P)).then_inc(small2_in, 16)
                    sp.dma_start(poolw, w["pool_w_2"].rearrange("g c d -> c g d")).then_inc(small2_in, 16)
                if name == "f1_3":
                    sp.wait_ge(xn_done, 3 * NT)
                    sp.dma_start(gfin, w["norm_final_2"].to_broadcast([P, D])).then_inc(gfin_in, 16)
            for i in range(NT):
                sp.wait_ge(y_done, i + 1)
                sp.dma_start(out[0, i * P:(i + 1) * P, :], x[:, i, :]).then_inc(out_done, 16)
            sp.wait_ge(out_done, 16 * NT)

        def arrived(eng, name):
            n = number[name]
            total = sum(2 if g[1] is None else len(g[1]) for g in groups[n % RING:n + 1:RING])
            eng.wait_ge(w_in[n % RING], 16 * total)

        @block.tensor
        def _(pe):
            mm = nc.tensor.matmul

            def a_bank(tile):
                n = AT[tile]
                if n >= 4 and n not in (A1_END, A2_END):
                    pe.wait_ge(a_free, n - 3)
                return bank[n % 4]

            def t_bank(tile):
                n = TT[tile]
                if n >= 2:
                    pe.wait_ge(t_free, n - 1)
                return bank[4 + n % 2]

            def nat_tiles(name, width=512):
                arrived(pe, name)
                for i in range(NT):
                    b = a_bank((name, i))
                    for k in range(KC):
                        last = mm(b[:, 0:width], hTk[:, k, i * P:(i + 1) * P], slot(name)[:, k, 0:width],
                                  start=(k == 0), stop=(k == KC - 1))
                    last.then_inc(a_full, 1)

            def t_tiles(name, tile, c, lhs, act=hTk, kc=KC, width=512):
                b = a_bank(tile)
                for k in range(kc):
                    last = mm(b[:, :], slot(name, width)[:, k, c * P:(c + 1) * P], act[:, k, :],
                              start=(k == 0), stop=(k == kc - 1))
                last.then_inc(a_full, 1)

            def h_transposes(name, xn, base, tiles=range(NT)):
                for i in tiles:
                    pe.wait_ge(xn_done, base + i + 1)
                    for c in range(2):
                        b = t_bank((name, i, c))
                        for k in range(4):
                            last = nc.tensor.transpose(b[:, k * P:(k + 1) * P],
                                                       xn[:, i, (4 * c + k) * P:(4 * c + k + 1) * P], ident)
                        last.then_inc(t_full, 1)

            def raw_transposes(n, g):
                pe.wait_ge(raw_done, n + 1)
                for c in range(4):
                    b = t_bank((g, c))
                    for i in range(NT):
                        last = nc.tensor.transpose(b[:, i * P:(i + 1) * P], raw[n % 2][:, i, c * P:(c + 1) * P], ident)
                    last.then_inc(t_full, 1)

            def attention(steps, base, query, key, value):
                n_steps = len(steps)
                for t in range(n_steps + 3):
                    if t < n_steps:
                        i, br, h = steps[t]
                        if t >= 3:
                            pe.wait_ge(l_done, base + t - 2)
                        mm(bank[t % 3][:, 0:(i + 1) * P], query(br, h)[:, i * P:(i + 1) * P],
                           key(br, h)[:, 0:(i + 1) * P], start=True, stop=True).then_inc(s_full, 1)
                    u = t - 2
                    if 0 <= u < n_steps:
                        i = steps[u][0]
                        pe.wait_ge(e_done, base + u + 1)
                        if u >= 2:
                            pe.wait_ge(pt_free, base + u - 1)
                        for j in range(i + 1):
                            last = nc.tensor.transpose(bank[3 + u % 2][:, j * P:(j + 1) * P],
                                                       logits[u % 3][:, j * P:(j + 1) * P], ident)
                        last.then_inc(pt_full, 1)
                    u = t - 3
                    if u >= 0:
                        i, br, h = steps[u]
                        o = u // NH
                        pe.wait_ge(pt_free, base + u + 1)
                        if u % NH == 0 and o >= 3:
                            pe.wait_ge(o_free, base // NH + o - 2)
                        for j in range(i + 1):
                            last = mm(bank[5 + o % 3][:, h * HD:(h + 1) * HD], probsT[u % 2][:, j * P:(j + 1) * P],
                                      value(br, h)[:, j, :], start=(j == 0), stop=(j == i))
                        last.then_inc(pv_done, 1)

            pe.wait_ge(table_in, 48)
            mm(bank[6][0:2 * NH, 0:512], table_sb, bucket_sb[:, 0:512], start=True, stop=True)
            mm(bank[7][0:2 * NH, 0:P], table_sb, bucket_sb[:, 512:VEC], start=True, stop=True).then_inc(vec_full, 1)

            pe.wait_ge(consts_in, 32)
            h_transposes("h1", xn1, 0)

            arrived(pe, "idx")
            pe.wait_ge(t_free, 2 * NT)
            for c in range(2):
                t_tiles("idx", ("qi", c), c, None)
            t_tiles("idx", ("ki", 0), 2, None)
            b = a_bank(("wi", 0))
            for i in range(NT):
                for k in range(KC):
                    last = mm(b[:, i * IDX_HEADS:(i + 1) * IDX_HEADS], hTk[:, k, i * P:(i + 1) * P],
                              slot("idx")[:, k, 384:384 + IDX_HEADS], start=(k == 0), stop=(k == KC - 1))
            last.then_inc(a_full, 1)
            nat_tiles("zb")
            pe.wait_ge(a_free, 3)
            for i in range(1, NT):
                for h in range(IDX_HEADS):
                    r = slice((h % 2) * HD, (h % 2) * HD + HD)
                    mm(a_bank(("rel", i, h))[:, 0:(i + 1) * P], qiT[r, h // 2, i * P:(i + 1) * P],
                       kiT[r, 0:(i + 1) * P], start=True, stop=True).then_inc(a_full, 1)
            for g in ("vb", "va", "kb", "qb"):
                nat_tiles(g)
            raw_transposes(0, "kb")
            nat_tiles("ka")
            raw_transposes(1, "qb")
            nat_tiles("qa")
            raw_transposes(2, "ka")
            nat_tiles("za")
            raw_transposes(3, "qa")

            pe.wait_ge(a_free, A1_END)
            pe.wait_ge(t_free, len(T1))
            rows = lambda h: slice((h % 2) * HD, (h % 2) * HD + HD)
            attention(steps1, 0, lambda br, h: qkT["q" + br][rows(h), h // 2, :], lambda br, h: qkT["k" + br][rows(h), h // 2, :],
                      lambda br, h: v1["v" + br][:, :, h * HD:(h + 1) * HD])

            pe.wait_ge(pt_free, NS)
            pe.wait_ge(o_free, NS // NH)
            for i in range(NT):
                for c in range(2):
                    b = t_bank(("mx", i, c))
                    for k in range(4):
                        last = nc.tensor.transpose(b[:, k * P:(k + 1) * P], zz[:, i, (4 * c + k) * P:(4 * c + k + 1) * P], ident)
                    last.then_inc(t_full, 1)

            def residual(names, src, r0, t_need):
                for i in range(NT):
                    pe.wait_ge(t_free, t_need + 2 * (i + 1) if t_need is not None else 1)
                    for n in range(2):
                        if i == 0:
                            arrived(pe, names[n])
                        r = r0 + 2 * i + n
                        if r - r0 >= 4:
                            pe.wait_ge(r_free, r - 3)
                        for k in range(KC):
                            last = mm(bank[r % 4][:, :], src[:, k, i * P:(i + 1) * P], slot(names[n])[:, k, :],
                                      start=(k == 0), stop=(k == KC - 1))
                        last.then_inc(r_full, 1)

            residual(("wo0", "wo1"), hTk, 0, TT[("mx", 0, 0)])

            h_transposes("h2", xn2, NT)
            pe.wait_ge(t_free, TT[("h2", NT - 1, 1)] + 1)
            pe.wait_ge(r_free, 2 * NT)
            nat_tiles("kv2")
            nat_tiles("kwvg", 280)
            nat_tiles("q2")

            pe.wait_ge(a_free, AT[("kwvg", NT - 1)] + 1)
            for n in range(4):
                if n == 2:
                    pe.wait_ge(rope_done, 1)
                for g in range(G2):
                    b = t_bank(("kv", n, g))
                    for i in range(NT):
                        last = nc.tensor.transpose(b[:, i * P:(i + 1) * P],
                                                   dup[:, n, i, g, :, :].rearrange("p r d -> p (r d)"), ident)
                    last.then_inc(t_full, 1)

            arrived(pe, "pool")
            for g in range(4):
                t_tiles("pool", ("pool", g), g, None)
            pe.wait_ge(t_free, TT[("kv", 1, G2 - 1)] + 1)
            for m, name in enumerate(("ck", "cv")):
                arrived(pe, name)
                b = a_bank((("hidk", "hidv")[m], 0))
                for c in range(2):
                    for j in range(16):
                        last = mm(b[:, 64 * c:64 * c + G2 * NC], slot(name, 256)[:, j, c * P:(c + 1) * P],
                                  blk[m][:, :, :, j].rearrange("p g c -> p (g c)"), start=(j == 0), stop=(j == 15))
                last.then_inc(a_full, 1)
            pe.wait_ge(rope_done, 2)
            for c in range(4):
                b = t_bank(("q2", c))
                for i in range(NT):
                    last = nc.tensor.transpose(b[:, i * P:(i + 1) * P], q2[:, i * 512 + c * P:i * 512 + (c + 1) * P], ident)
                last.then_inc(t_full, 1)
            arrived(pe, "ga0")
            for e in range(4):
                t_tiles("ga0", ("ga", e), e, None)
            pe.wait_ge(small2_in, 48)
            pe.wait_ge(a_free, AT[("hidv", 0)] + 1)
            b = a_bank(("kcmp", 0))
            for g in range(G2):
                for m in range(2):
                    last = mm(b[0:NC, g * HD:(g + 1) * HD], hidk[:, m, g, 0:NC], ccw[:, 0, m, :], start=(m == 0), stop=(m == 1))
            last.then_inc(a_full, 1)
            b = a_bank(("vcmp", 0))
            for g in range(G2):
                for m in range(2):
                    last = mm(b[:, g * HD:(g + 1) * HD], hidv[:, m, g, :, :].rearrange("p r c -> p (r c)"), ccw[:, 1, m, :],
                              start=(m == 0), stop=(m == 1))
            last.then_inc(a_full, 1)
            arrived(pe, "ga1")
            for e in range(4, 8):
                t_tiles("ga1", ("ga", e), e - 4, None)
            pe.wait_ge(kcn_done, 1)
            b = t_bank(("kcT", 0))
            for g in range(G2):
                last = nc.tensor.transpose(b[:, g * NCP:g * NCP + NC], kcn[0:NC, g, :, :].rearrange("p r d -> p (r d)"),
                                           ident[0:NC, 0:NC])
            last.then_inc(t_full, 1)
            arrived(pe, "gb0")
            for e in range(4):
                t_tiles("gb0", ("gb", e), e, None)
            pe.wait_ge(t_free, TT[("kcT", 0)] + 1)
            for n in range(2):
                for i in range(NT):
                    for m in range(NH // 2):
                        at = (i * NH // 2 + m) * NCP
                        last = mm(bank[6 + n][:, at:at + NCP], q2T[rows(n), m, i * P:(i + 1) * P],
                                  kcT[rows(n), m // 2, :], start=True, stop=True)
                last.then_inc(cs_full, 1)
            arrived(pe, "gb1")
            for e in range(4, 8):
                t_tiles("gb1", ("gb", e), e - 4, None)
            for n in range(2):
                pe.wait_ge(cp_done, 2)
                b = t_bank(("ec", n))
                for k in range(4):
                    last = nc.tensor.transpose(b[:, k * P:(k + 1) * P], ec[:, (4 * n + k) * P:(4 * n + k + 1) * P], ident)
                last.then_inc(t_full, 1)
            for g in range(4):
                pe.wait_ge(pooled, g + 1)
                mm(a_bank(("pm", g))[:, :], poolw[:, g, :], uT[:, g, :], start=True, stop=True).then_inc(a_full, 1)
            pe.wait_ge(a_free, AT[("vcmp", 0)] + 1)
            for i in range(NT):
                pe.wait_ge(t_free, TT[("ec", i // 2)] + 1)
                if i >= 2:
                    pe.wait_ge(co_free, i - 1)
                for g in range(G2):
                    last = mm(bank[6 + i % 2][:, g * 256:(g + 1) * 256], ecT[:, (2 * i + g) * P:(2 * i + g + 1) * P],
                              vdiag[:, g, :], start=True, stop=True)
                last.then_inc(co_full, 1)

            pe.wait_ge(a_free, A2_END)
            pe.wait_ge(t_free, TT[("ec", 1)] + 1)
            pe.wait_ge(co_free, NT)
            attention(steps2, NS, lambda br, h: q2T[rows(h), h // 2, :], lambda br, h: kT2[br][rows(h), h // GROUP, :],
                      lambda br, h: v2[br][:, :, (h // GROUP) * HD:(h // GROUP + 1) * HD])
            pe.wait_ge(pt_free, 2 * NS)
            pe.wait_ge(o_free, 2 * NS // NH)
            for i in range(NT):
                b = t_bank(("at", i))
                for k in range(4):
                    last = nc.tensor.transpose(b[:, k * P:(k + 1) * P], attn[:, i, k * P:(k + 1) * P], ident)
                last.then_inc(t_full, 1)
            pe.wait_ge(t_free, TT[("at", NT - 1)] + 1)
            arrived(pe, "ba")
            arrived(pe, "bp")
            R = 2 * NT
            for e in range(KC):
                for n, (name, src) in enumerate((("ba", aT), ("bp", pmT))):
                    r = R + 2 * e + n
                    if 2 * e + n >= 4:
                        pe.wait_ge(r_free, r - 3)
                    for k in range(4):
                        last = mm(bank[r % 4][:, :], slot(name, D)[:, k, e * P:(e + 1) * P], src[:, k, :],
                                  start=(k == 0), stop=(k == 3))
                    last.then_inc(r_full, 1)
            R += 2 * KC
            pe.wait_ge(mix_done, 1)
            residual(("w2o0", "w2o1"), gaT, R, None)
            R += 2 * NT
            h_transposes("h3", xn3, 2 * NT)
            pe.wait_ge(t_free, TT[("h3", NT - 1, 1)] + 1)
            pe.wait_ge(r_free, R)
            for c in range(DFF // P):
                name = f"f1_{c // 4}"
                if c % 4 == 0:
                    arrived(pe, name)
                t_tiles(name, ("ff", c), c % 4, None)
            pe.wait_ge(a_free, A2_END + DFF // P)
            for n in range(2):
                for kg in range(4):
                    name = f"f2_{n}_{kg}"
                    arrived(pe, name)
                    order = [(k, i) for k in range(KC) for i in range(NT)] if kg < 3 else [(k, i) for i in range(NT) for k in range(KC)]
                    for k, i in order:
                        last = mm(bank[4 * n + i][:, :], ffT[:, KC * kg + k, i * P:(i + 1) * P], slot(name)[:, k, :],
                                  start=(kg == 0 and k == 0), stop=(kg == 3 and k == KC - 1))
                        if kg == 3 and k == KC - 1:
                            last.then_inc(r_full, 1)
                    if kg < 3:
                        last.then_inc(w_used, 1)

        @block.scalar
        def _(act):
            run = nc.scalar.activation

            def root(base, i):
                act.wait_ge(ms_done, base + i + 1)
                run(rs[:, base + i:base + i + 1], ss[:, base + i:base + i + 1], ACT.Sqrt).then_inc(sq_done, 1)

            def take(tile):
                n = AT[tile]
                kind, i = tile[0], tile[1]
                b = bank[n % 4]
                act.wait_ge(a_full, n + 1)
                if kind == "qi":
                    last = run(qiT[:, i, :], b[:, :], ACT.Copy)
                elif kind == "ki":
                    last = run(kiT, b[:, :], ACT.Copy)
                elif kind == "wi":
                    last = run(wi, b[:, 0:NT * IDX_HEADS].rearrange("p (i h) -> p i h", i=NT), ACT.Copy)
                elif kind in ("za", "zb"):
                    at = 0 if kind == "za" else 512
                    last = run(zz[:, i, at:at + 512], b[:, :], ACT.Silu)
                elif kind == "rel":
                    r = 4 * (i - 1) + tile[2]
                    if r >= 2:
                        act.wait_ge(rel_free, r - 1)
                    last = run(rels[r % 2][:, 0:(i + 1) * P], b[:, 0:(i + 1) * P], ACT.Relu, scale=IDX_SCALE)
                elif kind in ("va", "vb"):
                    last = run(v1[kind][:, i, :], b[:, :], ACT.Copy)
                elif kind in ("kb", "qb", "ka", "qa"):
                    last = run(raw[("kb", "qb", "ka", "qa").index(kind) % 2][:, i, :], b[:, :], ACT.Copy)
                elif kind == "kv2":
                    twice = lambda n_, g: b[:, n_:n_ + g * HD].rearrange("p (g d) -> p g d", g=g).unsqueeze(2).to_broadcast([P, g, 2, HD])
                    for m in range(3):
                        run(dup[:, m, i, :, :, :], twice(m * P, G2), ACT.Copy)
                    last = run(v2["s"][:, i, :], b[:, 384:512], ACT.Copy)
                elif kind == "kwvg":
                    run(dup[:, 3, i, :, :, :], b[:, 0:P].rearrange("p (g d) -> p g d", g=G2).unsqueeze(2).to_broadcast([P, G2, 2, HD]), ACT.Copy)
                    run(v2["w"][:, i, :], b[:, P:2 * P], ACT.Copy)
                    last = run(gates[:, i, :], b[:, 256:280], ACT.Sigmoid)
                elif kind == "q2":
                    last = run(q2[:, i * 512:(i + 1) * 512], b[:, :], ACT.Copy)
                elif kind == "pool":
                    last = run(uT[:, i, :], b[:, :], ACT.Copy)
                elif kind == "hidk":
                    for c in range(2):
                        last = run(hidk[:, c, :, 0:NC], b[:, 64 * c:64 * c + G2 * NC].rearrange("p (g c) -> p g c", g=G2), ACT.Gelu_apprx_tanh)
                elif kind == "hidv":
                    for c in range(2):
                        for g in range(G2):
                            src = b[:, 64 * c + g * NC:64 * c + (g + 1) * NC].unsqueeze(1).to_broadcast([P, 4, NC])
                            last = run(hidv[:, c, g, :, 0:NC], src, ACT.Gelu_apprx_tanh)
                elif kind == "kcmp":
                    src = b[0:NC, 0:G2 * HD].rearrange("p (g d) -> p g d", g=G2).unsqueeze(2).to_broadcast([NC, G2, 2, HD])
                    last = run(kcn[0:NC, :, :, :], src, ACT.Copy)
                elif kind == "vcmp":
                    for r in range(4):
                        rows = slice(NCP * r, NCP * r + NCP)
                        last = run(vdiag[rows, :, r * HD:(r + 1) * HD], b[rows, 0:G2 * HD].rearrange("p (g d) -> p g d", g=G2), ACT.Copy)
                elif kind in ("ga", "gb"):
                    last = run((gaT if kind == "ga" else gbT)[:, i, :], b[:, :], ACT.Sigmoid)
                elif kind == "pm":
                    last = run(pmT[:, i, :], b[:, :], ACT.Copy, scale=small[:, V_PS + i:V_PS + i + 1])
                elif kind == "ff":
                    run(ffT[:, i, :], b[:, :], ACT.Relu).then_inc(relu_done, 1)
                    act.wait_ge(relu_done, i + 1)
                    last = run(ffT[:, i, :], ffT[:, i, :], ACT.Square)
                last.then_inc(a_free, 1)

            def exps(steps, base, dens):
                for t, (i, _, _) in enumerate(steps):
                    act.wait_ge(l_done, base + t + 1)
                    n = (i + 1) * P
                    run(logits[t % 3][:, 0:n], logits[t % 3][:, 0:n], ACT.Exp, scale=-1.0, bias=negm[:, t:t + 1],
                        accum_out=dens[:, t:t + 1]).then_inc(e_done, 1)

            for i in range(NT):
                act.wait_ge(x_in, 16 * NT)
                if i > 0:
                    act.wait_ge(ss_done, i)
                run(junk[:, :], x[:, i, :], ACT.Square, accum_out=ss[:, i:i + 1]).then_inc(ss_done, 1)
                root(0, i)
            done = [0]
            for tile in A1:
                take(tile)
                if tile[0] in ("qb", "ka", "qa", "za") and tile[1] == 1:
                    act.wait_ge(raw_ms, done[0] + 1)
                    run(rsq, ssq, ACT.Sqrt).then_inc(raw_sq, 1)
                    done[0] += 1
            act.wait_ge(strips_in, 16 * P // COPIES)
            exps(steps1, 0, den)
            for i in range(NT):
                act.wait_ge(ss_done, NT + i)
                act.wait_ge(r_free, 2 * (i + 1))
                run(junk[:, :], x[:, i, :], ACT.Square, accum_out=ss[:, NT + i:NT + i + 1]).then_inc(ss_done, 1)
                root(NT, i)
            for tile in A2:
                if tile == ("hidk", 0):
                    act.wait_ge(zeroed, 1)
                if tile == ("gb", 4):
                    for n in range(2):
                        act.wait_ge(cl_done, n + 1)
                        run(ec_of[n], ec_of[n], ACT.Exp).then_inc(ce_done, 1)
                take(tile)
            exps(steps2, NS, den2)
            for i in range(NT):
                act.wait_ge(ss_done, 2 * NT + i)
                act.wait_ge(r_free, R_OUT2 + 2 * (i + 1))
                run(junk[:, :], x[:, i, :], ACT.Square, accum_out=ss[:, 2 * NT + i:2 * NT + i + 1]).then_inc(ss_done, 1)
                root(2 * NT, i)
            for tile in A3:
                take(tile)
            for i in range(NT):
                act.wait_ge(ss_done, 3 * NT + i)
                act.wait_ge(r_free, R_FF + NT + i + 1)
                run(junk[:, :], x[:, i, :], ACT.Square, accum_out=ssf[:, i:i + 1]).then_inc(ss_done, 1)
                act.wait_ge(ms_done, 3 * NT + i + 1)
                run(rsf[:, i:i + 1], ssf[:, i:i + 1], ACT.Sqrt).then_inc(sq_done, 1)

        @block.vector
        def _(dve):
            v = nc.vector
            count = [0]

            def step(ins):
                count[0] += 1
                ins.then_inc(dve_step, 1)
                dve.wait_ge(dve_step, count[0])

            def norm(base, i, xn):
                dve.wait_ge(ss_done, base + i + 1)
                v.tensor_scalar(ss[:, base + i:base + i + 1], ss[:, base + i:base + i + 1], 1.0 / D, EPS, ALU.mult, ALU.add)\
                    .then_inc(ms_done, 1)
                dve.wait_ge(sq_done, base + i + 1)
                step(v.reciprocal(rs[:, base + i:base + i + 1], rs[:, base + i:base + i + 1]))
                v.tensor_scalar(xn[:, i, :], x[:, i, :], rs[:, base + i:base + i + 1], None, ALU.mult).then_inc(xn_done, 1)

            def take_h(name, i, gains):
                for c in range(2):
                    n = TT[(name, i, c)]
                    dve.wait_ge(t_full, n + 1)
                    src = bank[4 + n % 2][:, :].rearrange("p (k s) -> p k s", k=4)
                    dst = hTk[:, 4 * c:4 * c + 4, i * P:(i + 1) * P]
                    if gains is None:
                        v.tensor_copy(dst, src).then_inc(t_free, 1)
                    else:
                        g = small[:, gains + 4 * c:gains + 4 * c + 4].unsqueeze(2).to_broadcast([P, 4, P])
                        v.tensor_tensor(dst, src, g, ALU.mult).then_inc(t_free, 1)

            def head_norm(n, g):
                dve.wait_ge(a_free, AT[(g, NT - 1)] + 1)
                r = raw[n % 2]
                for half in range(2):
                    part = r[:, 2 * half:2 * half + 2, :].rearrange("p i n -> p (i n)")
                    step(v.tensor_tensor(junk[:, :], part, part, ALU.mult))
                    step(v.tensor_reduce(ssq[:, 16 * half:16 * half + 16], junk[:, :].rearrange("p (h d) -> p h d", d=HD), AX.X, ALU.add))
                v.tensor_scalar(ssq, ssq, 1.0 / HD, EPS, ALU.mult, ALU.add).then_inc(raw_ms, 1)
                dve.wait_ge(raw_sq, n + 1)
                step(v.reciprocal(rsq, rsq))
                allh = r.rearrange("p i (h d) -> p (i h) d", d=HD)
                v.tensor_tensor(allh, allh, rsq.unsqueeze(2).to_broadcast([P, NT * NH, HD]), ALU.mult).then_inc(raw_done, 1)

            def take_raw(g, gain):
                for c in range(4):
                    n = TT[(g, c)]
                    dve.wait_ge(t_full, n + 1)
                    v.tensor_scalar(qkT[g][:, c, :], bank[4 + n % 2][:, :], small[:, gain:gain + 1],
                                    SCALE if g[0] == "q" else 1.0, ALU.mult, ALU.mult).then_inc(t_free, 1)

            def attention(steps, base, bias, finish):
                n_steps = len(steps)
                for t in range(n_steps + 3):
                    if t < n_steps:
                        i, br, h = steps[t]
                        n = (i + 1) * P
                        b = bias(t)
                        dve.wait_ge(s_full, base + t + 1)
                        if t >= 3:
                            dve.wait_ge(pt_full, base + t - 2)
                        v.tensor_tensor_reduce(logits[t % 3][:, 0:n], bank[t % 3][:, 0:n], b, -1.0, BIG, ALU.add, ALU.min,
                                               negm[:, t:t + 1]).then_inc(l_done, 1)
                    u = t - 2
                    if 0 <= u < n_steps:
                        n = (steps[u][0] + 1) * P
                        dve.wait_ge(pt_full, base + u + 1)
                        if u >= 2:
                            dve.wait_ge(pv_done, base + u - 1)
                        v.tensor_copy(probsT[u % 2][:, 0:n], bank[3 + u % 2][:, 0:n]).then_inc(pt_free, 1)
                    if t >= 10 and (t - 3) % NH == NH - 1:
                        o = (t - 3) // NH
                        dve.wait_ge(pv_done, base + NH * (o + 1))
                        finish(o)

            dve.wait_ge(table_in, 48)
            dve.wait_ge(vec_full, 1)
            v.tensor_tensor(vec[:, 0:512], bank[6][0:2 * NH, 0:512], add_sb[:, 0:512], ALU.add)
            v.tensor_tensor(vec[:, 512:VEC], bank[7][0:2 * NH, 0:P], add_sb[:, 512:VEC], ALU.add).then_inc(vec_done, 1)
            dve.wait_ge(consts_in, 32)
            for i in range(NT):
                norm(0, i, xn1)
                if i > 0:
                    take_h("h1", i - 1, V_G1)
            take_h("h1", NT - 1, V_G1)

            dve.wait_ge(a_free, AT[("wi", 0)] + 1)
            for i in range(1, NT):
                n = (i + 1) * P
                s = score_of[i]
                for h in range(IDX_HEADS):
                    r = 4 * (i - 1) + h
                    dve.wait_ge(a_free, AT[("rel", i, h)] + 1)
                    if h == 0:
                        ins = v.tensor_scalar(s, rels[r % 2][:, 0:n], wi[:, i, 0:1], None, ALU.mult)
                    else:
                        ins = v.scalar_tensor_tensor(s, rels[r % 2][:, 0:n], wi[:, i, h:h + 1], s, ALU.mult, ALU.add)
                    ins.then_inc(rel_free, 1)
                    dve.wait_ge(rel_free, r + 1)
                step(v.tensor_tensor(s[:, i * P:n], s[:, i * P:n], consts[:, C_DIAG:C_DIAG + P], ALU.add))
            for i in range(1, NT):
                s = score_of[i]
                for _ in range(TOPK // 8):
                    step(v.max(top8, s))
                    step(v.match_replace(s, top8, s, TAKEN))

            head_norm(0, "kb")
            take_raw("kb", V_KB)
            head_norm(1, "qb")
            dve.wait_ge(vec_out, 16)
            take_raw("qb", V_QB)
            head_norm(2, "ka")
            take_raw("ka", V_KA)
            head_norm(3, "qa")
            for i in range(1, NT):
                v.tensor_scalar(mask_of[i], score_of[i], TAKEN, NEG, ALU.not_equal, ALU.mult).then_inc(masks_done, 1)
            dve.wait_ge(masks_done, NT - 1)
            take_raw("qa", V_QA)

            combo_of = {t: c for c, t in enumerate(combos)}

            def bias1(t):
                i, br, h = steps1[t]
                if t in combo_of:
                    dve.wait_ge(combo_done, combo_of[t] + 1)
                    return combo[combo_of[t] % 2][:, 0:(i + 1) * P]
                return strips[:, (h if br == "a" else NH + h), (NT - 1 - i) * P:S]

            def finish1(o):
                i, br, _ = steps1[NH * o]
                at = 0 if br == "a" else 512
                dve.wait_ge(e_done, NH * (o + 1))
                step(v.reciprocal(gr, den[:, NH * o:NH * (o + 1)]))
                z = zz[:, i, at:at + 512]
                zh = z.rearrange("p (h d) -> p h d", h=NH)
                step(v.tensor_tensor(zh, zh, gr.unsqueeze(2).to_broadcast([P, NH, HD]), ALU.mult))
                v.tensor_tensor(z, z, bank[5 + o % 3][:, :], ALU.mult).then_inc(o_free, 1)

            dve.wait_ge(a_free, A1_END)
            dve.wait_ge(strips_in, 16 * P // COPIES)
            attention(steps1, 0, bias1, finish1)

            def add_x(r0, then=None):
                for i in range(NT):
                    for n in range(2):
                        r = r0 + 2 * i + n
                        dve.wait_ge(r_full, r + 1)
                        xs = x[:, i, n * 512:(n + 1) * 512]
                        v.tensor_tensor(xs, xs, bank[r % 4][:, :], ALU.add).then_inc(r_free, 1)
                    then(i)

            for i in range(NT):
                take_h("mx", i, None)

            def then2(i):
                if i > 0:
                    norm(NT, i - 1, xn2)

            add_x(0, then2)
            norm(NT, NT - 1, xn2)
            for i in range(NT):
                take_h("h2", i, V_G2)

            def rope(view, heads, cos, sin, n=P, tiles=NT):
                x1, x2 = view[:, :, :, 0:ROT], view[:, :, :, ROT:2 * ROT]
                size = tiles * heads * ROT
                tmp = [r[0:n, 0:size].rearrange("p (i h d) -> p i h d", i=tiles, h=heads) for r in rope_tmp]
                v.tensor_tensor(tmp[0], x1, cos, ALU.mult)
                v.tensor_tensor(tmp[1], x2, sin, ALU.mult)
                v.tensor_tensor(tmp[2], x2, cos, ALU.mult)
                step(v.tensor_tensor(tmp[3], x1, sin, ALU.mult))
                v.tensor_tensor(x1, tmp[0], tmp[1], ALU.subtract)
                return v.tensor_tensor(x2, tmp[2], tmp[3], ALU.add)

            def angles(at, heads):
                return consts[:, at:at + NT * ROT].rearrange("p (i d) -> p i d", i=NT).unsqueeze(2).to_broadcast([P, NT, heads, ROT])

            dve.wait_ge(a_free, AT[("kwvg", NT - 1)] + 1)
            for m in (2, 3):
                last = rope(dup[:, m, :, :, :, :].rearrange("p i g r d -> p i (g r) d"), 4, angles(C_COS, 4), angles(C_SIN, 4))
                if m == 2:
                    step(last)
            last.then_inc(rope_done, 1)
            dve.wait_ge(rope_done, 1)
            for m in range(2):
                pe_at = (V_PEK, V_PEV)[m]
                for g in range(G2):
                    n = TT[("kv", m, g)]
                    dve.wait_ge(t_full, n + 1)
                    for half in range(2):
                        rows = slice(half * HD, (half + 1) * HD)
                        src = bank[4 + n % 2][rows, 16 * half:16 * half + NC * 16].rearrange("p (c j) -> p c j", j=16)
                        pos = small[rows, pe_at:pe_at + 16].unsqueeze(1).to_broadcast([HD, NC, 16])
                        last = v.tensor_tensor(blk[m][rows, g, :, :], src, pos, ALU.add)
                        if half == 0:
                            step(last)
                    last.then_inc(t_free, 1)
            for m, br in ((2, "s"), (3, "w")):
                for g in range(G2):
                    n = TT[("kv", m, g)]
                    dve.wait_ge(t_full, n + 1)
                    v.tensor_copy(kT2[br][:, g, :], bank[4 + n % 2][:, :]).then_inc(t_free, 1)
            dve.wait_ge(a_free, AT[("q2", NT - 1)] + 1)
            q2h = q2.rearrange("p (i h d) -> p i h d", i=NT, h=NH)
            rope(q2h, NH, angles(C_COS, NH), angles(C_SIN, NH)).then_inc(rope_done, 1)
            for c in range(4):
                n = TT[("q2", c)]
                dve.wait_ge(t_full, n + 1)
                v.tensor_scalar(q2T[:, c, :], bank[4 + n % 2][:, :], SCALE, None, ALU.mult).then_inc(t_free, 1)
            dve.wait_ge(a_free, AT[("kcmp", 0)] + 1)
            dve.wait_ge(rope_done, 2)
            pcos = consts[0:NC, C_PCOS:C_PCOS + ROT].unsqueeze(1).unsqueeze(1).to_broadcast([NC, 1, 4, ROT])
            psin = consts[0:NC, C_PSIN:C_PSIN + ROT].unsqueeze(1).unsqueeze(1).to_broadcast([NC, 1, 4, ROT])
            rope(kcn[0:NC, :, :, :].rearrange("p g r d -> p (g r) d").unsqueeze(1), 4, pcos, psin, NC, 1).then_inc(kcn_done, 1)
            n = TT[("kcT", 0)]
            dve.wait_ge(t_full, n + 1)
            dve.wait_ge(zeroed, 1)
            v.tensor_copy(kcT[:, :, 0:NC], bank[4 + n % 2][:, 0:G2 * NCP].rearrange("p (g c) -> p g c", g=G2)[:, :, 0:NC]).then_inc(t_free, 1)
            quads = lambda a: a.rearrange("p (i m) c -> p i m c", i=NT)
            per_tile = lambda at: consts[:, at:at + NT * NCP].rearrange("p (i c) -> p i c", i=NT).unsqueeze(2).to_broadcast([P, NT, NH // 2, NCP])
            for n in range(2):
                e = ec_of[n]
                m = cm[:, 16 * n:16 * n + 16]
                dve.wait_ge(cs_full, n + 1)
                step(v.tensor_tensor(quads(e), bank[6 + n][:, :].rearrange("p (i m c) -> p i m c", i=NT, c=NCP), per_tile(C_CADD), ALU.add))
                step(v.tensor_reduce(m, e, AX.X, ALU.max))
                v.tensor_tensor(e, e, m.unsqueeze(2).to_broadcast([P, 16, NCP]), ALU.subtract).then_inc(cl_done, 1)
            for n in range(2):
                dve.wait_ge(ce_done, n + 1)
                v.tensor_tensor(quads(ec_of[n]), quads(ec_of[n]), per_tile(C_C01), ALU.mult).then_inc(cp_done, 1)
            dve.wait_ge(cp_done, 2)
            step(v.tensor_reduce(cden, ec.rearrange("p (m c) -> p m c", c=NCP), AX.X, ALU.add))
            step(v.tensor_scalar(cden, cden, 1e-30, None, ALU.max))
            step(v.reciprocal(cden, cden))
            cdh = cden.rearrange("p (i h) -> p i h", i=NT)
            step(v.tensor_tensor(cdh, cdh, gates[:, :, 0:NH], ALU.mult))
            for n in range(2):
                k = TT[("ec", n)]
                dve.wait_ge(t_full, k + 1)
                v.tensor_copy(ecT[:, 512 * n:512 * n + 512], bank[4 + k % 2][:, :]).then_inc(t_free, 1)
            heads = lambda a: a.rearrange("p (h d) -> p h d", h=NH)
            for i in range(NT):
                dve.wait_ge(co_full, i + 1)
                v.tensor_tensor(heads(attn[:, i, :]), heads(bank[6 + i % 2][:, :]),
                                cden[:, NH * i:NH * (i + 1)].unsqueeze(2).to_broadcast([P, NH, HD]), ALU.mult).then_inc(co_free, 1)

            def bias2(t):
                return strip0[:, (NT - 1 - steps2[t][0]) * P:S]

            def finish2(o):
                i, br, _ = steps2[NH * o]
                dve.wait_ge(e_done, NS + NH * (o + 1))
                at = NH if br == "s" else 2 * NH
                step(v.reciprocal(gr, den2[:, NH * o:NH * (o + 1)]))
                step(v.tensor_tensor(gr, gr, gates[:, i, at:at + NH], ALU.mult))
                part = heads(junk[:, 0:512])
                v.tensor_tensor(part, heads(bank[5 + o % 3][:, :]), gr.unsqueeze(2).to_broadcast([P, NH, HD]), ALU.mult).then_inc(o_free, 1)
                dve.wait_ge(o_free, NS // NH + o + 1)
                step(v.tensor_tensor(attn[:, i, :], attn[:, i, :], junk[:, 0:512], ALU.add))

            dve.wait_ge(co_free, NT)
            attention(steps2, NS, bias2, finish2)
            for i in range(NT):
                n = TT[("at", i)]
                dve.wait_ge(t_full, n + 1)
                v.tensor_copy(aT[:, :, i * P:(i + 1) * P], bank[4 + n % 2][:, :].rearrange("p (k s) -> p k s", k=4)).then_inc(t_free, 1)
            R = 2 * NT
            for e in range(KC):
                for n, g in enumerate((gaT, gbT)):
                    r = R + 2 * e + n
                    dve.wait_ge(r_full, r + 1)
                    v.tensor_tensor(g[:, e, :], g[:, e, :], bank[r % 4][:, :], ALU.mult).then_inc(r_free, 1)
                dve.wait_ge(r_free, R + 2 * e + 2)
                last = v.tensor_tensor(gaT[:, e, :], gaT[:, e, :], gbT[:, e, :], ALU.add)
            last.then_inc(mix_done, 1)
            R += 2 * KC

            def then3(i):
                if i > 0:
                    norm(2 * NT, i - 1, xn3)

            add_x(R, then3)
            norm(2 * NT, NT - 1, xn3)
            R += 2 * NT
            for i in range(NT):
                take_h("h3", i, V_G3)
            for n in range(2):
                for i in range(NT):
                    r = R + NT * n + i
                    dve.wait_ge(r_full, r + 1)
                    xs = x[:, i, n * 512:(n + 1) * 512]
                    v.tensor_tensor(xs, xs, bank[4 * n + i][:, :], ALU.add).then_inc(r_free, 1)
            dve.wait_ge(gfin_in, 16)
            for i in range(NT):
                dve.wait_ge(ss_done, 3 * NT + i + 1)
                v.tensor_scalar(ssf[:, i:i + 1], ssf[:, i:i + 1], 1.0 / D, EPS, ALU.mult, ALU.add).then_inc(ms_done, 1)
                dve.wait_ge(sq_done, 3 * NT + i + 1)
                step(v.reciprocal(rsf[:, i:i + 1], rsf[:, i:i + 1]))
                v.scalar_tensor_tensor(x[:, i, :], x[:, i, :], rsf[:, i:i + 1], gfin, ALU.mult, ALU.mult).then_inc(y_done, 1)

        @block.gpsimd
        def _(pool):
            g = nc.gpsimd
            pool.wait_ge(vec_done, 1)
            pool.dma_start(copies.rearrange("m h x -> h m x"), vec.unsqueeze(1).to_broadcast([2 * NH, COPIES, VEC]))\
                .then_inc(vec_out, 16)
            pool.wait_ge(vec_out, 16)
            pitch = 2 * NH * VEC
            for p in range(0, P, COPIES):
                diagonal = bass.AP(copies.tensor, P - 1 - p, [[pitch - 1, COPIES], [VEC, 2 * NH], [1, S]])
                pool.dma_start(strips[p:p + COPIES, :, :], diagonal).then_inc(strips_in, 16)
            pool.wait_ge(strips_in, 16 * P // COPIES)
            pool.wait_ge(masks_done, NT - 1)
            pool.wait_ge(a_full, A1_END)
            for c, t in enumerate(combos):
                i, _, h = steps1[t]
                if c >= 2:
                    pool.wait_ge(l_done, combos[c - 2] + 1)
                g.tensor_tensor(combo[c % 2][:, 0:(i + 1) * P], strips[:, h, (NT - 1 - i) * P:S], mask_of[i], ALU.add)\
                    .then_inc(combo_done, 1)
            pool.wait_ge(xn_done, 2 * NT)
            pool.wait_ge(t_free, TT[("mx", NT - 1, 1)] + 1)
            for z in (hidk, hidv, kcT):
                g.memset(z, 0.0)
            g.memset(vdiag, 0.0).then_inc(zeroed, 1)
            chain = [0]

            def link(ins):
                chain[0] += 1
                ins.then_inc(pool_chain, 1)
                pool.wait_ge(pool_chain, chain[0])

            for n, width in enumerate(POOL_WINDOWS):
                pool.wait_ge(a_free, AT[("pool", n)] + 1)
                src, shift, k = uT[:, n, :], 1, 0
                while shift < width:
                    dst = ptmp[k % 2]
                    g.tensor_copy(dst[:, 0:shift], src[:, 0:shift])
                    link(g.tensor_tensor(dst[:, shift:S], src[:, shift:S], src[:, 0:S - shift], ALU.add))
                    src, shift, k = dst, 2 * shift, k + 1
                g.tensor_tensor(src[:, 0:16], src[:, 0:16], consts[:, C_INV + 16 * n:C_INV + 16 * n + 16], ALU.mult)
                link(g.tensor_scalar(src[:, 16:S], src[:, 16:S], 1.0 / width, None, ALU.mult))
                g.tensor_tensor(uT[:, n, :], src, uT[:, n, :], ALU.subtract).then_inc(pooled, 1)
                pool.wait_ge(pooled, n + 1)


_CONSTANTS = ("consts", "onehot", "vec_add")
_DIRECT = ("x", "rel_bias", "w_in", "w_out", "w_in_2", "cmp_k_w1_2", "cmp_k_w2_2", "cmp_v_w1_2", "cmp_v_w2_2",
           "w_branch_attn_2", "pool_w_2", "w_branch_pool_2", "w_out_2", "w_ff1_2", "w_ff2_2")


def kernel(**inputs):
    from concourse import bacc
    from concourse.bass_utils import run_bass_kernel_spmd

    a = {k: np.asarray(v) for k, v in inputs.items()}
    arrays = dict(zip(_CONSTANTS, shape_constants()))
    for name in _DIRECT:
        arr = a[name]
        arrays[name] = np.ascontiguousarray(arr if name in ("x", "rel_bias") else arr[0])
    arrays["norm_final_2"] = np.ascontiguousarray(a["norm_final_2"].reshape(1, D))
    per_chunk = lambda g: g.reshape(-1, P).T
    per_head = lambda g: np.concatenate([g[0], g[0]])[:, None]
    blocks = lambda pe: pe[0].reshape(2, 16, HD).transpose(0, 2, 1).reshape(P, 16)
    arrays["small"] = np.ascontiguousarray(np.concatenate(
        [per_chunk(a["norm_gain"][0]), per_chunk(a["norm_mix_2"][0]), per_chunk(a["norm_mlp_2"][0]),
         per_head(a["q_norm_b"]), per_head(a["k_norm_b"]), per_head(a["q_norm_a"]), per_head(a["k_norm_a"]),
         per_chunk(a["pool_scale_2"][0]), blocks(a["cmp_pe_k_2"]), blocks(a["cmp_pe_v_2"])], axis=1))
    nc = bacc.Bacc("TRN2", target_bir_lowering=False, num_devices=1)
    w = {n: nc.dram_tensor(f"in_{n}", v.shape, F32, kind="ExternalInput").ap() for n, v in arrays.items()}
    out = nc.dram_tensor("out", (1, S, D), F32, kind="ExternalOutput").ap()
    build(nc, w, out)
    r = run_bass_kernel_spmd(nc, [{f"in_{n}": v for n, v in arrays.items()}], core_ids=[0])
    return r.results[0]["out"]
```

```python
from contextlib import ExitStack

import numpy as np

import concourse.bass as bass
from concourse import mybir

F32 = mybir.dt.float32
F32R = mybir.dt.float32r
ALU = mybir.AluOpType
ACT = mybir.ActivationFunctionType
AX = mybir.AxisListType

P = 128
S = 512
D = 1024
NT = S // P
KC = D // P
HD = 64
NH = 8
EPS = 1e-6
SCALE = HD ** -0.5
TOPK = min(256, S // 4)
N_BUCKETS = 32
IDX_HEADS = 4
IDX_SCALE = (IDX_HEADS * HD) ** -0.5
NEG = -1e30
FUTURE = -3.0e38
TAKEN = -3.4e38
BIG = 3.0e38
DFF = 4 * D
VEC = S + P

QA, KA, VA, ZA, QI, KI, WI, QB, KB, VB, ZB = np.cumsum([0, 512, 512, 512, 512, 256, 64, 4, 512, 512, 512]).tolist()
Q2, KV2, KWVG, POOL, MERGE = 0, 512, 1024, 1304, 1816
GATES = 24
G2 = 2
GROUP = NH // G2
ROT = 8
CMP_BLOCK, CMP_STRIDE = 32, 16
NC = (S - CMP_BLOCK) // CMP_STRIDE + 1
NCP = NC + 1
POOL_WINDOWS = (2, 4, 8, 16)
THETA = 500000.0

C_ID, C_DIAG, C_STRIP, C_COS, C_SIN, C_CADD, C_C01, C_PCOS, C_PSIN, C_INV, C_END = np.cumsum(
    [0, P, P, S, NT * ROT, NT * ROT, NT * NCP, NT * NCP, ROT, ROT, 4 * 16]).tolist()
V_G1, V_G2, V_G3, V_QB, V_KB, V_QA, V_KA, V_PS, V_PEK, V_PEV, V_END = np.cumsum(
    [0, KC, KC, KC, 1, 1, 1, 1, 4, 16, 16]).tolist()

COPIES = 16
RING = 3
SLOT = 8 * 512


def shape_constants():
    c = np.zeros((P, C_END), np.float32)
    p = np.arange(P)[:, None]
    c[:, C_ID:C_ID + P] = np.eye(P)
    c[:, C_DIAG:C_DIAG + P] = np.where(np.arange(P)[None, :] > p, FUTURE, 0)
    c[:, C_STRIP:C_STRIP + S] = np.where((S - P) + p - np.arange(S)[None, :] < 0, NEG, 0)
    inv = THETA ** (-np.arange(0, 2 * ROT, 2, dtype=np.float32) / np.float32(2 * ROT))
    t = np.arange(S, dtype=np.float32)
    ang = (t[:, None] * inv.astype(np.float32)).astype(np.float32)
    tiled = lambda a: a.reshape(NT, P, -1).transpose(1, 0, 2).reshape(P, -1)
    c[:, C_COS:C_COS + NT * ROT] = tiled(np.cos(ang))
    c[:, C_SIN:C_SIN + NT * ROT] = tiled(np.sin(ang))
    pos = np.arange(NC) * CMP_STRIDE + CMP_BLOCK - 1
    seen = np.zeros((S, NCP), bool)
    seen[:, :NC] = pos[None, :] <= np.arange(S)[:, None]
    c[:, C_CADD:C_CADD + NT * NCP] = tiled(np.where(seen, 0, NEG))
    c[:, C_C01:C_C01 + NT * NCP] = tiled(seen.astype(np.float32))
    pang = (pos.astype(np.float32)[:, None] * inv.astype(np.float32)).astype(np.float32)
    c[:NC, C_PCOS:C_PCOS + ROT] = np.cos(pang)
    c[:NC, C_PSIN:C_PSIN + ROT] = np.sin(pang)
    for g, w in enumerate(POOL_WINDOWS):
        c[:, C_INV + 16 * g:C_INV + 16 * g + 16] = 1.0 / np.minimum(np.arange(16) + 1, w)
    d = (S - 1) - np.arange(VEC)
    df = np.maximum(d, 1).astype(np.float32)
    half = N_BUCKETS // 2
    large = half + (np.log(df / np.float32(half)) / np.float32(np.log(128 / half)) * np.float32(half)).astype(np.int32)
    bucket = np.where(d < half, np.maximum(d, 0), np.minimum(large, N_BUCKETS - 1))
    onehot = (bucket[None, :] == np.arange(N_BUCKETS)[:, None]).astype(np.float32)
    times = ((d <= 128).astype(int) + (d % 4 == 0) + (d % 16 == 0)) * (d >= 0)
    add = np.zeros((2 * NH, VEC), np.float32)
    add[:NH] = np.where(d >= 0, 0, NEG)
    add[NH:] = np.where(times > 0, np.log(np.maximum(times, 1)), NEG)
    return c, onehot, add


def weight_groups(w):
    def cols(a, c, n, at=0, width=512):
        return (at, n, width, a[:, c:c + n].rearrange("(k p) n -> p k n", p=P))

    def whole(a, k, n):
        return (0, n, n, a.rearrange("(k p) n -> p k n", p=P))

    w1, w2 = w["w_in"], w["w_in_2"]
    groups = [("idx", [cols(w1, QI, 320), cols(w1, KI, 64, 320), cols(w1, WI, IDX_HEADS, 384)])]
    groups += [(n, [cols(w1, c, 512)]) for n, c in
               (("vb", VB), ("va", VA), ("kb", KB), ("qb", QB), ("zb", ZB), ("ka", KA), ("qa", QA), ("za", ZA))]
    groups += [(f"wo{n}", [cols(w["w_out"], 512 * n, 512)]) for n in range(2)]
    groups += [("kv2", [cols(w2, KV2, 512)]), ("kwvg", [cols(w2, KWVG, 280)]), ("q2", [cols(w2, Q2, 512)])]
    groups += [("ck", None), ("cv", None)]
    groups += [("pool", [cols(w2, POOL, 512)])]
    groups += [(f"ga{n}", [cols(w2, MERGE + 512 * n, 512)]) for n in range(2)]
    groups += [(f"gb{n}", [cols(w2, MERGE + D + 512 * n, 512)]) for n in range(2)]
    groups += [("ba", [whole(w["w_branch_attn_2"], 4, D)]), ("bp", [whole(w["w_branch_pool_2"], 4, D)])]
    groups += [(f"w2o{n}", [cols(w["w_out_2"], 512 * n, 512)]) for n in range(2)]
    groups += [(f"f1_{n}", [cols(w["w_ff1_2"], 512 * n, 512)]) for n in range(8)]
    groups += [(f"f2_{n}", [whole(w["w_ff2_2"][512 * n:512 * (n + 1), :], 4, D)]) for n in range(8)]
    return groups


def build(nc, w, out):
    groups = weight_groups(w)
    number = {name: n for n, (name, _) in enumerate(groups)}
    copies = nc.dram_tensor("bias_copies", (COPIES, 2 * NH, VEC), F32).ap()

    steps1 = [(i, br, h) for br in ("b", "a") for i in range(NT) for h in range(NH)]
    steps2 = [(i, br, h) for i in range(NT) for br in ("s", "w") for h in range(NH)]
    combos = [t for t, (i, br, h) in enumerate(steps1) if br == "a" and i > 0]
    NS = len(steps1)
    HALF = NS // 2

    FILL1 = [("zb", 0)] + [("ka", i) for i in range(NT)] + [("zb", 1), ("zb", 2)] + [("qa", i) for i in range(NT)] + [("zb", 3)]
    SEAM = [("za", 0), ("za", 1)]
    FILL1B = [("za", 2), ("za", 3)]
    FILL2 = [("gb", e) for e in range(2, 8)]
    fill1 = [(m // 3, FILL1[m // KC], m % KC) for m in range(KC * len(FILL1))]
    fill1 += [(HALF + m, FILL1B[m // KC], m % KC) for m in range(KC * len(FILL1B))]
    fill2 = [(m, FILL2[m // KC], m % KC) for m in range(KC * len(FILL2))]
    KA_ROOT, KA_NORM, KA_TURN = 15, 16, 17
    QA_ROOT = 31
    MASKS = KA_TURN + 4

    A1 = [("qi", 0), ("qi", 1), ("ki", 0), ("wi", 0)]
    A1 += [("rel", i, h) for i in range(1, NT) for h in range(IDX_HEADS)]
    A1 += [(g, i) for g in ("vb", "va", "kb", "qb") for i in range(NT)]
    A1_DENSE = len(A1)
    A1 += FILL1 + SEAM + FILL1B
    A2 = [(g, i) for g in ("kv2", "kwvg", "q2") for i in range(NT)]
    A2 += [("pool", g) for g in range(4)]
    A2 += [("hidk", 0), ("hidv", 0)]
    A2 += [("ga", e) for e in range(4)]
    A2 += [("kcmp", 0), ("vcmp", 0)]
    A2 += [("ga", e) for e in range(4, 8)]
    A2 += [("pm", g) for g in range(4)]
    A2 += [("gb", e) for e in range(2)]
    A2_DENSE = len(A2)
    A2 += FILL2
    A3 = [("ff", c) for c in range(DFF // P)]
    AT = {tile: n for n, tile in enumerate(A1 + A2 + A3)}
    A1_END, A2_END = len(A1), len(A1) + len(A2)

    T1 = [("h1", i, c) for i in range(NT) for c in range(2)]
    T1 += [(g, c) for g in ("kb", "qb") for c in range(4)]
    for t in range(NS + 2):
        if t == HALF:
            T1 += [("qa", c) for c in range(4)]
        if t >= 2:
            T1 += [("pt", t - 2)]
        if KA_TURN <= t < KA_TURN + 4:
            T1 += [("ka", t - KA_TURN)]
    T2 = [("mx", i, c) for i in range(NT) for c in range(2)]
    T2 += [("h2", i, c) for i in range(NT) for c in range(2)]
    T2 += [("kv", n, g) for n in range(4) for g in range(G2)]
    T2 += [("q2", c) for c in range(4)]
    T2 += [("kcT", 0)] + [("ec", n) for n in range(2)]
    T3 = [("pt", NS + t) for t in range(NS)]
    T3 += [("at", i) for i in range(NT)] + [("h3", i, c) for i in range(NT) for c in range(2)]
    TT = {tile: n for n, tile in enumerate(T1 + T2 + T3)}

    with ExitStack() as ctx:
        def sb(name, shape):
            return ctx.enter_context(nc.sbuf_tensor(name, shape, F32))

        def sem(name):
            return ctx.enter_context(nc.semaphore(name))

        bank = [ctx.enter_context(nc.psum_tensor(f"bank{b}", [P, 512], F32)) for b in range(8)]

        x = sb("x", [P, NT, D])
        hT_at = nc.sbuf_base
        hT = sb("hT", [P, KC * 512])
        wring = sb("wring", [P, RING, SLOT])
        consts = sb("consts", [P, C_END])
        small = sb("small", [P, V_END])
        junk = sb("junk", [P, D])
        stats = sb("stats", [P, 512])
        ARENA = 28900
        arena_at = nc.sbuf_base
        arena = sb("arena", [P, ARENA])
        used = [0]

        def region(n, at=None):
            if at is not None:
                return arena[:, at:at + n]
            used[0] += n
            return arena[:, used[0] - n:used[0]]

        hTk = hT[:, :].rearrange("p (k s) -> p k s", k=KC)
        qkT = {g: region(4 * S).rearrange("p (c s) -> p c s", c=4) for g in ("kb", "qb", "ka", "qa")}
        v1 = {g: region(NT * 512).rearrange("p (i n) -> p i n", i=NT) for g in ("vb", "va")}
        zz = region(NT * D).rearrange("p (i n) -> p i n", i=NT)
        raw_at = used[0]
        raw = [region(NT * 512).rearrange("p (i n) -> p i n", i=NT) for _ in range(2)]
        xn1 = region(NT * D, raw_at).rearrange("p (i n) -> p i n", i=NT)
        strips = region(2 * NH * S).rearrange("p (h u) -> p h u", h=2 * NH)
        scores = qkT["qa"].rearrange("p c s -> p (c s)")
        spans = {1: slice(0, 256), 2: slice(256, 640), 3: slice(640, 1152)}
        score_of = {i: scores[:, r] for i, r in spans.items()}
        mask_of = {i: raw[0].rearrange("p i n -> p (i n)")[:, r] for i, r in spans.items()}
        qiT = qkT["kb"][:, 0:2, :]
        kiT = qkT["kb"][:, 2, :]
        rels = [qkT["kb"][:, 3, :], qkT["qb"][:, 0, :]]
        vec = qkT["qb"][0:2 * NH, 1:3, :].rearrange("p a b -> p (a b)")[:, 0:VEC]
        bucket_sb = qkT["ka"][0:N_BUCKETS, 0:2, :].rearrange("p a b -> p (a b)")[:, 0:VEC]
        add_sb = qkT["ka"][0:2 * NH, 2:4, :].rearrange("p a b -> p (a b)")[:, 0:VEC]
        table_sb = qkT["qa"][0:N_BUCKETS, 3, 0:2 * NH]
        assert used[0] <= ARENA, used
        xflat = x[:, :, :].rearrange("p i n -> p (i n)")
        logits1 = [xflat[:, 1024 + 512 * n:1536 + 512 * n] for n in range(3)]
        probsT1 = [xflat[:, 2560 + 512 * n:3072 + 512 * n] for n in range(2)]
        combo = [junk[:, 512 * n:512 * n + 512] for n in range(2)]
        squares_of = {(g, i): xflat[:, 512 * (NT * n + i):512 * (NT * n + i) + 512] for n, g in enumerate(("kb", "qb")) for i in range(NT)}
        squares_of.update({(g, i): junk[:, 512 * (i % 2):512 * (i % 2) + 512] for g in ("ka", "qa") for i in range(NT)})
        used[0] = 0
        q2 = region(NT * 512)
        dup = region(4 * NT * G2 * 2 * HD).rearrange("p (m i g r d) -> p m i g r d", m=4, i=NT, g=G2, r=2)
        xn2 = region(NT * D, 0).rearrange("p (i n) -> p i n", i=NT)
        v2 = {g: region(NT * G2 * HD).rearrange("p (i n) -> p i n", i=NT) for g in ("s", "w")}
        gates = region(NT * GATES).rearrange("p (i n) -> p i n", i=NT)
        q2T = region(4 * S).rearrange("p (c s) -> p c s", c=4)
        kT2 = {g: region(G2 * S).rearrange("p (g s) -> p g s", g=G2) for g in ("s", "w")}
        uT = region(4 * S).rearrange("p (g s) -> p g s", g=4)
        ptmp = [region(S) for _ in range(2)]
        gaT = region(KC * S).rearrange("p (e s) -> p e s", e=KC)
        gbT = region(KC * S).rearrange("p (e s) -> p e s", e=KC)
        blk = {m: region(G2 * NC * 16).rearrange("p (g c j) -> p g c j", g=G2, c=NC) for m in range(2)}
        hidk = region(2 * G2 * NCP).rearrange("p (m g c) -> p m g c", m=2, g=G2)
        hidv = region(2 * G2 * 4 * NCP).rearrange("p (m g r c) -> p m g r c", m=2, g=G2, r=4)
        kcn = region(G2 * 2 * HD).rearrange("p (g r d) -> p g r d", g=G2, r=2)
        kcT = region(G2 * NCP).rearrange("p (g c) -> p g c", g=G2)
        vdiag = region(G2 * 4 * HD).rearrange("p (g n) -> p g n", g=G2)
        pmT = uT
        attn = region(NT * 512).rearrange("p (i n) -> p i n", i=NT)
        ccw = region(2 * 2 * HD).rearrange("p (m k d) -> p m k d", m=2, k=2)
        poolw = region(4 * P).rearrange("p (g d) -> p g d", g=4)
        assert used[0] <= ARENA, used
        ec = dup[:, 0, :, :, :, :].rearrange("p i g r d -> p (i g r d)")
        ecT = dup[:, 1, :, :, :, :].rearrange("p i g r d -> p (i g r d)")
        ec_of = [ec.rearrange("p (m r c) -> p m r c", r=2, c=NCP)[:, :, n, :] for n in range(2)]
        spare = dup[:, 2:4, :, :, :, :].rearrange("p m i g r d -> p (m i g r d)")
        logits2 = [spare[:, 512 * n:512 * n + 512] for n in range(3)]
        probsT2 = [spare[:, 1536:2048], q2[:, 0:512]]
        aT = hT[:, 0:2048].rearrange("p (k s) -> p k s", k=4)
        ffT = region((DFF // P) * S, 0).rearrange("p (c s) -> p c s", c=DFF // P)
        xn3 = gbT.rearrange("p e s -> p (e s)").rearrange("p (i n) -> p i n", i=NT)
        gfin = region(D, ARENA - D)
        def half(name, n, at):
            base = hT_at if at[0] == "hT" else arena_at
            return nc.alloc_sbuf_tensor_at(name, [P, n], F32R, offset=base + 4 * at[1])

        h3_hi = half("h3_hi", KC * S, ("hT", 0))
        h3_lo = half("h3_lo", KC * S, ("arena", 22624))
        unit_at = [16384, 18528, 18528 + 2 * D]
        w_hi = [half(f"w_hi{n}", D, ("arena", at)) for n, at in enumerate(unit_at)]
        w_lo = [half(f"w_lo{n}", D, ("arena", at + D)) for n, at in enumerate(unit_at)]
        ff_at = [("arena", 26720), ("hT", 0), ("hT", 2 * S)]
        ff_hi = [half(f"ff_hi{n}", S, at) for n, at in enumerate(ff_at)]
        ff_lo = [half(f"ff_lo{n}", S, (at[0], at[1] + S)) for n, at in enumerate(ff_at)]

        ident = consts[:, C_ID:C_ID + P]
        strip0 = consts[:, C_STRIP:C_STRIP + S]
        ss = stats[:, 0:12]
        rs = stats[:, 12:24]
        ssq = stats[:, 24:56]
        rsq = stats[:, 56:88]
        wi = stats[:, 88:104].rearrange("p (i h) -> p i h", i=NT)
        top8 = stats[:, 104:112]
        den = stats[:, 112:112 + NS]
        negm = stats[:, 176:176 + NS]
        gr = stats[:, 240:248]
        cm = stats[:, 248:280]
        cden = stats[:, 280:312]
        ssf = stats[:, 312:316]
        rsf = stats[:, 316:320]
        den2 = stats[:, 320:320 + NS]
        rope_tmp = [junk[:, 256 * n:256 * n + 256] for n in range(4)]

        x_in = sem("x_in")
        consts_in = sem("consts_in")
        table_in = sem("table_in")
        small2_in = sem("small2_in")
        gfin_in = sem("gfin_in")
        w_in = [sem(f"w_in{r}") for r in range(RING)]
        unit_used = sem("unit_used")
        vec_full = sem("vec_full")
        vec_done = sem("vec_done")
        vec_out = sem("vec_out")
        strips_in = sem("strips_in")
        ss_done = sem("ss_done")
        ms_done = sem("ms_done")
        sq_done = sem("sq_done")
        xn_done = sem("xn_done")
        a_full = sem("a_full")
        a_free = sem("a_free")
        t_full = sem("t_full")
        t_free = sem("t_free")
        r_full = sem("r_full")
        r_free = sem("r_free")
        rel_free = sem("rel_free")
        raw_ms = sem("raw_ms")
        raw_sq = sem("raw_sq")
        raw_done = sem("raw_done")
        masks_done = sem("masks_done")
        combo_done = sem("combo_done")
        s_full = sem("s_full")
        l_done = sem("l_done")
        e_done = sem("e_done")
        sq_free = sem("sq_free")
        pv_done = sem("pv_done")
        o_free = sem("o_free")
        zeroed = sem("zeroed")
        rope_done = sem("rope_done")
        kcn_done = sem("kcn_done")
        pooled = sem("pooled")
        pool_chain = sem("pool_chain")
        cs_full = sem("cs_full")
        cl_done = sem("cl_done")
        ce_done = sem("ce_done")
        cp_done = sem("cp_done")
        co_full = sem("co_full")
        co_free = sem("co_free")
        mix_done = sem("mix_done")
        h3_tmp = sem("h3_tmp")
        h3_hi_done = sem("h3_hi_done")
        w_hi_done = sem("w_hi_done")
        w_lo_done = sem("w_lo_done")
        ff_hi_done = sem("ff_hi_done")
        ff_lo_done = sem("ff_lo_done")
        relu_done = sem("relu_done")
        dve_step = sem("dve_step")
        y_done = sem("y_done")
        out_done = sem("out_done")

        def slot(name, width=512):
            s = number[name] % RING
            return wring[:, s, :].rearrange("p (k n) -> p k n", n=width)

        R_BRANCH, R_OUT2, R_FF = 2 * NT, 2 * NT + 2 * KC, 4 * NT + 2 * KC

        def last_use(name):
            if name[0] == "f":
                return w_lo_done, 4 * (int(name[3:]) + 1) + (DFF // P if name[1] == "2" else 0)
            if name[:2] in ("wo", "ba", "bp") or name.startswith("w2o"):
                return r_full, {"wo": R_BRANCH, "ba": R_OUT2, "bp": R_OUT2, "w2": R_FF}[name[:2]] - \
                    (1 if name in ("wo0", "w2o0", "ba") else 0)
            last = {"pool": ("pool", 3), "idx": ("wi", 0), "ck": ("hidk", 0), "cv": ("hidv", 0), "ga0": ("ga", 3), "ga1": ("ga", 7),
                    "gb0": ("gb", 3), "gb1": ("gb", 7)}.get(name, (name, NT - 1))
            return a_full, AT[last] + 1

        block = ctx.enter_context(nc.Block())

        @block.sync
        def _(sp):
            for i in range(NT):
                sp.dma_start(x[:, i, :], w["x"][0, i * P:(i + 1) * P, :]).then_inc(x_in, 16)
            sp.dma_start(consts[:, :], w["consts"]).then_inc(consts_in, 16)
            sp.dma_start(small[:, :], w["small"]).then_inc(consts_in, 16)
            sp.dma_start(bucket_sb, w["onehot"]).then_inc(table_in, 16)
            sp.dma_start(add_sb, w["vec_add"]).then_inc(table_in, 16)
            sp.dma_start(table_sb, w["rel_bias"]).then_inc(table_in, 16)
            for n, (name, parts) in enumerate(groups):
                if n >= RING:
                    done, value = last_use(groups[n - RING][0])
                    sp.wait_ge(done, value)
                if parts is None:
                    src = w["cmp_k_w1_2" if name == "ck" else "cmp_v_w1_2"]
                    for half in range(2):
                        rows = src[half * D:(half + 1) * D, :].rearrange("(j d) n -> d j n", d=HD)
                        sp.dma_start(slot(name, 256)[half * HD:(half + 1) * HD, :, :], rows).then_inc(w_in[n % RING], 16)
                else:
                    for at, cols, width, view in parts:
                        sp.dma_start(slot(name, width)[:, :, at:at + cols], view).then_inc(w_in[n % RING], 16)
                if name == "kv2":
                    for i in range(NT):
                        sp.wait_ge(pv_done, 1 if i == 0 else NS)
                        sp.dma_start(x[:, i, :], w["x"][0, i * P:(i + 1) * P, :]).then_inc(x_in, 16)
                if name == "kwvg":
                    sp.wait_ge(zeroed, 1)
                    for m, a in enumerate(("cmp_k_w2_2", "cmp_v_w2_2")):
                        sp.dma_start(ccw[:, m, :, :], w[a].rearrange("(k p) d -> p k d", p=P)).then_inc(small2_in, 16)
                    sp.dma_start(poolw, w["pool_w_2"].rearrange("g c d -> c g d")).then_inc(small2_in, 16)
                if name == "f1_3":
                    sp.wait_ge(xn_done, 3 * NT)
                    sp.dma_start(gfin, w["norm_final_2"].to_broadcast([P, D])).then_inc(gfin_in, 16)
            for i in range(NT):
                sp.wait_ge(y_done, i + 1)
                sp.dma_start(out[0, i * P:(i + 1) * P, :], x[:, i, :]).then_inc(out_done, 16)
            sp.wait_ge(out_done, 16 * NT)

        def arrived(eng, name):
            n = number[name]
            total = sum(2 if g[1] is None else len(g[1]) for g in groups[n % RING:n + 1:RING])
            eng.wait_ge(w_in[n % RING], 16 * total)

        @block.tensor
        def _(pe):
            mm = nc.tensor.matmul

            def a_bank(tile):
                n = AT[tile]
                if n >= 2:
                    pe.wait_ge(a_free, n - 1)
                return bank[n % 2]

            def t_bank(tile):
                n = TT[tile]
                if n >= 2:
                    pe.wait_ge(t_free, n - 1)
                return bank[4 + n % 2]

            def nat_tiles(name, width=512):
                arrived(pe, name)
                for i in range(NT):
                    b = a_bank((name, i))
                    for k in range(KC):
                        last = mm(b[:, 0:width], hTk[:, k, i * P:(i + 1) * P], slot(name)[:, k, 0:width],
                                  start=(k == 0), stop=(k == KC - 1))
                    last.then_inc(a_full, 1)

            def t_tiles(name, tile, c, lhs, act=hTk, kc=KC, width=512):
                b = a_bank(tile)
                for k in range(kc):
                    last = mm(b[:, :], slot(name, width)[:, k, c * P:(c + 1) * P], act[:, k, :],
                              start=(k == 0), stop=(k == kc - 1))
                last.then_inc(a_full, 1)

            def h_transposes(name, xn, base, tiles=range(NT)):
                for i in tiles:
                    pe.wait_ge(xn_done, base + i + 1)
                    for c in range(2):
                        b = t_bank((name, i, c))
                        for k in range(4):
                            last = nc.tensor.transpose(b[:, k * P:(k + 1) * P],
                                                       xn[:, i, (4 * c + k) * P:(4 * c + k + 1) * P], ident)
                        last.then_inc(t_full, 1)

            def raw_transposes(n, g, chunks=range(4)):
                pe.wait_ge(raw_done, n + 1)
                for c in chunks:
                    b = t_bank((g, c))
                    for i in range(NT):
                        last = nc.tensor.transpose(b[:, i * P:(i + 1) * P], raw[n % 2][:, i, c * P:(c + 1) * P], ident)
                    last.then_inc(t_full, 1)

            def fill(work, t):
                for _, tile, k in [f for f in work if f[0] == t]:
                    g, i = tile
                    b = a_bank(tile) if k == 0 else bank[AT[tile] % 2]
                    if g == "gb":
                        name = f"gb{i // 4}"
                        if k == 0:
                            arrived(pe, name)
                        last = mm(b[:, :], slot(name)[:, k, (i % 4) * P:(i % 4 + 1) * P], hTk[:, k, :], start=(k == 0), stop=(k == KC - 1))
                    else:
                        if k == 0:
                            arrived(pe, g)
                        last = mm(b[:, :], hTk[:, k, i * P:(i + 1) * P], slot(g)[:, k, :], start=(k == 0), stop=(k == KC - 1))
                    if k == KC - 1:
                        last.then_inc(a_full, 1)

            def attention(t, steps, base, query, key, value, logits, probsT):
                if t < NS:
                    i, br, h = steps[t]
                    if t >= 2:
                        pe.wait_ge(l_done, base + t - 1)
                    mm(bank[2 + t % 2][:, 0:(i + 1) * P], query(br, h)[:, i * P:(i + 1) * P],
                       key(br, h)[:, 0:(i + 1) * P], start=True, stop=True).then_inc(s_full, 1)
                u = t - 2
                if 0 <= u < NS:
                    pe.wait_ge(e_done, base + u + 1)
                    b = t_bank(("pt", base + u))
                    for j in range(steps[u][0] + 1):
                        last = nc.tensor.transpose(b[:, j * P:(j + 1) * P], logits[u % 3][:, j * P:(j + 1) * P], ident)
                    last.then_inc(t_full, 1)
                u = t - 3
                if u >= 0:
                    i, br, h = steps[u]
                    o = u // NH
                    pe.wait_ge(t_free, TT[("pt", base + u)] + 1)
                    if u % NH == 0 and o >= 2:
                        pe.wait_ge(o_free, base // NH + o - 1)
                    for j in range(i + 1):
                        last = mm(bank[6 + o % 2][:, h * HD:(h + 1) * HD], probsT[u % 2][:, j * P:(j + 1) * P],
                                  value(br, h)[:, j, :], start=(j == 0), stop=(j == i))
                    last.then_inc(pv_done, 1)

            pe.wait_ge(table_in, 48)
            mm(bank[6][0:2 * NH, 0:512], table_sb, bucket_sb[:, 0:512], start=True, stop=True)
            mm(bank[7][0:2 * NH, 0:P], table_sb, bucket_sb[:, 512:VEC], start=True, stop=True).then_inc(vec_full, 1)

            pe.wait_ge(consts_in, 32)
            h_transposes("h1", xn1, 0)

            arrived(pe, "idx")
            pe.wait_ge(t_free, 2 * NT)
            for c in range(2):
                t_tiles("idx", ("qi", c), c, None)
            t_tiles("idx", ("ki", 0), 2, None)
            b = a_bank(("wi", 0))
            for i in range(NT):
                for k in range(KC):
                    last = mm(b[:, i * IDX_HEADS:(i + 1) * IDX_HEADS], hTk[:, k, i * P:(i + 1) * P],
                              slot("idx")[:, k, 384:384 + IDX_HEADS], start=(k == 0), stop=(k == KC - 1))
            last.then_inc(a_full, 1)
            pe.wait_ge(a_free, 3)
            for i in range(1, NT):
                for h in range(IDX_HEADS):
                    r = slice((h % 2) * HD, (h % 2) * HD + HD)
                    mm(a_bank(("rel", i, h))[:, 0:(i + 1) * P], qiT[r, h // 2, i * P:(i + 1) * P],
                       kiT[r, 0:(i + 1) * P], start=True, stop=True).then_inc(a_full, 1)
            for g in ("vb", "va", "kb"):
                nat_tiles(g)
            nat_tiles("qb")
            raw_transposes(0, "kb")
            raw_transposes(1, "qb")
            pe.wait_ge(t_free, TT[("qb", 3)] + 1)
            pe.wait_ge(a_free, AT[("vb", NT - 1)] + 1)
            rows = lambda h: slice((h % 2) * HD, (h % 2) * HD + HD)
            for t in range(NS + 3):
                if t == HALF:
                    for tile in SEAM:
                        fill([(t, tile, k) for k in range(KC)], t)
                    raw_transposes(3, "qa")
                    pe.wait_ge(t_free, TT[("qa", 3)] + 1)
                attention(t, steps1, 0, lambda br, h: qkT["q" + br][rows(h), h // 2, :],
                          lambda br, h: qkT["k" + br][rows(h), h // 2, :], lambda br, h: v1["v" + br][:, :, h * HD:(h + 1) * HD],
                          logits1, probsT1)
                if KA_TURN <= t < KA_TURN + 4:
                    raw_transposes(2, "ka", [t - KA_TURN])
                fill(fill1, t)

            pe.wait_ge(a_free, A1_END)
            pe.wait_ge(o_free, NS // NH)
            for i in range(NT):
                for c in range(2):
                    b = t_bank(("mx", i, c))
                    for k in range(4):
                        last = nc.tensor.transpose(b[:, k * P:(k + 1) * P], zz[:, i, (4 * c + k) * P:(4 * c + k + 1) * P], ident)
                    last.then_inc(t_full, 1)

            def residual(names, src, r0, t_need):
                for i in range(NT):
                    pe.wait_ge(t_free, t_need + 2 * (i + 1) if t_need is not None else 1)
                    for n in range(2):
                        if i == 0:
                            arrived(pe, names[n])
                        r = r0 + 2 * i + n
                        if r - r0 >= 4:
                            pe.wait_ge(r_free, r - 3)
                        for k in range(KC):
                            last = mm(bank[r % 4][:, :], src[:, k, i * P:(i + 1) * P], slot(names[n])[:, k, :],
                                      start=(k == 0), stop=(k == KC - 1))
                        last.then_inc(r_full, 1)

            residual(("wo0", "wo1"), hTk, 0, TT[("mx", 0, 0)])

            h_transposes("h2", xn2, NT)
            pe.wait_ge(t_free, TT[("h2", NT - 1, 1)] + 1)
            pe.wait_ge(r_free, 2 * NT)
            nat_tiles("kv2")
            nat_tiles("kwvg", 280)
            nat_tiles("q2")

            pe.wait_ge(a_free, AT[("kwvg", NT - 1)] + 1)
            for n in range(4):
                if n == 2:
                    pe.wait_ge(rope_done, 1)
                for g in range(G2):
                    b = t_bank(("kv", n, g))
                    for i in range(NT):
                        last = nc.tensor.transpose(b[:, i * P:(i + 1) * P],
                                                   dup[:, n, i, g, :, :].rearrange("p r d -> p (r d)"), ident)
                    last.then_inc(t_full, 1)

            arrived(pe, "pool")
            for g in range(4):
                t_tiles("pool", ("pool", g), g, None)
            pe.wait_ge(t_free, TT[("kv", 1, G2 - 1)] + 1)
            for m, name in enumerate(("ck", "cv")):
                arrived(pe, name)
                b = a_bank((("hidk", "hidv")[m], 0))
                for c in range(2):
                    for j in range(16):
                        last = mm(b[:, 64 * c:64 * c + G2 * NC], slot(name, 256)[:, j, c * P:(c + 1) * P],
                                  blk[m][:, :, :, j].rearrange("p g c -> p (g c)"), start=(j == 0), stop=(j == 15))
                last.then_inc(a_full, 1)
            pe.wait_ge(rope_done, 2)
            for c in range(4):
                b = t_bank(("q2", c))
                for i in range(NT):
                    last = nc.tensor.transpose(b[:, i * P:(i + 1) * P], q2[:, i * 512 + c * P:i * 512 + (c + 1) * P], ident)
                last.then_inc(t_full, 1)
            arrived(pe, "ga0")
            for e in range(4):
                t_tiles("ga0", ("ga", e), e, None)
            pe.wait_ge(small2_in, 48)
            pe.wait_ge(a_free, AT[("hidv", 0)] + 1)
            b = a_bank(("kcmp", 0))
            for g in range(G2):
                for m in range(2):
                    last = mm(b[0:NC, g * HD:(g + 1) * HD], hidk[:, m, g, 0:NC], ccw[:, 0, m, :], start=(m == 0), stop=(m == 1))
            last.then_inc(a_full, 1)
            b = a_bank(("vcmp", 0))
            for g in range(G2):
                for m in range(2):
                    last = mm(b[:, g * HD:(g + 1) * HD], hidv[:, m, g, :, :].rearrange("p r c -> p (r c)"), ccw[:, 1, m, :],
                              start=(m == 0), stop=(m == 1))
            last.then_inc(a_full, 1)
            arrived(pe, "ga1")
            for e in range(4, 8):
                t_tiles("ga1", ("ga", e), e - 4, None)
            pe.wait_ge(kcn_done, 1)
            b = t_bank(("kcT", 0))
            for g in range(G2):
                last = nc.tensor.transpose(b[:, g * NCP:g * NCP + NC], kcn[0:NC, g, :, :].rearrange("p r d -> p (r d)"),
                                           ident[0:NC, 0:NC])
            last.then_inc(t_full, 1)
            pe.wait_ge(t_free, TT[("kcT", 0)] + 1)
            for n in range(2):
                for i in range(NT):
                    for m in range(NH // 2):
                        at = (i * NH // 2 + m) * NCP
                        last = mm(bank[6 + n][:, at:at + NCP], q2T[rows(n), m, i * P:(i + 1) * P],
                                  kcT[rows(n), m // 2, :], start=True, stop=True)
                last.then_inc(cs_full, 1)
            for g in range(4):
                pe.wait_ge(pooled, g + 1)
                mm(a_bank(("pm", g))[:, :], poolw[:, g, :], uT[:, g, :], start=True, stop=True).then_inc(a_full, 1)
            arrived(pe, "gb0")
            for e in range(2):
                t_tiles("gb0", ("gb", e), e, None)
            for n in range(2):
                pe.wait_ge(cp_done, 2)
                b = t_bank(("ec", n))
                for k in range(4):
                    last = nc.tensor.transpose(b[:, k * P:(k + 1) * P], ec[:, (4 * n + k) * P:(4 * n + k + 1) * P], ident)
                last.then_inc(t_full, 1)
            pe.wait_ge(a_free, AT[("vcmp", 0)] + 1)
            for i in range(NT):
                pe.wait_ge(t_free, TT[("ec", i // 2)] + 1)
                if i >= 2:
                    pe.wait_ge(co_free, i - 1)
                for g in range(G2):
                    last = mm(bank[6 + i % 2][:, g * 256:(g + 1) * 256], ecT[:, (2 * i + g) * P:(2 * i + g + 1) * P],
                              vdiag[:, g, :], start=True, stop=True)
                last.then_inc(co_full, 1)

            pe.wait_ge(co_free, NT)
            for t in range(NS + 3):
                attention(t, steps2, NS, lambda br, h: q2T[rows(h), h // 2, :], lambda br, h: kT2[br][rows(h), h // GROUP, :],
                          lambda br, h: v2[br][:, :, (h // GROUP) * HD:(h // GROUP + 1) * HD], logits2, probsT2)
                fill(fill2, t)
            pe.wait_ge(a_free, A2_END)
            pe.wait_ge(o_free, 2 * NS // NH)
            for i in range(NT):
                b = t_bank(("at", i))
                for k in range(4):
                    last = nc.tensor.transpose(b[:, k * P:(k + 1) * P], attn[:, i, k * P:(k + 1) * P], ident)
                last.then_inc(t_full, 1)
            pe.wait_ge(t_free, TT[("at", NT - 1)] + 1)
            arrived(pe, "ba")
            arrived(pe, "bp")
            R = 2 * NT
            for e in range(KC):
                for n, (name, src) in enumerate((("ba", aT), ("bp", pmT))):
                    r = R + 2 * e + n
                    if 2 * e + n >= 4:
                        pe.wait_ge(r_free, r - 3)
                    for k in range(4):
                        last = mm(bank[r % 4][:, :], slot(name, D)[:, k, e * P:(e + 1) * P], src[:, k, :],
                                  start=(k == 0), stop=(k == 3))
                    last.then_inc(r_full, 1)
            R += 2 * KC
            pe.wait_ge(mix_done, 1)
            residual(("w2o0", "w2o1"), gaT, R, None)
            R += 2 * NT
            h_transposes("h3", xn3, 2 * NT)
            pe.wait_ge(t_free, TT[("h3", NT - 1, 1)] + 1)
            pe.wait_ge(r_free, R)

            def three(b, w_n, cols, a_hi, a_lo, rows, weights_first, start, stop):
                for n, (wt, a) in enumerate(((w_hi, a_hi), (w_hi, a_lo), (w_lo, a_hi))):
                    lhs, rhs = wt[w_n][:, cols], a[:, rows]
                    if not weights_first:
                        lhs, rhs = rhs, lhs
                    last = mm(b[:, :], lhs, rhs, start=(start and n == 0), stop=(stop and n == 2))
                return last

            NF = DFF // P
            for c in range(NF):
                b = a_bank(("ff", c))
                pe.wait_ge(w_lo_done, c + 1)
                for k in range(KC):
                    last = three(b, c % 3, slice(k * P, (k + 1) * P), h3_hi, h3_lo, slice(k * S, (k + 1) * S), True, k == 0, k == KC - 1)
                last.then_inc(a_full, 1)
            pe.wait_ge(a_free, A2_END + NF)
            for k in range(NF):
                pe.wait_ge(w_lo_done, NF + k + 1)
                pe.wait_ge(ff_lo_done, k + 1)
                for i in range(NT):
                    for n in range(2):
                        last = three(bank[2 * i + n], (NF + k) % 3, slice(512 * n, 512 * (n + 1)), ff_hi[k % 3], ff_lo[k % 3],
                                     slice(i * P, (i + 1) * P), False, k == 0, k == NF - 1)
                        if k == NF - 1:
                            last.then_inc(r_full, 1)
                if k < NF - 1:
                    last.then_inc(unit_used, 1)

        @block.scalar
        def _(act):
            run = nc.scalar.activation

            def root(base, i):
                act.wait_ge(ms_done, base + i + 1)
                run(rs[:, base + i:base + i + 1], ss[:, base + i:base + i + 1], ACT.Sqrt).then_inc(sq_done, 1)

            def take(tile):
                n = AT[tile]
                kind, i = tile[0], tile[1]
                b = bank[n % 2]
                act.wait_ge(a_full, n + 1)
                if kind == "qi":
                    last = run(qiT[:, i, :], b[:, :], ACT.Copy)
                elif kind == "ki":
                    last = run(kiT, b[:, :], ACT.Copy)
                elif kind == "wi":
                    last = run(wi, b[:, 0:NT * IDX_HEADS].rearrange("p (i h) -> p i h", i=NT), ACT.Copy)
                elif kind in ("za", "zb"):
                    at = 0 if kind == "za" else 512
                    last = run(zz[:, i, at:at + 512], b[:, :], ACT.Silu)
                elif kind == "rel":
                    r = 4 * (i - 1) + tile[2]
                    if r >= 2:
                        act.wait_ge(rel_free, r - 1)
                    last = run(rels[r % 2][:, 0:(i + 1) * P], b[:, 0:(i + 1) * P], ACT.Relu, scale=IDX_SCALE)
                elif kind in ("va", "vb"):
                    last = run(v1[kind][:, i, :], b[:, :], ACT.Copy)
                elif kind in ("kb", "qb", "ka", "qa"):
                    order = ("kb", "qb", "ka", "qa")
                    run(raw[order.index(kind) % 2][:, i, :], b[:, :], ACT.Copy)
                    if kind[1] == "a" and i >= 2:
                        act.wait_ge(sq_free, NT * order.index(kind) + i - 1)
                    if kind == "qa" and i < 2:
                        act.wait_ge(sq_free, NT * 2 + i + 3)
                    last = run(squares_of[(kind, i)], b[:, :], ACT.Square)
                elif kind == "kv2":
                    twice = lambda n_, g: b[:, n_:n_ + g * HD].rearrange("p (g d) -> p g d", g=g).unsqueeze(2).to_broadcast([P, g, 2, HD])
                    for m in range(3):
                        run(dup[:, m, i, :, :, :], twice(m * P, G2), ACT.Copy)
                    last = run(v2["s"][:, i, :], b[:, 384:512], ACT.Copy)
                elif kind == "kwvg":
                    run(dup[:, 3, i, :, :, :], b[:, 0:P].rearrange("p (g d) -> p g d", g=G2).unsqueeze(2).to_broadcast([P, G2, 2, HD]), ACT.Copy)
                    run(v2["w"][:, i, :], b[:, P:2 * P], ACT.Copy)
                    last = run(gates[:, i, :], b[:, 256:280], ACT.Sigmoid)
                elif kind == "q2":
                    last = run(q2[:, i * 512:(i + 1) * 512], b[:, :], ACT.Copy)
                elif kind == "pool":
                    last = run(uT[:, i, :], b[:, :], ACT.Copy)
                elif kind == "hidk":
                    for c in range(2):
                        last = run(hidk[:, c, :, 0:NC], b[:, 64 * c:64 * c + G2 * NC].rearrange("p (g c) -> p g c", g=G2), ACT.Gelu_apprx_tanh)
                elif kind == "hidv":
                    for c in range(2):
                        for g in range(G2):
                            src = b[:, 64 * c + g * NC:64 * c + (g + 1) * NC].unsqueeze(1).to_broadcast([P, 4, NC])
                            last = run(hidv[:, c, g, :, 0:NC], src, ACT.Gelu_apprx_tanh)
                elif kind == "kcmp":
                    src = b[0:NC, 0:G2 * HD].rearrange("p (g d) -> p g d", g=G2).unsqueeze(2).to_broadcast([NC, G2, 2, HD])
                    last = run(kcn[0:NC, :, :, :], src, ACT.Copy)
                elif kind == "vcmp":
                    for r in range(4):
                        rows = slice(NCP * r, NCP * r + NCP)
                        last = run(vdiag[rows, :, r * HD:(r + 1) * HD], b[rows, 0:G2 * HD].rearrange("p (g d) -> p g d", g=G2), ACT.Copy)
                elif kind in ("ga", "gb"):
                    last = run((gaT if kind == "ga" else gbT)[:, i, :], b[:, :], ACT.Sigmoid)
                elif kind == "pm":
                    last = run(pmT[:, i, :], b[:, :], ACT.Copy, scale=small[:, V_PS + i:V_PS + i + 1])
                elif kind == "ff":
                    run(ffT[:, i, :], b[:, :], ACT.Relu).then_inc(relu_done, 1)
                    act.wait_ge(relu_done, i + 1)
                    last = run(ffT[:, i, :], ffT[:, i, :], ACT.Square)
                last.then_inc(a_free, 1)

            def exps(t, steps, base, dens, logits):
                act.wait_ge(l_done, base + t + 1)
                n = (steps[t][0] + 1) * P
                run(logits[t % 3][:, 0:n], logits[t % 3][:, 0:n], ACT.Exp, scale=-1.0, bias=negm[:, t:t + 1],
                    accum_out=dens[:, t:t + 1]).then_inc(e_done, 1)

            def raw_root(n):
                act.wait_ge(raw_ms, n + 1)
                run(rsq, ssq, ACT.Sqrt).then_inc(raw_sq, 1)

            def takes(work, t):
                for _, tile, k in [f for f in work if f[0] == t]:
                    if k == KC - 1:
                        take(tile)

            for i in range(NT):
                act.wait_ge(x_in, 16 * NT)
                if i > 0:
                    act.wait_ge(ss_done, i)
                run(junk[:, :], x[:, i, :], ACT.Square, accum_out=ss[:, i:i + 1]).then_inc(ss_done, 1)
                root(0, i)
            for tile in A1[:A1_DENSE]:
                if tile == ("kb", 0):
                    act.wait_ge(xn_done, NT)
                take(tile)
                if tile == ("qb", 1):
                    raw_root(0)
            raw_root(1)
            for t in range(NS):
                if t == HALF:
                    for tile in SEAM:
                        take(tile)
                exps(t, steps1, 0, den, logits1)
                if t == KA_ROOT:
                    raw_root(2)
                if t == QA_ROOT:
                    raw_root(3)
                takes(fill1, t)
            for i in range(NT):
                act.wait_ge(ss_done, NT + i)
                act.wait_ge(r_free, 2 * (i + 1))
                run(junk[:, :], x[:, i, :], ACT.Square, accum_out=ss[:, NT + i:NT + i + 1]).then_inc(ss_done, 1)
                root(NT, i)
            for tile in A2[:A2_DENSE]:
                if tile == ("hidk", 0):
                    act.wait_ge(zeroed, 1)
                if tile == ("gb", 0):
                    for n in range(2):
                        act.wait_ge(cl_done, n + 1)
                        run(ec_of[n], ec_of[n], ACT.Exp).then_inc(ce_done, 1)
                take(tile)
            for t in range(NS):
                exps(t, steps2, NS, den2, logits2)
                takes(fill2, t)
            for i in range(NT):
                act.wait_ge(ss_done, 2 * NT + i)
                act.wait_ge(r_free, R_OUT2 + 2 * (i + 1))
                run(junk[:, :], x[:, i, :], ACT.Square, accum_out=ss[:, 2 * NT + i:2 * NT + i + 1]).then_inc(ss_done, 1)
                root(2 * NT, i)
            for m in range(2 * NT):
                act.wait_ge(h3_tmp, m + 1)
                i, c = m // 2, m % 2
                run(h3_hi[:, :].rearrange("p (k s) -> p k s", k=KC)[:, 4 * c:4 * c + 4, i * P:(i + 1) * P],
                    junk[:, 512 * c:512 * c + 512].rearrange("p (k s) -> p k s", k=4), ACT.Copy).then_inc(h3_hi_done, 1)

            def unit_raw(m):
                if m < NF:
                    return slot(f"f1_{m // 4}")[:, :, (m % 4) * P:(m % 4 + 1) * P], w_hi[m % 3][:, :].rearrange("p (k n) -> p k n", k=KC)
                k = m - NF
                return slot(f"f2_{k // 4}", D)[:, k % 4, :], w_hi[m % 3][:, :]

            def unit_hi(m):
                if m % 4 == 0:
                    arrived(act, f"f{1 + m // NF}_{m % NF // 4}")
                if 1 <= m <= 2:
                    act.wait_ge(t_full, TT[("h3", NT - 1, 1)] + 1)
                if m >= NF + 3:
                    act.wait_ge(unit_used, m - NF - 2)
                elif m >= 3:
                    act.wait_ge(a_full, AT[("ff", m - 3)] + 1)
                src, dst = unit_raw(m)
                run(dst, src, ACT.Copy).then_inc(w_hi_done, 1)

            NF = DFF // P
            for m in range(3):
                unit_hi(m)
            for c in range(NF):
                if c + 3 < NF + 1:
                    unit_hi(c + 3)
                take(("ff", c))
            for k in range(NF):
                if k == 1:
                    act.wait_ge(a_full, A2_END + NF)
                if k >= 3:
                    act.wait_ge(unit_used, k - 2)
                run(ff_hi[k % 3][:, :], ffT[:, k, :], ACT.Copy).then_inc(ff_hi_done, 1)
                if NF + k + 1 < 2 * NF:
                    unit_hi(NF + k + 1)
            for i in range(NT):
                act.wait_ge(ss_done, 3 * NT + i)
                act.wait_ge(r_free, R_FF + 2 * (i + 1))
                run(junk[:, :], x[:, i, :], ACT.Square, accum_out=ssf[:, i:i + 1]).then_inc(ss_done, 1)
                act.wait_ge(ms_done, 3 * NT + i + 1)
                run(rsf[:, i:i + 1], ssf[:, i:i + 1], ACT.Sqrt).then_inc(sq_done, 1)

        @block.vector
        def _(dve):
            v = nc.vector
            count = [0]

            def step(ins):
                count[0] += 1
                ins.then_inc(dve_step, 1)
                dve.wait_ge(dve_step, count[0])

            def norm(base, i, xn):
                dve.wait_ge(ss_done, base + i + 1)
                v.tensor_scalar(ss[:, base + i:base + i + 1], ss[:, base + i:base + i + 1], 1.0 / D, EPS, ALU.mult, ALU.add)\
                    .then_inc(ms_done, 1)
                dve.wait_ge(sq_done, base + i + 1)
                step(v.reciprocal(rs[:, base + i:base + i + 1], rs[:, base + i:base + i + 1]))
                v.tensor_scalar(xn[:, i, :], x[:, i, :], rs[:, base + i:base + i + 1], None, ALU.mult).then_inc(xn_done, 1)

            def take_h(name, i, gains):
                for c in range(2):
                    n = TT[(name, i, c)]
                    dve.wait_ge(t_full, n + 1)
                    src = bank[4 + n % 2][:, :].rearrange("p (k s) -> p k s", k=4)
                    dst = hTk[:, 4 * c:4 * c + 4, i * P:(i + 1) * P]
                    if gains is None:
                        v.tensor_copy(dst, src).then_inc(t_free, 1)
                    else:
                        g = small[:, gains + 4 * c:gains + 4 * c + 4].unsqueeze(2).to_broadcast([P, 4, P])
                        v.tensor_tensor(dst, src, g, ALU.mult).then_inc(t_free, 1)

            def head_sum(n, g, i):
                dve.wait_ge(a_free, AT[(g, i)] + 1)
                v.tensor_reduce(ssq[:, NH * i:NH * (i + 1)], squares_of[(g, i)].rearrange("p (h d) -> p h d", d=HD), AX.X, ALU.add)\
                    .then_inc(sq_free, 1)
                if i == NT - 1:
                    dve.wait_ge(sq_free, NT * (n + 1))
                    v.tensor_scalar(ssq, ssq, 1.0 / HD, EPS, ALU.mult, ALU.add).then_inc(raw_ms, 1)

            def head_scale(n):
                dve.wait_ge(raw_sq, n + 1)
                step(v.reciprocal(rsq, rsq))
                allh = raw[n % 2].rearrange("p i (h d) -> p (i h) d", d=HD)
                v.tensor_tensor(allh, allh, rsq.unsqueeze(2).to_broadcast([P, NT * NH, HD]), ALU.mult).then_inc(raw_done, 1)

            def take_raw(g, gain, chunks=range(4)):
                for c in chunks:
                    n = TT[(g, c)]
                    dve.wait_ge(t_full, n + 1)
                    v.tensor_scalar(qkT[g][:, c, :], bank[4 + n % 2][:, :], small[:, gain:gain + 1],
                                    SCALE if g[0] == "q" else 1.0, ALU.mult, ALU.mult).then_inc(t_free, 1)

            def attention(t, steps, base, bias, finish, logits, probsT):
                if t < NS:
                    i, br, h = steps[t]
                    n = (i + 1) * P
                    b = bias(t)
                    dve.wait_ge(s_full, base + t + 1)
                    if t >= 3:
                        dve.wait_ge(t_full, TT[("pt", base + t - 3)] + 1)
                    v.tensor_tensor_reduce(logits[t % 3][:, 0:n], bank[2 + t % 2][:, 0:n], b, -1.0, BIG, ALU.add, ALU.min,
                                           negm[:, t:t + 1]).then_inc(l_done, 1)
                u = t - 2
                if 0 <= u < NS:
                    k = TT[("pt", base + u)]
                    n = (steps[u][0] + 1) * P
                    dve.wait_ge(t_full, k + 1)
                    if u >= 2:
                        dve.wait_ge(pv_done, base + u - 1)
                    v.tensor_copy(probsT[u % 2][:, 0:n], bank[4 + k % 2][:, 0:n]).then_inc(t_free, 1)
                if t >= 10 and (t - 3) % NH == NH - 1:
                    o = (t - 3) // NH
                    dve.wait_ge(pv_done, base + NH * (o + 1))
                    finish(o)

            dve.wait_ge(table_in, 48)
            dve.wait_ge(vec_full, 1)
            v.tensor_tensor(vec[:, 0:512], bank[6][0:2 * NH, 0:512], add_sb[:, 0:512], ALU.add)
            v.tensor_tensor(vec[:, 512:VEC], bank[7][0:2 * NH, 0:P], add_sb[:, 512:VEC], ALU.add).then_inc(vec_done, 1)
            dve.wait_ge(consts_in, 32)
            for i in range(NT):
                norm(0, i, xn1)
                if i > 0:
                    take_h("h1", i - 1, V_G1)
            take_h("h1", NT - 1, V_G1)

            dve.wait_ge(a_free, AT[("wi", 0)] + 1)
            for i in range(1, NT):
                n = (i + 1) * P
                s = score_of[i]
                for h in range(IDX_HEADS):
                    r = 4 * (i - 1) + h
                    dve.wait_ge(a_free, AT[("rel", i, h)] + 1)
                    if h == 0:
                        ins = v.tensor_scalar(s, rels[r % 2][:, 0:n], wi[:, i, 0:1], None, ALU.mult)
                    else:
                        ins = v.scalar_tensor_tensor(s, rels[r % 2][:, 0:n], wi[:, i, h:h + 1], s, ALU.mult, ALU.add)
                    ins.then_inc(rel_free, 1)
                    dve.wait_ge(rel_free, r + 1)
                step(v.tensor_tensor(s[:, i * P:n], s[:, i * P:n], consts[:, C_DIAG:C_DIAG + P], ALU.add))
            for i in range(1, NT):
                s = score_of[i]
                for _ in range(TOPK // 8):
                    step(v.max(top8, s))
                    step(v.match_replace(s, top8, s, TAKEN))

            dve.wait_ge(vec_out, 16)
            for n, g in enumerate(("kb", "qb")):
                for i in range(NT):
                    head_sum(n, g, i)
                head_scale(n)
            take_raw("kb", V_KB)
            take_raw("qb", V_QB)

            combo_of = {t: c for c, t in enumerate(combos)}

            def bias1(t):
                i, br, h = steps1[t]
                if t in combo_of:
                    dve.wait_ge(combo_done, combo_of[t] + 1)
                    return combo[combo_of[t] % 2][:, 0:(i + 1) * P]
                return strips[:, (h if br == "a" else NH + h), (NT - 1 - i) * P:S]

            def finish1(o):
                i, br, _ = steps1[NH * o]
                at = 0 if br == "a" else 512
                dve.wait_ge(e_done, NH * (o + 1))
                dve.wait_ge(a_free, AT[("z" + br, i)] + 1)
                step(v.reciprocal(gr, den[:, NH * o:NH * (o + 1)]))
                z = zz[:, i, at:at + 512]
                zh = z.rearrange("p (h d) -> p h d", h=NH)
                step(v.tensor_tensor(zh, zh, gr.unsqueeze(2).to_broadcast([P, NH, HD]), ALU.mult))
                v.tensor_tensor(z, z, bank[6 + o % 2][:, :], ALU.mult).then_inc(o_free, 1)

            def sums(work, t, n, g):
                for at, tile, k in work:
                    if at == t - 1 and k == KC - 1 and tile[0] == g:
                        head_sum(n, g, tile[1])

            dve.wait_ge(strips_in, 16 * P // COPIES)
            for t in range(NS + 3):
                if t == HALF:
                    take_raw("qa", V_QA)
                attention(t, steps1, 0, bias1, finish1, logits1, probsT1)
                sums(fill1, t, 2, "ka")
                sums(fill1, t, 3, "qa")
                if t == KA_NORM:
                    head_scale(2)
                if KA_TURN <= t < KA_TURN + 4:
                    take_raw("ka", V_KA, [t - KA_TURN])
                if t == MASKS:
                    for i in range(1, NT):
                        v.tensor_scalar(mask_of[i], score_of[i], TAKEN, NEG, ALU.not_equal, ALU.mult).then_inc(masks_done, 1)
                    dve.wait_ge(masks_done, NT - 1)
                if t == QA_ROOT:
                    head_scale(3)

            def add_x(r0, then=None):
                for i in range(NT):
                    for n in range(2):
                        r = r0 + 2 * i + n
                        dve.wait_ge(r_full, r + 1)
                        xs = x[:, i, n * 512:(n + 1) * 512]
                        v.tensor_tensor(xs, xs, bank[r % 4][:, :], ALU.add).then_inc(r_free, 1)
                    then(i)

            for i in range(NT):
                take_h("mx", i, None)
            dve.wait_ge(x_in, 2 * 16 * NT)

            def then2(i):
                if i > 0:
                    norm(NT, i - 1, xn2)

            add_x(0, then2)
            norm(NT, NT - 1, xn2)
            for i in range(NT):
                take_h("h2", i, V_G2)

            def rope(view, heads, cos, sin, n=P, tiles=NT):
                x1, x2 = view[:, :, :, 0:ROT], view[:, :, :, ROT:2 * ROT]
                size = tiles * heads * ROT
                tmp = [r[0:n, 0:size].rearrange("p (i h d) -> p i h d", i=tiles, h=heads) for r in rope_tmp]
                v.tensor_tensor(tmp[0], x1, cos, ALU.mult)
                v.tensor_tensor(tmp[1], x2, sin, ALU.mult)
                v.tensor_tensor(tmp[2], x2, cos, ALU.mult)
                step(v.tensor_tensor(tmp[3], x1, sin, ALU.mult))
                v.tensor_tensor(x1, tmp[0], tmp[1], ALU.subtract)
                return v.tensor_tensor(x2, tmp[2], tmp[3], ALU.add)

            def angles(at, heads):
                return consts[:, at:at + NT * ROT].rearrange("p (i d) -> p i d", i=NT).unsqueeze(2).to_broadcast([P, NT, heads, ROT])

            dve.wait_ge(a_free, AT[("kwvg", NT - 1)] + 1)
            for m in (2, 3):
                last = rope(dup[:, m, :, :, :, :].rearrange("p i g r d -> p i (g r) d"), 4, angles(C_COS, 4), angles(C_SIN, 4))
                if m == 2:
                    step(last)
            last.then_inc(rope_done, 1)
            dve.wait_ge(rope_done, 1)
            for m in range(2):
                pe_at = (V_PEK, V_PEV)[m]
                for g in range(G2):
                    n = TT[("kv", m, g)]
                    dve.wait_ge(t_full, n + 1)
                    for half in range(2):
                        rows = slice(half * HD, (half + 1) * HD)
                        src = bank[4 + n % 2][rows, 16 * half:16 * half + NC * 16].rearrange("p (c j) -> p c j", j=16)
                        pos = small[rows, pe_at:pe_at + 16].unsqueeze(1).to_broadcast([HD, NC, 16])
                        last = v.tensor_tensor(blk[m][rows, g, :, :], src, pos, ALU.add)
                        if half == 0:
                            step(last)
                    last.then_inc(t_free, 1)
            for m, br in ((2, "s"), (3, "w")):
                for g in range(G2):
                    n = TT[("kv", m, g)]
                    dve.wait_ge(t_full, n + 1)
                    v.tensor_copy(kT2[br][:, g, :], bank[4 + n % 2][:, :]).then_inc(t_free, 1)
            dve.wait_ge(a_free, AT[("q2", NT - 1)] + 1)
            q2h = q2.rearrange("p (i h d) -> p i h d", i=NT, h=NH)
            rope(q2h, NH, angles(C_COS, NH), angles(C_SIN, NH)).then_inc(rope_done, 1)
            for c in range(4):
                n = TT[("q2", c)]
                dve.wait_ge(t_full, n + 1)
                v.tensor_scalar(q2T[:, c, :], bank[4 + n % 2][:, :], SCALE, None, ALU.mult).then_inc(t_free, 1)
            dve.wait_ge(a_free, AT[("kcmp", 0)] + 1)
            dve.wait_ge(rope_done, 2)
            pcos = consts[0:NC, C_PCOS:C_PCOS + ROT].unsqueeze(1).unsqueeze(1).to_broadcast([NC, 1, 4, ROT])
            psin = consts[0:NC, C_PSIN:C_PSIN + ROT].unsqueeze(1).unsqueeze(1).to_broadcast([NC, 1, 4, ROT])
            rope(kcn[0:NC, :, :, :].rearrange("p g r d -> p (g r) d").unsqueeze(1), 4, pcos, psin, NC, 1).then_inc(kcn_done, 1)
            n = TT[("kcT", 0)]
            dve.wait_ge(t_full, n + 1)
            dve.wait_ge(zeroed, 1)
            v.tensor_copy(kcT[:, :, 0:NC], bank[4 + n % 2][:, 0:G2 * NCP].rearrange("p (g c) -> p g c", g=G2)[:, :, 0:NC]).then_inc(t_free, 1)
            quads = lambda a: a.rearrange("p (i m) c -> p i m c", i=NT)
            per_tile = lambda at: consts[:, at:at + NT * NCP].rearrange("p (i c) -> p i c", i=NT).unsqueeze(2).to_broadcast([P, NT, NH // 2, NCP])
            for n in range(2):
                e = ec_of[n]
                m = cm[:, 16 * n:16 * n + 16]
                dve.wait_ge(cs_full, n + 1)
                step(v.tensor_tensor(quads(e), bank[6 + n][:, :].rearrange("p (i m c) -> p i m c", i=NT, c=NCP), per_tile(C_CADD), ALU.add))
                step(v.tensor_reduce(m, e, AX.X, ALU.max))
                v.tensor_tensor(e, e, m.unsqueeze(2).to_broadcast([P, 16, NCP]), ALU.subtract).then_inc(cl_done, 1)
            for n in range(2):
                dve.wait_ge(ce_done, n + 1)
                v.tensor_tensor(quads(ec_of[n]), quads(ec_of[n]), per_tile(C_C01), ALU.mult).then_inc(cp_done, 1)
            dve.wait_ge(cp_done, 2)
            step(v.tensor_reduce(cden, ec.rearrange("p (m c) -> p m c", c=NCP), AX.X, ALU.add))
            step(v.tensor_scalar(cden, cden, 1e-30, None, ALU.max))
            step(v.reciprocal(cden, cden))
            cdh = cden.rearrange("p (i h) -> p i h", i=NT)
            step(v.tensor_tensor(cdh, cdh, gates[:, :, 0:NH], ALU.mult))
            for n in range(2):
                k = TT[("ec", n)]
                dve.wait_ge(t_full, k + 1)
                v.tensor_copy(ecT[:, 512 * n:512 * n + 512], bank[4 + k % 2][:, :]).then_inc(t_free, 1)
            heads = lambda a: a.rearrange("p (h d) -> p h d", h=NH)
            for i in range(NT):
                dve.wait_ge(co_full, i + 1)
                v.tensor_tensor(heads(attn[:, i, :]), heads(bank[6 + i % 2][:, :]),
                                cden[:, NH * i:NH * (i + 1)].unsqueeze(2).to_broadcast([P, NH, HD]), ALU.mult).then_inc(co_free, 1)

            def bias2(t):
                return strip0[:, (NT - 1 - steps2[t][0]) * P:S]

            def finish2(o):
                i, br, _ = steps2[NH * o]
                dve.wait_ge(e_done, NS + NH * (o + 1))
                at = NH if br == "s" else 2 * NH
                step(v.reciprocal(gr, den2[:, NH * o:NH * (o + 1)]))
                step(v.tensor_tensor(gr, gr, gates[:, i, at:at + NH], ALU.mult))
                part = heads(junk[:, 0:512])
                v.tensor_tensor(part, heads(bank[6 + o % 2][:, :]), gr.unsqueeze(2).to_broadcast([P, NH, HD]), ALU.mult).then_inc(o_free, 1)
                dve.wait_ge(o_free, NS // NH + o + 1)
                step(v.tensor_tensor(attn[:, i, :], attn[:, i, :], junk[:, 0:512], ALU.add))

            dve.wait_ge(co_free, NT)
            for t in range(NS + 3):
                attention(t, steps2, NS, bias2, finish2, logits2, probsT2)
            for i in range(NT):
                n = TT[("at", i)]
                dve.wait_ge(t_full, n + 1)
                v.tensor_copy(aT[:, :, i * P:(i + 1) * P], bank[4 + n % 2][:, :].rearrange("p (k s) -> p k s", k=4)).then_inc(t_free, 1)
            R = 2 * NT
            for e in range(KC):
                for n, g in enumerate((gaT, gbT)):
                    r = R + 2 * e + n
                    dve.wait_ge(r_full, r + 1)
                    v.tensor_tensor(g[:, e, :], g[:, e, :], bank[r % 4][:, :], ALU.mult).then_inc(r_free, 1)
                dve.wait_ge(r_free, R + 2 * e + 2)
                last = v.tensor_tensor(gaT[:, e, :], gaT[:, e, :], gbT[:, e, :], ALU.add)
            last.then_inc(mix_done, 1)
            R += 2 * KC

            def then3(i):
                if i > 0:
                    norm(2 * NT, i - 1, xn3)

            add_x(R, then3)
            norm(2 * NT, NT - 1, xn3)
            R += 2 * NT
            for m in range(2 * NT):
                i, c = m // 2, m % 2
                n = TT[("h3", i, c)]
                tmp = junk[:, 512 * c:512 * c + 512].rearrange("p (k s) -> p k s", k=4)
                dve.wait_ge(t_full, n + 1)
                v.tensor_tensor(tmp, bank[4 + n % 2][:, :].rearrange("p (k s) -> p k s", k=4),
                                small[:, V_G3 + 4 * c:V_G3 + 4 * c + 4].unsqueeze(2).to_broadcast([P, 4, P]), ALU.mult).then_inc(h3_tmp, 1)
                dve.wait_ge(h3_tmp, m + 1)
                dve.wait_ge(h3_hi_done, m + 1)
                part = lambda t: t[:, :].rearrange("p (k s) -> p k s", k=KC)[:, 4 * c:4 * c + 4, i * P:(i + 1) * P]
                v.tensor_tensor(part(h3_lo), tmp, part(h3_hi).bitcast(F32), ALU.subtract).then_inc(t_free, 1)

            def unit_lo(m):
                dve.wait_ge(w_hi_done, m + 1)
                if m < NF:
                    src, cut = slot(f"f1_{m // 4}")[:, :, (m % 4) * P:(m % 4 + 1) * P], lambda t: t[:, :].rearrange("p (k n) -> p k n", k=KC)
                else:
                    src, cut = slot(f"f2_{(m - NF) // 4}", D)[:, (m - NF) % 4, :], lambda t: t[:, :]
                v.tensor_tensor(cut(w_lo[m % 3]), src, cut(w_hi[m % 3]).bitcast(F32), ALU.subtract).then_inc(w_lo_done, 1)

            NF = DFF // P
            for m in range(NF + 1):
                unit_lo(m)
            for k in range(NF):
                dve.wait_ge(ff_hi_done, k + 1)
                v.tensor_tensor(ff_lo[k % 3][:, :], ffT[:, k, :], ff_hi[k % 3][:, :].bitcast(F32), ALU.subtract).then_inc(ff_lo_done, 1)
                if NF + k + 1 < 2 * NF:
                    unit_lo(NF + k + 1)
            for i in range(NT):
                for n in range(2):
                    r = R + 2 * i + n
                    dve.wait_ge(r_full, r + 1)
                    xs = x[:, i, n * 512:(n + 1) * 512]
                    v.tensor_tensor(xs, xs, bank[2 * i + n][:, :], ALU.add).then_inc(r_free, 1)
            dve.wait_ge(gfin_in, 16)
            for i in range(NT):
                dve.wait_ge(ss_done, 3 * NT + i + 1)
                v.tensor_scalar(ssf[:, i:i + 1], ssf[:, i:i + 1], 1.0 / D, EPS, ALU.mult, ALU.add).then_inc(ms_done, 1)
                dve.wait_ge(sq_done, 3 * NT + i + 1)
                step(v.reciprocal(rsf[:, i:i + 1], rsf[:, i:i + 1]))
                v.scalar_tensor_tensor(x[:, i, :], x[:, i, :], rsf[:, i:i + 1], gfin, ALU.mult, ALU.mult).then_inc(y_done, 1)

        @block.gpsimd
        def _(pool):
            g = nc.gpsimd
            pool.wait_ge(vec_done, 1)
            pool.dma_start(copies.rearrange("m h x -> h m x"), vec.unsqueeze(1).to_broadcast([2 * NH, COPIES, VEC]))\
                .then_inc(vec_out, 16)
            pool.wait_ge(vec_out, 16)
            pitch = 2 * NH * VEC
            for p in range(0, P, COPIES):
                diagonal = bass.AP(copies.tensor, P - 1 - p, [[pitch - 1, COPIES], [VEC, 2 * NH], [1, S]])
                pool.dma_start(strips[p:p + COPIES, :, :], diagonal).then_inc(strips_in, 16)
            pool.wait_ge(strips_in, 16 * P // COPIES)
            pool.wait_ge(masks_done, NT - 1)
            pool.wait_ge(raw_done, 4)
            for c, t in enumerate(combos):
                i, _, h = steps1[t]
                if c >= 2:
                    pool.wait_ge(l_done, combos[c - 2] + 1)
                g.tensor_tensor(combo[c % 2][:, 0:(i + 1) * P], strips[:, h, (NT - 1 - i) * P:S], mask_of[i], ALU.add)\
                    .then_inc(combo_done, 1)
            pool.wait_ge(xn_done, 2 * NT)
            pool.wait_ge(t_free, TT[("mx", NT - 1, 1)] + 1)
            for z in (hidk, hidv, kcT):
                g.memset(z, 0.0)
            g.memset(vdiag, 0.0).then_inc(zeroed, 1)
            chain = [0]

            def link(ins):
                chain[0] += 1
                ins.then_inc(pool_chain, 1)
                pool.wait_ge(pool_chain, chain[0])

            for n, width in enumerate(POOL_WINDOWS):
                pool.wait_ge(a_free, AT[("pool", n)] + 1)
                src, shift, k = uT[:, n, :], 1, 0
                while shift < width:
                    dst = ptmp[k % 2]
                    g.tensor_copy(dst[:, 0:shift], src[:, 0:shift])
                    link(g.tensor_tensor(dst[:, shift:S], src[:, shift:S], src[:, 0:S - shift], ALU.add))
                    src, shift, k = dst, 2 * shift, k + 1
                g.tensor_tensor(src[:, 0:16], src[:, 0:16], consts[:, C_INV + 16 * n:C_INV + 16 * n + 16], ALU.mult)
                link(g.tensor_scalar(src[:, 16:S], src[:, 16:S], 1.0 / width, None, ALU.mult))
                g.tensor_tensor(uT[:, n, :], src, uT[:, n, :], ALU.subtract).then_inc(pooled, 1)
                pool.wait_ge(pooled, n + 1)


_CONSTANTS = ("consts", "onehot", "vec_add")
_DIRECT = ("x", "rel_bias", "w_in", "w_out", "w_in_2", "cmp_k_w1_2", "cmp_k_w2_2", "cmp_v_w1_2", "cmp_v_w2_2",
           "w_branch_attn_2", "pool_w_2", "w_branch_pool_2", "w_out_2", "w_ff1_2", "w_ff2_2")


def kernel(**inputs):
    from concourse import bacc
    from concourse.bass_utils import run_bass_kernel_spmd

    a = {k: np.asarray(v) for k, v in inputs.items()}
    arrays = dict(zip(_CONSTANTS, shape_constants()))
    for name in _DIRECT:
        arr = a[name]
        arrays[name] = np.ascontiguousarray(arr if name in ("x", "rel_bias") else arr[0])
    arrays["norm_final_2"] = np.ascontiguousarray(a["norm_final_2"].reshape(1, D))
    per_chunk = lambda g: g.reshape(-1, P).T
    per_head = lambda g: np.concatenate([g[0], g[0]])[:, None]
    blocks = lambda pe: pe[0].reshape(2, 16, HD).transpose(0, 2, 1).reshape(P, 16)
    arrays["small"] = np.ascontiguousarray(np.concatenate(
        [per_chunk(a["norm_gain"][0]), per_chunk(a["norm_mix_2"][0]), per_chunk(a["norm_mlp_2"][0]),
         per_head(a["q_norm_b"]), per_head(a["k_norm_b"]), per_head(a["q_norm_a"]), per_head(a["k_norm_a"]),
         per_chunk(a["pool_scale_2"][0]), blocks(a["cmp_pe_k_2"]), blocks(a["cmp_pe_v_2"])], axis=1))
    nc = bacc.Bacc("TRN2", target_bir_lowering=False, num_devices=1)
    w = {n: nc.dram_tensor(f"in_{n}", v.shape, F32, kind="ExternalInput").ap() for n, v in arrays.items()}
    out = nc.dram_tensor("out", (1, S, D), F32, kind="ExternalOutput").ap()
    build(nc, w, out)
    r = run_bass_kernel_spmd(nc, [{f"in_{n}": v for n, v in arrays.items()}], core_ids=[0])
    return r.results[0]["out"]
```

```python
from contextlib import ExitStack

import numpy as np

import concourse.bass as bass
from concourse import mybir

F32 = mybir.dt.float32
F32R = mybir.dt.float32r
ALU = mybir.AluOpType
ACT = mybir.ActivationFunctionType
AX = mybir.AxisListType

P = 128
S = 512
D = 1024
NT = S // P
KC = D // P
HD = 64
NH = 8
EPS = 1e-6
SCALE = HD ** -0.5
TOPK = min(256, S // 4)
N_BUCKETS = 32
IDX_HEADS = 4
IDX_SCALE = (IDX_HEADS * HD) ** -0.5
NEG = -1e30
FUTURE = -3.0e38
TAKEN = -3.4e38
BIG = 3.0e38
DFF = 4 * D
VEC = S + P

QA, KA, VA, ZA, QI, KI, WI, QB, KB, VB, ZB = np.cumsum([0, 512, 512, 512, 512, 256, 64, 4, 512, 512, 512]).tolist()
Q2, KV2, KWVG, POOL, MERGE = 0, 512, 1024, 1304, 1816
GATES = 24
G2 = 2
GROUP = NH // G2
ROT = 8
CMP_BLOCK, CMP_STRIDE = 32, 16
NC = (S - CMP_BLOCK) // CMP_STRIDE + 1
NCP = NC + 1
POOL_WINDOWS = (2, 4, 8, 16)
THETA = 500000.0

C_ID, C_DIAG, C_STRIP, C_COS, C_SIN, C_CADD, C_C01, C_PCOS, C_PSIN, C_INV, C_HEADS, C_END = np.cumsum(
    [0, P, P, S, NT * ROT, NT * ROT, NT * NCP, NT * NCP, ROT, ROT, 4 * 16, 2 * NH - 2]).tolist()
V_G1, V_G2, V_G3, V_QB, V_KB, V_QA, V_KA, V_PS, V_PEK, V_PEV, V_END = np.cumsum(
    [0, KC, KC, KC, 1, 1, 1, 1, 4, 16, 16]).tolist()

COPIES = 16
RING = 3
SLOT = 8 * 512
UNIT = 1024
RAW_UNITS, HI_UNITS = 5, 4


def shape_constants():
    c = np.zeros((P, C_END), np.float32)
    p = np.arange(P)[:, None]
    c[:, C_ID:C_ID + P] = np.eye(P)
    c[:, C_DIAG:C_DIAG + P] = np.where(np.arange(P)[None, :] > p, FUTURE, 0)
    c[:, C_STRIP:C_STRIP + S] = np.where((S - P) + p - np.arange(S)[None, :] < 0, NEG, 0)
    inv = THETA ** (-np.arange(0, 2 * ROT, 2, dtype=np.float32) / np.float32(2 * ROT))
    t = np.arange(S, dtype=np.float32)
    ang = (t[:, None] * inv.astype(np.float32)).astype(np.float32)
    tiled = lambda a: a.reshape(NT, P, -1).transpose(1, 0, 2).reshape(P, -1)
    c[:, C_COS:C_COS + NT * ROT] = tiled(np.cos(ang))
    c[:, C_SIN:C_SIN + NT * ROT] = tiled(np.sin(ang))
    pos = np.arange(NC) * CMP_STRIDE + CMP_BLOCK - 1
    seen = np.zeros((S, NCP), bool)
    seen[:, :NC] = pos[None, :] <= np.arange(S)[:, None]
    c[:, C_CADD:C_CADD + NT * NCP] = tiled(np.where(seen, 0, NEG))
    c[:, C_C01:C_C01 + NT * NCP] = tiled(seen.astype(np.float32))
    pang = (pos.astype(np.float32)[:, None] * inv.astype(np.float32)).astype(np.float32)
    c[:NC, C_PCOS:C_PCOS + ROT] = np.cos(pang)
    c[:NC, C_PSIN:C_PSIN + ROT] = np.sin(pang)
    for g, w in enumerate(POOL_WINDOWS):
        c[:, C_INV + 16 * g:C_INV + 16 * g + 16] = 1.0 / np.minimum(np.arange(16) + 1, w)
    c[:HD, C_HEADS + NH - 2] = 1
    c[HD:, C_HEADS + NH - 1] = 1
    spread = np.kron(np.eye(NH), np.ones((1, HD))).astype(np.float32)
    d = (S - 1) - np.arange(VEC)
    df = np.maximum(d, 1).astype(np.float32)
    half = N_BUCKETS // 2
    large = half + (np.log(df / np.float32(half)) / np.float32(np.log(128 / half)) * np.float32(half)).astype(np.int32)
    bucket = np.where(d < half, np.maximum(d, 0), np.minimum(large, N_BUCKETS - 1))
    onehot = (bucket[None, :] == np.arange(N_BUCKETS)[:, None]).astype(np.float32)
    times = ((d <= 128).astype(int) + (d % 4 == 0) + (d % 16 == 0)) * (d >= 0)
    add = np.zeros((2 * NH, VEC), np.float32)
    add[:NH] = np.where(d >= 0, 0, NEG)
    add[NH:] = np.where(times > 0, np.log(np.maximum(times, 1)), NEG)
    return c, onehot, add, spread


def weight_groups(w):
    def cols(a, c, n, at=0, width=512):
        return (at, n, width, a[:, c:c + n].rearrange("(k p) n -> p k n", p=P))

    def whole(a, k, n):
        return (0, n, n, a.rearrange("(k p) n -> p k n", p=P))

    groups = [(f"wo{n}", [cols(w["w_out"], 512 * n, 512)]) for n in range(2)]
    groups += [("block2", [])]
    groups += [(f"w2o{n}", [cols(w["w_out_2"], 512 * n, 512)]) for n in range(2)]
    groups += [(f"f1_{n}", [cols(w["w_ff1_2"], 512 * n, 512)]) for n in range(8)]
    groups += [(f"f2_{n}", [whole(w["w_ff2_2"][512 * n:512 * (n + 1), :], 4, D)]) for n in range(8)]
    return groups


ORDER = ("kb", "qb", "ka", "qa")
NATS = ("vb", "va", "kv2", "kwvg", "q2")


def weight_units(w):
    w1, w2 = w["w_in"], w["w_in_2"]

    def rows(a, c, n, u):
        return (n, [(0, n, a[2 * u * P:2 * (u + 1) * P, c:c + n].rearrange("(k p) n -> p k n", p=P))])

    def cols(a, c, n=P, at=0):
        return (at, n, a[:, c:c + n].rearrange("(k p) n -> p k n", p=P))

    def many(a, name, c, count=4):
        return [(name, e, P, [cols(a, c + P * e)]) for e in range(count)]

    def nats(a, name, c, n=512):
        return [(name, u, *rows(a, c, n, u)) for u in range(4)]

    units = many(w1, "qi", QI, 2) + [("ki", 0, P, [cols(w1, KI, HD), cols(w1, KI, HD, HD)])]
    units += [("wi", 0, IDX_HEADS, [cols(w1, WI, IDX_HEADS)])]
    units += many(w1, "kb", KB) + many(w1, "qb", QB) + nats(w1, "vb", VB) + nats(w1, "va", VA)
    units += many(w1, "ka", KA) + many(w1, "qa", QA) + many(w1, "zb", ZB) + many(w1, "za", ZA)
    units += nats(w2, "kv2", KV2) + nats(w2, "kwvg", KWVG, 280) + nats(w2, "q2", Q2)
    units += many(w2, "pool", POOL) + many(w2, "ga", MERGE, KC) + many(w2, "gb", MERGE + D, KC)
    branch = [[(4 * P * n, 4 * P, P, w[a][:, P * e:P * (e + 1)].rearrange("(k p) n -> p k n", p=P))
               for n, a in enumerate(("w_branch_attn_2", "w_branch_pool_2"))] for e in range(KC)]
    return units, branch


def build(nc, w, out):
    groups = weight_groups(w)
    number = {name: n for n, (name, _) in enumerate(groups)}
    units, branch = weight_units(w)
    unit_of = {(name, k): u for u, (name, k, _, _) in enumerate(units)}
    U2 = unit_of[("kv2", 0)]
    copies = nc.dram_tensor("bias_copies", (COPIES, 2 * NH, VEC), F32).ap()

    steps1 = [(i, br, h) for br in ("b", "a") for i in range(NT) for h in range(NH)]
    steps2 = [(i, br, h) for i in range(NT) for br in ("s", "w") for h in range(NH)]
    combos = [t for t, (i, br, h) in enumerate(steps1) if br == "a" and i > 0]
    NS = len(steps1)
    HALF = NS // 2

    FILL1 = [(g, c) for g in ("ka", "qa", "zb", "za") for c in range(4)]
    FILL2 = [("gb", e) for e in range(2, 8)]
    EARLY = 8 * KC
    LATE = EARLY // 3 + 1
    fill1 = [(m // 3 if m < EARLY else LATE + (m - EARLY) * (HALF + 22 - LATE) // EARLY, FILL1[m // KC], m % KC) for m in range(KC * len(FILL1))]
    fill2 = [(m, FILL2[m // KC], m % KC) for m in range(KC * len(FILL2))]
    filled = {tile: t for t, tile, k in fill1 if k == KC - 1}
    SUM = {filled[(g, 3)] + 2: g for g in ("ka", "qa")}
    ROOT = {filled[(g, 3)] + 3: g for g in ("ka", "qa")}
    INVERT = {filled[(g, 3)] + 4 + n: (g, n) for g in ("ka", "qa") for n in range(2)}
    SPREAD = {filled[(g, 3)] + 6 + c: [(g, c)] for g in ("ka", "qa") for c in range(4)}
    LOW1 = {1: unit_of[("qa", 0)] - 1, **{filled[tile] + 2: unit_of[tile] + HI_UNITS for tile in FILL1 if unit_of[tile] + HI_UNITS < U2}}
    WO_LOW = {HALF + 28 + m: m for m in range(4)}
    ROUNDS = TOPK // 8 * (NT - 1)
    EARLY_ROUNDS = 36
    MASKS = ROUNDS - EARLY_ROUNDS + 1
    GB_HIGH = {8 * n + 8: unit_of[("gb", 6 + n)] for n in range(2)}
    BRANCH_HIGH = {56: 0, 59: 1}

    A1 = [("qi", 0), ("qi", 1), ("ki", 0), ("wi", 0)]
    A1 += [("rel", i, h) for i in range(1, NT) for h in range(IDX_HEADS)]
    A1 += [(g, i) for g in ("kb", "qb", "vb", "va") for i in range(4)]
    A1_DENSE = len(A1)
    A1 += FILL1
    A2 = [(g, i) for g in ("kv2", "kwvg", "q2") for i in range(NT)]
    A2 += [("pool", g) for g in range(4)]
    A2 += [("hidk", 0), ("hidv", 0)]
    A2 += [("ga", e) for e in range(4)]
    A2 += [("kcmp", 0), ("vcmp", 0)]
    A2 += [("ga", e) for e in range(4, 8)]
    A2 += [("pm", g) for g in range(4)]
    A2 += [("gb", e) for e in range(2)]
    A2_DENSE = len(A2)
    A2 += FILL2
    A3 = [("ff", c) for c in range(DFF // P)]
    AT = {tile: n for n, tile in enumerate(A1 + A2 + A3)}
    A1_END, A2_END = len(A1), len(A1) + len(A2)

    T1 = [("h1", i, c) for i in range(NT) for c in range(2)]
    T1 += [("wi", 0), ("sum", "kb"), ("sum", "qb")] + [("spread", g, c) for g in ("kb", "qb") for c in range(4)]
    for t in range(NS + 2):
        if t >= 2:
            T1 += [("pt", t - 2)]
        if t in SUM:
            T1 += [("sum", SUM[t])]
        T1 += [("spread", *part) for part in SPREAD.get(t, [])]
    T2 = [("mx", i, c) for i in range(NT) for c in range(2)]
    T2 += [("h2", i, c) for i in range(NT) for c in range(2)]
    T2 += [("kv", n, g) for n in range(4) for g in range(G2)]
    T2 += [("q2", c) for c in range(4)]
    T2 += [("kcT", 0)] + [("ec", n) for n in range(2)]
    T3 = [("pt", NS + t) for t in range(NS)]
    T3 += [("at", i) for i in range(NT)] + [("h3", i, c) for i in range(NT) for c in range(2)]
    TT = {tile: n for n, tile in enumerate(T1 + T2 + T3)}

    with ExitStack() as ctx:
        def sb(name, shape):
            return ctx.enter_context(nc.sbuf_tensor(name, shape, F32))

        def sem(name):
            return ctx.enter_context(nc.semaphore(name))

        bank = [ctx.enter_context(nc.psum_tensor(f"bank{b}", [P, 512], F32)) for b in range(8)]

        x = sb("x", [P, NT, D])
        hT_at = nc.sbuf_base
        hT = sb("hT", [P, KC * 512])
        wring_at = nc.sbuf_base
        wring = sb("wring", [P, (RAW_UNITS + HI_UNITS) * UNIT + KC * S])
        consts = sb("consts", [P, C_END])
        small = sb("small", [P, V_END])
        junk = sb("junk", [P, D])
        stats = sb("stats", [P, 416])
        ARENA = 28900
        arena_at = nc.sbuf_base
        arena = sb("arena", [P, ARENA])
        used = [0]

        def region(n, at=None):
            if at is not None:
                return arena[:, at:at + n]
            used[0] += n
            return arena[:, used[0] - n:used[0]]

        qkT = {g: region(4 * S).rearrange("p (c s) -> p c s", c=4) for g in ("kb", "qb", "ka", "qa")}
        v1 = {g: region(NT * 512).rearrange("p (i n) -> p i n", i=NT) for g in ("vb", "va")}
        zT_at = used[0]
        zT = region(KC * S).rearrange("p (c s) -> p c s", c=KC)
        outs_at = used[0]
        outs = region(NT * D).rearrange("p (i n) -> p i n", i=NT)
        xn1 = outs
        strips_at = used[0]
        strips = region(2 * NH * S).rearrange("p (h u) -> p h u", h=2 * NH)
        squares_at = {"kb": outs_at, "qb": outs_at + 4 * S, "ka": outs_at, "qa": zT_at}
        squares_of = {g: region(4 * S, at).rearrange("p (c s) -> p c s", c=4) for g, at in squares_at.items()}
        inv = {g: region(S, zT_at + 4 * S + S * n)[0:NH, :] for n, g in enumerate(("kb", "qb", "ka"))}
        inv["qa"] = junk[0:NH, S:2 * S]
        spread_sb = junk[0:NH, 0:S]
        outs_of = {"a": region(NT * 512, outs_at).rearrange("p (i n) -> p i n", i=NT),
                   "b": region(NT * 512, outs_at + NT * 512).rearrange("p (i n) -> p i n", i=NT)}
        wo_place = {"wo0": arena[:, 0:SLOT], "wo1": region(SLOT, strips_at + NH * S)}
        xflat = x[:, :, :].rearrange("p i n -> p (i n)")
        scores = qkT["qa"].rearrange("p c s -> p (c s)")
        spans = {1: slice(0, 256), 2: slice(256, 640), 3: slice(640, 1152)}
        score_of = {i: scores[:, r] for i, r in spans.items()}
        mask_of = {i: xflat[:, r] for i, r in spans.items()}
        qiT = qkT["ka"][:, 0:2, :]
        kiT = qkT["ka"][:, 2, :]
        rels = [qkT["ka"][:, 3, :], junk[:, 512:1024]]
        vec = qkT["qb"][0:2 * NH, 1:3, :].rearrange("p a b -> p (a b)")[:, 0:VEC]
        bucket_sb = qkT["ka"][0:N_BUCKETS, 0:2, :].rearrange("p a b -> p (a b)")[:, 0:VEC]
        add_sb = qkT["ka"][0:2 * NH, 2:4, :].rearrange("p a b -> p (a b)")[:, 0:VEC]
        table_sb = qkT["qa"][0:N_BUCKETS, 3, 0:2 * NH]
        assert used[0] <= ARENA, used
        at0 = spans[3].stop
        logits1 = [xflat[:, at0 + 512 * n:at0 + 512 * (n + 1)] for n in range(3)]
        probsT1 = [xflat[:, at0 + 1536 + 512 * n:at0 + 2048 + 512 * n] for n in range(2)]
        combo = [junk[:, 512 * n:512 * n + 512] for n in range(2)]
        used[0] = 0
        q2 = region(NT * 512)
        dup = region(4 * NT * G2 * 2 * HD).rearrange("p (m i g r d) -> p m i g r d", m=4, i=NT, g=G2, r=2)
        xn2 = region(NT * D, 2 * SLOT).rearrange("p (i n) -> p i n", i=NT)
        v2 = {g: region(NT * G2 * HD).rearrange("p (i n) -> p i n", i=NT) for g in ("s", "w")}
        gates = region(NT * GATES).rearrange("p (i n) -> p i n", i=NT)
        q2T = region(4 * S).rearrange("p (c s) -> p c s", c=4)
        kT2 = {g: region(G2 * S).rearrange("p (g s) -> p g s", g=G2) for g in ("s", "w")}
        uT_at = used[0]
        uT = region(4 * S).rearrange("p (g s) -> p g s", g=4)
        ptmp_at = used[0]
        ptmp = [region(S) for _ in range(2)]
        ga_at = used[0]
        gaT = region(KC * S).rearrange("p (e s) -> p e s", e=KC)
        gbT = region(KC * S).rearrange("p (e s) -> p e s", e=KC)
        blk_at = used[0]
        blk = {m: region(G2 * NC * 16).rearrange("p (g c j) -> p g c j", g=G2, c=NC) for m in range(2)}
        hidk = region(2 * G2 * NCP).rearrange("p (m g c) -> p m g c", m=2, g=G2)
        hidv = region(2 * G2 * 4 * NCP).rearrange("p (m g r c) -> p m g r c", m=2, g=G2, r=4)
        kcn = region(G2 * 2 * HD).rearrange("p (g r d) -> p g r d", g=G2, r=2)
        kcT = region(G2 * NCP).rearrange("p (g c) -> p g c", g=G2)
        vdiag = region(G2 * 4 * HD).rearrange("p (g n) -> p g n", g=G2)
        pmT = uT
        attn = region(NT * 512).rearrange("p (i n) -> p i n", i=NT)
        ckv = {"ck": gbT.rearrange("p e s -> p (e s)").rearrange("p (k n) -> p k n", n=256),
               "cv": gaT.rearrange("p e s -> p (e s)").rearrange("p (k n) -> p k n", n=256)}
        ccw = region(2 * 2 * HD).rearrange("p (m k d) -> p m k d", m=2, k=2)
        poolw = region(4 * P).rearrange("p (g d) -> p g d", g=4)
        assert used[0] <= ARENA, used
        ec = dup[:, 0, :, :, :, :].rearrange("p i g r d -> p (i g r d)")
        ecT = dup[:, 1, :, :, :, :].rearrange("p i g r d -> p (i g r d)")
        ec_of = [ec.rearrange("p (m r c) -> p m r c", r=2, c=NCP)[:, :, n, :] for n in range(2)]
        spare = dup[:, 2:4, :, :, :, :].rearrange("p m i g r d -> p (m i g r d)")
        logits2 = [spare[:, 512 * n:512 * n + 512] for n in range(3)]
        probsT2 = [spare[:, 1536:2048], q2[:, 0:512]]
        ffT = region((DFF // P) * S, 0).rearrange("p (c s) -> p c s", c=DFF // P)
        xn3 = gbT.rearrange("p e s -> p (e s)").rearrange("p (i n) -> p i n", i=NT)
        gfin = region(D, ARENA - D)
        places = {"hT": hT_at, "wring": wring_at, "arena": arena_at}

        def half(name, n, at):
            return nc.alloc_sbuf_tensor_at(name, [P, n], F32R, offset=places[at[0]] + 4 * at[1])

        h_tmp = {"h1": region(D, zT_at), "mx": region(D, strips_at), "h2": region(D, strips_at + D), "h3": region(D, ptmp_at)}
        h_hi = half("h_hi", KC * S, ("hT", 0))
        h_lo = half("h_lo", KC * S, ("wring", (RAW_UNITS + HI_UNITS) * UNIT))
        h3_lo = half("h3_lo", KC * S, ("arena", 22624))
        a_hi = half("a_hi", 4 * S, ("hT", 0))
        a_lo = half("a_lo", 4 * S, ("hT", 4 * S))
        pm_hi = half("pm_hi", 4 * S, ("arena", blk_at))
        pm_lo = half("pm_lo", 4 * S, ("arena", uT_at))
        u_lo = [half(f"u_lo{n}", UNIT, ("wring", UNIT * n)) for n in range(RAW_UNITS)]
        u_hi = [half(f"u_hi{n}", UNIT, ("wring", UNIT * (RAW_UNITS + n))) for n in range(HI_UNITS)]
        branch_at = [2 * SLOT + UNIT * n for n in range(5)]
        br_lo = [half(f"br_lo{n}", UNIT, ("wring", branch_at[n])) for n in range(3)]
        br_hi = [half(f"br_hi{n}", UNIT, ("wring", branch_at[3 + n])) for n in range(2)]
        wo_hi = [half("wo_hi0", SLOT, ("wring", RAW_UNITS * UNIT)), half("wo_hi1", SLOT, ("arena", SLOT))]
        wo_lo = [half("wo_lo0", SLOT, ("arena", 0)), half("wo_lo1", SLOT, ("arena", strips_at + NH * S))]
        w2o_hi = [half(f"w2o_hi{n}", SLOT, ("arena", SLOT * n)) for n in range(2)]
        w2o_lo = [half(f"w2o_lo{n}", SLOT, ("wring", SLOT * n)) for n in range(2)]
        m_hi = [half(f"m_hi{k}", S, ("arena", 2 * SLOT + S * k if k < 6 else 26720 + S * (k - 6))) for k in range(KC)]
        m_lo = [half(f"m_lo{k}", S, ("arena", ga_at + S * k)) for k in range(KC)]
        unit_at = [16384, 18528, 18528 + 2 * D]
        unit_at.append(uT_at)
        w_hi = [half(f"w_hi{n}", D, ("arena", at)) for n, at in enumerate(unit_at)]
        w_lo = [half(f"w_lo{n}", D, ("arena", at + D)) for n, at in enumerate(unit_at)]
        ring3 = lambda m: m % 3 if m else 3
        ff_at = [("arena", 26720), ("hT", 0), ("hT", 2 * S)]
        ff_hi = [half(f"ff_hi{n}", S, at) for n, at in enumerate(ff_at)]
        ff_lo = [half(f"ff_lo{n}", S, (at[0], at[1] + S)) for n, at in enumerate(ff_at)]

        ident = consts[:, C_ID:C_ID + P]
        strip0 = consts[:, C_STRIP:C_STRIP + S]
        ss = stats[:, 0:12]
        rs = stats[:, 12:24]
        wi = stats[:, 88:104].rearrange("p (i h) -> p i h", i=NT)
        wiT = region(S, zT_at + 4 * S)[0:IDX_HEADS, :]
        top8 = stats[:, 104:112]
        den = stats[:, 112:112 + NS]
        negm = stats[:, 176:176 + NS]
        gr = stats[:, 240:248]
        cm = stats[:, 248:280]
        cden = stats[:, 280:312]
        ssf = stats[:, 312:316]
        rsf = stats[:, 316:320]
        den2 = stats[:, 320:320 + NS]
        rope_tmp = [junk[:, 256 * n:256 * n + 256] for n in range(4)]

        x_tile_in = [sem(f"x_tile_in{i}") for i in range(NT)]
        x_in = sem("x_in")
        consts_in = sem("consts_in")
        table_in = sem("table_in")
        small2_in = sem("small2_in")
        ckv_in = sem("ckv_in")
        gfin_in = sem("gfin_in")
        w_in = [sem(f"w_in{r}") for r in range(RING)]
        unit_used = sem("unit_used")
        vec_full = sem("vec_full")
        vec_done = sem("vec_done")
        vec_out = sem("vec_out")
        strips_in = sem("strips_in")
        ss_done = sem("ss_done")
        ms_done = sem("ms_done")
        sq_done = sem("sq_done")
        xn_done = sem("xn_done")
        a_full = sem("a_full")
        a_free = sem("a_free")
        t_full = sem("t_full")
        t_free = sem("t_free")
        r_full = sem("r_full")
        r_free = sem("r_free")
        rel_free = sem("rel_free")
        inv_root = sem("inv_root")
        inv_done = sem("inv_done")
        spread_in = sem("spread_in")
        masks_done = sem("masks_done")
        combo_done = sem("combo_done")
        s_full = sem("s_full")
        l_done = sem("l_done")
        e_done = sem("e_done")
        pv_done = sem("pv_done")
        o_free = sem("o_free")
        zeroed = sem("zeroed")
        rope_done = sem("rope_done")
        kcn_done = sem("kcn_done")
        pooled = sem("pooled")
        pool_chain = sem("pool_chain")
        cs_full = sem("cs_full")
        cl_done = sem("cl_done")
        ce_done = sem("ce_done")
        cp_done = sem("cp_done")
        co_full = sem("co_full")
        co_free = sem("co_free")
        mix_done = sem("mix_done")
        unit_in = [sem(f"unit_in{n}") for n in range(RAW_UNITS)]
        branch_in = [sem(f"branch_in{n}") for n in range(3)]
        nat_used = sem("nat_used")
        u_hi_done = sem("u_hi_done")
        u_lo_done = sem("u_lo_done")
        br_hi_done = sem("br_hi_done")
        br_lo_done = sem("br_lo_done")
        wo_hi_done = sem("wo_hi_done")
        wo_lo_done = sem("wo_lo_done")
        w2o_hi_done = sem("w2o_hi_done")
        w2o_lo_done = sem("w2o_lo_done")
        m_hi_done = sem("m_hi_done")
        m_lo_done = sem("m_lo_done")
        pm_done = sem("pm_done")
        pm_lo_done = sem("pm_lo_done")
        at_hi_done = sem("at_hi_done")
        h_lo_done = sem("h_lo_done")
        h_hi_done = sem("h_hi_done")
        w_hi_done = sem("w_hi_done")
        w_lo_done = sem("w_lo_done")
        ff_hi_done = sem("ff_hi_done")
        ff_lo_done = sem("ff_lo_done")
        relu_done = sem("relu_done")
        dve_step = sem("dve_step")
        y_done = sem("y_done")
        out_done = sem("out_done")

        def slot(name, width=512):
            s = number[name] % RING
            place = wo_place.get(name, wring[:, s * SLOT:(s + 1) * SLOT])
            return place.rearrange("p (k n) -> p k n", n=width)

        R_BRANCH, R_OUT2, R_FF = 2 * NT, 2 * NT + 2 * KC, 4 * NT + 2 * KC

        def last_use(name):
            if name[0] == "f":
                return w_lo_done, 4 * (int(name[3:]) + 1) + (DFF // P if name[1] == "2" else 0)
            if name == "block2":
                return r_full, R_OUT2
            if name[:2] == "wo" or name[:3] == "w2o":
                return r_full, (R_BRANCH if name[:2] == "wo" else R_FF) - (1 if name[-1] == "0" else 0)

        def halves(name, i, c):
            return 2 * NT * ("h1", "mx", "h2", "h3").index(name) + 2 * i + c

        def unit_free(u):
            name, k, _, _ = units[u]
            if name in NATS and k < 3:
                return nat_used, 3 * NATS.index(name) + k + 1
            return a_full, AT[(name, k)] + 1

        def raw_unit(u):
            return wring[:, UNIT * (u % RAW_UNITS):UNIT * (u % RAW_UNITS) + unit_cols(u)]

        def unit_cols(u):
            width = units[u][2]
            return 2 * width if units[u][0] in NATS else KC * width

        block = ctx.enter_context(nc.Block())

        @block.sync
        def _(sp):
            def load_unit(u):
                if u >= RAW_UNITS:
                    sp.wait_ge(*unit_free(u - RAW_UNITS))
                _, _, width, parts = units[u]
                for at, cols, view in parts:
                    sp.dma_start(raw_unit(u).rearrange("p (k n) -> p k n", n=width)[:, :, at:at + cols], view)\
                        .then_inc(unit_in[u % RAW_UNITS], 16)

            def load_branch(e):
                sp.wait_ge(a_full, A2_END)
                if e >= 3:
                    sp.wait_ge(r_full, R_BRANCH + 2 * (e - 2))
                for at, cols, width, view in branch[e]:
                    dst = wring[:, branch_at[e % 3] + at:branch_at[e % 3] + at + cols]
                    sp.dma_start(dst.rearrange("p (k n) -> p k n", n=width), view).then_inc(branch_in[e % 3], 16)

            for i in range(NT):
                sp.dma_start(x[:, i, :], w["x"][0, i * P:(i + 1) * P, :]).then_inc(x_tile_in[i], 16)
                if i == 0:
                    sp.dma_start(consts[:, :], w["consts"]).then_inc(consts_in, 16)
                    sp.dma_start(small[:, :], w["small"]).then_inc(consts_in, 16)
            sp.dma_start(bucket_sb, w["onehot"]).then_inc(table_in, 16)
            sp.dma_start(add_sb, w["vec_add"]).then_inc(table_in, 16)
            sp.dma_start(table_sb, w["rel_bias"]).then_inc(table_in, 16)
            for u in range(U2):
                load_unit(u)
                if u == RAW_UNITS - 1:
                    sp.wait_ge(ss_done, NT)
                    sp.dma_start(spread_sb, w["spread"]).then_inc(spread_in, 16)
            for n, (name, parts) in enumerate(groups):
                if name == "wo0":
                    sp.wait_ge(pv_done, HALF)
                if n >= RING:
                    done, value = last_use(groups[n - RING][0])
                    sp.wait_ge(done, value)
                if name in ("w2o0", "w2o1"):
                    sp.wait_ge(a_full, A2_END)
                for at, cols, width, view in parts:
                    sp.dma_start(slot(name, width)[:, :, at:at + cols], view).then_inc(w_in[n % RING], 16)
                if name == "wo1":
                    for u in range(U2, U2 + RAW_UNITS):
                        load_unit(u)
                    sp.wait_ge(pv_done, NS)
                    for i in range(NT):
                        sp.dma_start(x[:, i, :], w["x"][0, i * P:(i + 1) * P, :]).then_inc(x_in, 16)
                if name == "block2":
                    for u in range(U2 + RAW_UNITS, len(units)):
                        load_unit(u)
                        if u == U2 + 5:
                            sp.wait_ge(zeroed, 1)
                            for m, a in enumerate(("cmp_k_w2_2", "cmp_v_w2_2")):
                                sp.dma_start(ccw[:, m, :, :], w[a].rearrange("(k p) d -> p k d", p=P)).then_inc(small2_in, 16)
                            sp.dma_start(poolw, w["pool_w_2"].rearrange("g c d -> c g d")).then_inc(small2_in, 16)
                        if u in (U2 + 7, U2 + 10):
                            src = w["cmp_k_w1_2" if u == U2 + 7 else "cmp_v_w1_2"]
                            for half in range(2):
                                rows = src[half * D:(half + 1) * D, :].rearrange("(j d) n -> d j n", d=HD)
                                sp.dma_start(ckv["ck" if u == U2 + 7 else "cv"][half * HD:(half + 1) * HD, :, :], rows).then_inc(ckv_in, 16)
                    for e in range(3):
                        load_branch(e)
                if name == "w2o1":
                    for e in range(3, KC):
                        load_branch(e)
                if name == "f1_3":
                    sp.wait_ge(xn_done, 3 * NT)
                    sp.dma_start(gfin, w["norm_final_2"].to_broadcast([P, D])).then_inc(gfin_in, 16)
            for i in range(NT):
                sp.wait_ge(y_done, i + 1)
                sp.dma_start(out[0, i * P:(i + 1) * P, :], x[:, i, :]).then_inc(out_done, 16)
            sp.wait_ge(out_done, 16 * NT)

        def unit_arrived(eng, u):
            eng.wait_ge(unit_in[u % RAW_UNITS], 16 * sum(len(units[m][3]) for m in range(u % RAW_UNITS, u + 1, RAW_UNITS)))

        def arrived(eng, name):
            n = number[name]
            total = sum(len(g[1]) for g in groups[n % RING:n + 1:RING])
            eng.wait_ge(w_in[n % RING], 16 * total)

        @block.tensor
        def _(pe):
            mm = nc.tensor.matmul

            def a_bank(tile):
                n = AT[tile]
                if n >= 2:
                    pe.wait_ge(a_free, n - 1)
                return bank[n % 2]

            def t_bank(tile):
                n = TT[tile]
                if n >= 2:
                    pe.wait_ge(t_free, n - 1)
                return bank[4 + n % 2]

            def three(b, weights, cols, act, rows, weights_first, start, stop):
                (w_high, w_low), (a_high, a_low) = weights, act
                for n, (wt, a) in enumerate(((w_high, a_high), (w_high, a_low), (w_low, a_high))):
                    lhs, rhs = wt[:, cols], a[:, rows]
                    if not weights_first:
                        lhs, rhs = rhs, lhs
                    last = mm(b, lhs, rhs, start=(start and n == 0), stop=(stop and n == 2))
                return last

            def unit(u):
                return u_hi[u % HI_UNITS], u_lo[u % RAW_UNITS]

            def nat_unit(name, k, width=512, tiles=range(NT)):
                u = unit_of[(name, k)]
                pe.wait_ge(u_lo_done, u + 1)
                for i in tiles:
                    if k == 0:
                        if name == "vb":
                            pe.wait_ge(a_free, AT[("qb", 3 if i < 2 else 0)] + 1)
                        elif name == "kv2":
                            pe.wait_ge(h_lo_done, halves("h2", i, 1) + 1)
                            pe.wait_ge(r_free, R_BRANCH)
                        else:
                            pe.wait_ge(a_free, AT[(NATS[NATS.index(name) - 1], i)] + 1)
                    for c in range(2):
                        last = three(bank[i][:, 0:width], unit(u), slice(c * width, (c + 1) * width), (h_hi, h_lo),
                                     slice((2 * k + c) * S + i * P, (2 * k + c) * S + (i + 1) * P), False,
                                     2 * k + c == 0, 2 * k + c == KC - 1)
                    if k == 3:
                        last.then_inc(a_full, 1)
                if k < 3 and NT - 1 in tiles:
                    last.then_inc(nat_used, 1)

            def t_unit(name, e, chunks=range(KC), width=P):
                u = unit_of[(name, e)]
                if chunks[0] == 0:
                    pe.wait_ge(u_lo_done, u + 1)
                    a_bank((name, e))
                for k in chunks:
                    last = three(bank[AT[(name, e)] % 2][0:width, :], unit(u), slice(k * width, (k + 1) * width), (h_hi, h_lo),
                                 slice(k * S, (k + 1) * S), True, k == 0, k == KC - 1)
                if chunks[-1] == KC - 1:
                    last.then_inc(a_full, 1)

            def h_transposes(name, xn, base, tiles=range(NT)):
                for i in tiles:
                    pe.wait_ge(xn_done, base + i + 1)
                    for c in range(2):
                        b = t_bank((name, i, c))
                        for k in range(4):
                            last = nc.tensor.transpose(b[:, k * P:(k + 1) * P],
                                                       xn[:, i, (4 * c + k) * P:(4 * c + k + 1) * P], ident)
                        last.then_inc(t_full, 1)

            def head_sums(g):
                pe.wait_ge(a_free, AT[(g, 3)] + 1)
                b = t_bank(("sum", g))
                for c in range(4):
                    last = mm(b[0:NH, :], consts[:, C_HEADS + NH - 2 - 2 * c:C_HEADS + 2 * NH - 2 - 2 * c], squares_of[g][:, c, :],
                              start=(c == 0), stop=(c == 3))
                last.then_inc(t_full, 1)

            def spread_norms(g, c):
                pe.wait_ge(inv_done, 2 * ORDER.index(g) + 2)
                mm(t_bank(("spread", g, c))[:, :], spread_sb[:, c * P:(c + 1) * P], inv[g], start=True, stop=True).then_inc(t_full, 1)

            def fill(work, t):
                for _, (name, e), k in [f for f in work if f[0] == t]:
                    t_unit(name, e, [k])

            def attention(t, steps, base, query, key, value, logits, probsT):
                if t < NS:
                    i, br, h = steps[t]
                    if t >= 2:
                        pe.wait_ge(l_done, base + t - 1)
                    mm(bank[2 + t % 2][:, 0:(i + 1) * P], query(br, h)[:, i * P:(i + 1) * P],
                       key(br, h)[:, 0:(i + 1) * P], start=True, stop=True).then_inc(s_full, 1)
                u = t - 2
                if 0 <= u < NS:
                    pe.wait_ge(e_done, base + u + 1)
                    b = t_bank(("pt", base + u))
                    for j in range(steps[u][0] + 1):
                        last = nc.tensor.transpose(b[:, j * P:(j + 1) * P], logits[u % 3][:, j * P:(j + 1) * P], ident)
                    last.then_inc(t_full, 1)
                u = t - 3
                if u >= 0:
                    i, br, h = steps[u]
                    o = u // NH
                    pe.wait_ge(t_free, TT[("pt", base + u)] + 1)
                    if u % NH == 0 and o >= 2:
                        pe.wait_ge(o_free, base // NH + o - 1)
                    for j in range(i + 1):
                        last = mm(bank[6 + o % 2][:, h * HD:(h + 1) * HD], probsT[u % 2][:, j * P:(j + 1) * P],
                                  value(br, h)[:, j, :], start=(j == 0), stop=(j == i))
                    last.then_inc(pv_done, 1)

            pe.wait_ge(consts_in, 32)
            h_transposes("h1", xn1, 0)

            pe.wait_ge(table_in, 48)
            mm(bank[6][0:2 * NH, 0:512], table_sb, bucket_sb[:, 0:512], start=True, stop=True)
            mm(bank[7][0:2 * NH, 0:P], table_sb, bucket_sb[:, 512:VEC], start=True, stop=True).then_inc(vec_full, 1)

            pe.wait_ge(h_lo_done, 2 * NT)
            for c in range(2):
                t_unit("qi", c)
            t_unit("ki", 0)
            t_unit("wi", 0, width=IDX_HEADS)
            pe.wait_ge(a_free, AT[("wi", 0)] + 1)
            b = t_bank(("wi", 0))
            for i in range(NT):
                last = nc.tensor.transpose(b[:, i * IDX_HEADS:(i + 1) * IDX_HEADS], wiT[:, i * P:(i + 1) * P], ident[0:IDX_HEADS, 0:IDX_HEADS])
            last.then_inc(t_full, 1)
            pe.wait_ge(a_free, 3)
            for i in range(1, NT):
                for h in range(IDX_HEADS):
                    r = slice((h % 2) * HD, (h % 2) * HD + HD)
                    mm(a_bank(("rel", i, h))[:, 0:(i + 1) * P], qiT[r, h // 2, i * P:(i + 1) * P],
                       kiT[r, 0:(i + 1) * P], start=True, stop=True).then_inc(a_full, 1)
            pe.wait_ge(spread_in, 16)
            for c in range(4):
                t_unit("kb", c)
            for c in range(4):
                t_unit("qb", c)
                if c == 0:
                    head_sums("kb")
            for k in range(4):
                nat_unit("vb", k, tiles=[2, 3, 0, 1] if k == 0 else range(NT))
                if k == 0:
                    head_sums("qb")
                if k in (1, 2):
                    for c in (2 * k - 2, 2 * k - 1):
                        spread_norms("kb", c)
            for k in range(4):
                nat_unit("va", k)
                if k in (1, 2):
                    for c in (2 * k - 2, 2 * k - 1):
                        spread_norms("qb", c)
            pe.wait_ge(t_free, TT[("spread", "qb", 3)] + 1)
            pe.wait_ge(a_free, AT[("va", NT - 1)] + 1)
            rows = lambda h: slice((h % 2) * HD, (h % 2) * HD + HD)
            for t in range(NS + 3):
                if t == HALF:
                    pe.wait_ge(t_free, TT[("spread", "qa", 3)] + 1)
                attention(t, steps1, 0, lambda br, h: qkT["q" + br][rows(h), h // 2, :],
                          lambda br, h: qkT["k" + br][rows(h), h // 2, :], lambda br, h: v1["v" + br][:, :, h * HD:(h + 1) * HD],
                          logits1, probsT1)
                if t in SUM:
                    head_sums(SUM[t])
                for part in SPREAD.get(t, []):
                    spread_norms(*part)
                fill(fill1, t)

            pe.wait_ge(a_free, A1_END)
            pe.wait_ge(o_free, NS // NH)

            def mixed_transposes(i):
                for c in range(2):
                    b = t_bank(("mx", i, c))
                    for k in range(4):
                        last = nc.tensor.transpose(b[:, k * P:(k + 1) * P], outs_of["ab"[c]][:, i, k * P:(k + 1) * P], ident)
                    last.then_inc(t_full, 1)

            def residual(r0, ready, product, then):
                for i in range(NT):
                    if i >= 2:
                        then(i - 2)
                    for n in range(2):
                        ready(i, n)
                        r = r0 + 2 * i + n
                        if r >= 4:
                            pe.wait_ge(r_free, r - 3)
                        for k in range(KC):
                            last = product(bank[r % 4][:, :], i, n, k)
                        last.then_inc(r_full, 1)

            h2 = lambda i: h_transposes("h2", xn2, NT, [i])

            def ready1(i, n):
                pe.wait_ge(h_lo_done, halves("mx", i, 1) + 1)
                if i == 0:
                    pe.wait_ge(wo_lo_done, 4 * (n + 1))
                if n == 1 and i + 2 < NT:
                    mixed_transposes(i + 2)

            mixed_transposes(0)
            mixed_transposes(1)
            residual(0, ready1, lambda b, i, n, k: three(b, (wo_hi[n], wo_lo[n]), slice(k * 512, (k + 1) * 512), (h_hi, h_lo),
                                                         slice(k * S + i * P, k * S + (i + 1) * P), False, k == 0, k == KC - 1), h2)

            h2(2)
            for k in range(2):
                nat_unit("kv2", k, tiles=[0, 1])
            h2(3)
            for k in range(2):
                nat_unit("kv2", k, tiles=[2, 3])
            for k in range(2, 4):
                nat_unit("kv2", k)
            for k in range(4):
                nat_unit("kwvg", k, 280)
            for k in range(4):
                nat_unit("q2", k)

            pe.wait_ge(a_free, AT[("kwvg", NT - 1)] + 1)
            for n in range(4):
                if n == 2:
                    pe.wait_ge(rope_done, 1)
                for g in range(G2):
                    b = t_bank(("kv", n, g))
                    for i in range(NT):
                        last = nc.tensor.transpose(b[:, i * P:(i + 1) * P],
                                                   dup[:, n, i, g, :, :].rearrange("p r d -> p (r d)"), ident)
                    last.then_inc(t_full, 1)

            for g in range(4):
                t_unit("pool", g)
            pe.wait_ge(t_free, TT[("kv", 1, G2 - 1)] + 1)
            for m, name in enumerate(("ck", "cv")):
                pe.wait_ge(ckv_in, 32 * (m + 1))
                b = a_bank((("hidk", "hidv")[m], 0))
                for c in range(2):
                    for j in range(16):
                        last = mm(b[:, 64 * c:64 * c + G2 * NC], ckv[name][:, j, c * P:(c + 1) * P],
                                  blk[m][:, :, :, j].rearrange("p g c -> p (g c)"), start=(j == 0), stop=(j == 15))
                last.then_inc(a_full, 1)
            pe.wait_ge(rope_done, 2)
            for c in range(4):
                b = t_bank(("q2", c))
                for i in range(NT):
                    last = nc.tensor.transpose(b[:, i * P:(i + 1) * P], q2[:, i * 512 + c * P:i * 512 + (c + 1) * P], ident)
                last.then_inc(t_full, 1)
            for e in range(4):
                t_unit("ga", e)
            pe.wait_ge(small2_in, 48)
            pe.wait_ge(a_free, AT[("hidv", 0)] + 1)
            b = a_bank(("kcmp", 0))
            for g in range(G2):
                for m in range(2):
                    last = mm(b[0:NC, g * HD:(g + 1) * HD], hidk[:, m, g, 0:NC], ccw[:, 0, m, :], start=(m == 0), stop=(m == 1))
            last.then_inc(a_full, 1)
            b = a_bank(("vcmp", 0))
            for g in range(G2):
                for m in range(2):
                    last = mm(b[:, g * HD:(g + 1) * HD], hidv[:, m, g, :, :].rearrange("p r c -> p (r c)"), ccw[:, 1, m, :],
                              start=(m == 0), stop=(m == 1))
            last.then_inc(a_full, 1)
            for e in range(4, 8):
                t_unit("ga", e)
            pe.wait_ge(kcn_done, 1)
            b = t_bank(("kcT", 0))
            for g in range(G2):
                last = nc.tensor.transpose(b[:, g * NCP:g * NCP + NC], kcn[0:NC, g, :, :].rearrange("p r d -> p (r d)"),
                                           ident[0:NC, 0:NC])
            last.then_inc(t_full, 1)
            pe.wait_ge(t_free, TT[("kcT", 0)] + 1)
            for n in range(2):
                for i in range(NT):
                    for m in range(NH // 2):
                        at = (i * NH // 2 + m) * NCP
                        last = mm(bank[6 + n][:, at:at + NCP], q2T[rows(n), m, i * P:(i + 1) * P],
                                  kcT[rows(n), m // 2, :], start=True, stop=True)
                last.then_inc(cs_full, 1)
            for g in range(4):
                pe.wait_ge(pooled, g + 1)
                mm(a_bank(("pm", g))[:, :], poolw[:, g, :], uT[:, g, :], start=True, stop=True).then_inc(a_full, 1)
            for e in range(2):
                t_unit("gb", e)
            for n in range(2):
                pe.wait_ge(cp_done, 2)
                b = t_bank(("ec", n))
                for k in range(4):
                    last = nc.tensor.transpose(b[:, k * P:(k + 1) * P], ec[:, (4 * n + k) * P:(4 * n + k + 1) * P], ident)
                last.then_inc(t_full, 1)
            pe.wait_ge(a_free, AT[("vcmp", 0)] + 1)
            for i in range(NT):
                pe.wait_ge(t_free, TT[("ec", i // 2)] + 1)
                if i >= 2:
                    pe.wait_ge(co_free, i - 1)
                for g in range(G2):
                    last = mm(bank[6 + i % 2][:, g * 256:(g + 1) * 256], ecT[:, (2 * i + g) * P:(2 * i + g + 1) * P],
                              vdiag[:, g, :], start=True, stop=True)
                last.then_inc(co_full, 1)

            pe.wait_ge(co_free, NT)
            for t in range(NS + 3):
                attention(t, steps2, NS, lambda br, h: q2T[rows(h), h // 2, :], lambda br, h: kT2[br][rows(h), h // GROUP, :],
                          lambda br, h: v2[br][:, :, (h // GROUP) * HD:(h // GROUP + 1) * HD], logits2, probsT2)
                fill(fill2, t)
            pe.wait_ge(a_free, A2_END)
            pe.wait_ge(o_free, 2 * NS // NH)
            for i in range(NT):
                b = t_bank(("at", i))
                for k in range(4):
                    last = nc.tensor.transpose(b[:, k * P:(k + 1) * P], attn[:, i, k * P:(k + 1) * P], ident)
                last.then_inc(t_full, 1)
            pe.wait_ge(t_free, TT[("at", NT - 1)] + 1)
            pe.wait_ge(pm_lo_done, 4)
            R = 2 * NT
            for e in range(KC):
                pe.wait_ge(br_lo_done, e + 1)
                for n, act in enumerate(((a_hi, a_lo), (pm_hi, pm_lo))):
                    r = R + 2 * e + n
                    if 2 * e + n >= 4:
                        pe.wait_ge(r_free, r - 3)
                    for k in range(4):
                        last = three(bank[r % 4][:, :], (br_hi[e % 2], br_lo[e % 3]), slice((4 * n + k) * P, (4 * n + k + 1) * P),
                                     act, slice(k * S, (k + 1) * S), True, k == 0, k == 3)
                    last.then_inc(r_full, 1)
            R += 2 * KC

            def ready2(i, n):
                if i == 0:
                    pe.wait_ge(w2o_lo_done, 4 * (n + 1))

            def product2(b, i, n, k):
                if i == 0 and n == 0:
                    pe.wait_ge(m_lo_done, k + 1)
                return three(b, (w2o_hi[n], w2o_lo[n]), slice(k * 512, (k + 1) * 512), (m_hi[k], m_lo[k]),
                             slice(i * P, (i + 1) * P), False, k == 0, k == KC - 1)

            h3 = lambda i: h_transposes("h3", xn3, 2 * NT, [i])
            residual(R, ready2, product2, h3)
            R += 2 * NT
            for i in range(2, NT):
                h3(i)
            pe.wait_ge(h_lo_done, 8 * NT)
            pe.wait_ge(r_free, R)

            NF = DFF // P
            for c in range(NF):
                b = a_bank(("ff", c))
                pe.wait_ge(w_lo_done, c + 1)
                for k in range(KC):
                    last = three(b[:, :], (w_hi[ring3(c)], w_lo[ring3(c)]), slice(k * P, (k + 1) * P), (h_hi, h3_lo), slice(k * S, (k + 1) * S),
                                 True, k == 0, k == KC - 1)
                last.then_inc(a_full, 1)
            for k in range(NF):
                pe.wait_ge(w_lo_done, NF + k + 1)
                pe.wait_ge(ff_lo_done, k + 1)
                for i in (1, 2, 3, 0) if k == 0 else range(NT):
                    if k == 0 and i == 0:
                        pe.wait_ge(a_free, A2_END + NF)
                    for n in range(2):
                        last = three(bank[2 * i + n][:, :], (w_hi[ring3(NF + k)], w_lo[ring3(NF + k)]), slice(512 * n, 512 * (n + 1)),
                                     (ff_hi[k % 3], ff_lo[k % 3]), slice(i * P, (i + 1) * P), False, k == 0, k == NF - 1)
                        if k == NF - 1:
                            last.then_inc(r_full, 1)
                if k < NF - 1:
                    last.then_inc(unit_used, 1)

        @block.scalar
        def _(act):
            run = nc.scalar.activation

            def root(base, i):
                act.wait_ge(ms_done, base + i + 1)
                run(rs[:, base + i:base + i + 1], ss[:, base + i:base + i + 1], ACT.Sqrt).then_inc(sq_done, 1)

            def take(tile):
                n = AT[tile]
                kind, i = tile[0], tile[1]
                b = bank[i if kind in NATS else n % 2]
                act.wait_ge(a_full, n + 1)
                if kind == "qi":
                    act.wait_ge(vec_done, 1)
                    last = run(qiT[:, i, :], b[:, :], ACT.Copy)
                elif kind == "ki":
                    last = run(kiT, b[:, :], ACT.Copy)
                elif kind == "wi":
                    last = run(wiT, b[0:IDX_HEADS, :], ACT.Copy)
                elif kind in ("za", "zb"):
                    last = run(zT[:, (0 if kind == "za" else 4) + i, :], b[:, :], ACT.Silu)
                elif kind == "rel":
                    r = 4 * (i - 1) + tile[2]
                    if r >= 2:
                        act.wait_ge(rel_free, r - 1)
                    last = run(rels[r % 2][:, 0:(i + 1) * P], b[:, 0:(i + 1) * P], ACT.Relu, scale=IDX_SCALE)
                elif kind in ("va", "vb"):
                    last = run(v1[kind][:, i, :], b[:, :], ACT.Copy)
                elif kind in ("kb", "qb", "ka", "qa"):
                    if i == 0:
                        if kind == "kb":
                            act.wait_ge(rel_free, 4 * (NT - 1))
                        if kind == "qb":
                            act.wait_ge(vec_out, 16)
                        if kind == "qa":
                            act.wait_ge(masks_done, NT - 1)
                    run(qkT[kind][:, i, :], b[:, :], ACT.Copy)
                    last = run(squares_of[kind][:, i, :], b[:, :], ACT.Square)
                elif kind == "kv2":
                    twice = lambda n_, g: b[:, n_:n_ + g * HD].rearrange("p (g d) -> p g d", g=g).unsqueeze(2).to_broadcast([P, g, 2, HD])
                    for m in range(3):
                        run(dup[:, m, i, :, :, :], twice(m * P, G2), ACT.Copy)
                    last = run(v2["s"][:, i, :], b[:, 384:512], ACT.Copy)
                elif kind == "kwvg":
                    run(dup[:, 3, i, :, :, :], b[:, 0:P].rearrange("p (g d) -> p g d", g=G2).unsqueeze(2).to_broadcast([P, G2, 2, HD]), ACT.Copy)
                    run(v2["w"][:, i, :], b[:, P:2 * P], ACT.Copy)
                    last = run(gates[:, i, :], b[:, 256:280], ACT.Sigmoid)
                elif kind == "q2":
                    last = run(q2[:, i * 512:(i + 1) * 512], b[:, :], ACT.Copy)
                elif kind == "pool":
                    last = run(uT[:, i, :], b[:, :], ACT.Copy)
                elif kind == "hidk":
                    for c in range(2):
                        last = run(hidk[:, c, :, 0:NC], b[:, 64 * c:64 * c + G2 * NC].rearrange("p (g c) -> p g c", g=G2), ACT.Gelu_apprx_tanh)
                elif kind == "hidv":
                    for c in range(2):
                        for g in range(G2):
                            src = b[:, 64 * c + g * NC:64 * c + (g + 1) * NC].unsqueeze(1).to_broadcast([P, 4, NC])
                            last = run(hidv[:, c, g, :, 0:NC], src, ACT.Gelu_apprx_tanh)
                elif kind == "kcmp":
                    src = b[0:NC, 0:G2 * HD].rearrange("p (g d) -> p g d", g=G2).unsqueeze(2).to_broadcast([NC, G2, 2, HD])
                    last = run(kcn[0:NC, :, :, :], src, ACT.Copy)
                elif kind == "vcmp":
                    for r in range(4):
                        rows = slice(NCP * r, NCP * r + NCP)
                        last = run(vdiag[rows, :, r * HD:(r + 1) * HD], b[rows, 0:G2 * HD].rearrange("p (g d) -> p g d", g=G2), ACT.Copy)
                elif kind in ("ga", "gb"):
                    last = run((gaT if kind == "ga" else gbT)[:, i, :], b[:, :], ACT.Sigmoid)
                elif kind == "pm":
                    run(pmT[:, i, :], b[:, :], ACT.Copy, scale=small[:, V_PS + i:V_PS + i + 1]).then_inc(pm_done, 1)
                    act.wait_ge(pm_done, i + 1)
                    last = run(pm_hi[:, i * S:(i + 1) * S], pmT[:, i, :], ACT.Copy)
                elif kind == "ff":
                    run(ffT[:, i, :], b[:, :], ACT.Relu).then_inc(relu_done, 1)
                    act.wait_ge(relu_done, i + 1)
                    last = run(ffT[:, i, :], ffT[:, i, :], ACT.Square)
                last.then_inc(a_free, 1)

            def exps(t, steps, base, dens, logits):
                act.wait_ge(l_done, base + t + 1)
                n = (steps[t][0] + 1) * P
                run(logits[t % 3][:, 0:n], logits[t % 3][:, 0:n], ACT.Exp, scale=-1.0, bias=negm[:, t:t + 1],
                    accum_out=dens[:, t:t + 1]).then_inc(e_done, 1)

            def head_root(g):
                act.wait_ge(t_free, TT[("sum", g)] + 1)
                run(inv[g], inv[g], ACT.Sqrt).then_inc(inv_root, 1)

            def takes(work, t):
                for _, tile, k in [f for f in work if f[0] == t]:
                    if k == KC - 1:
                        take(tile)

            def high(u):
                unit_arrived(act, u)
                if U2 <= u < U2 + HI_UNITS:
                    act.wait_ge(r_full, R_BRANCH)
                elif u >= HI_UNITS:
                    act.wait_ge(*unit_free(u - HI_UNITS))
                run(u_hi[u % HI_UNITS][:, 0:unit_cols(u)], raw_unit(u), ACT.Copy).then_inc(u_hi_done, 1)

            def branch_high(e):
                act.wait_ge(branch_in[e % 3], 32 * (e // 3 + 1))
                if e >= 2:
                    act.wait_ge(r_full, R_BRANCH + 2 * (e - 1))
                run(br_hi[e % 2][:, :], wring[:, branch_at[e % 3]:branch_at[e % 3] + UNIT], ACT.Copy).then_inc(br_hi_done, 1)

            def input_high(name, i):
                for c in range(2):
                    act.wait_ge(t_free, TT[(name, i, c)] + 1)
                    run(h_hi[:, :].rearrange("p (k s) -> p k s", k=KC)[:, 4 * c:4 * c + 4, i * P:(i + 1) * P],
                        h_tmp[name][:, 512 * c:512 * c + 512].rearrange("p (k s) -> p k s", k=4), ACT.Copy).then_inc(h_hi_done, 1)

            def squares(base, r0, i):
                act.wait_ge(ss_done, base + i)
                act.wait_ge(r_free, r0 + 2 * (i + 1))
                run(junk[:, :], x[:, i, :], ACT.Square, accum_out=ss[:, base + i:base + i + 1]).then_inc(ss_done, 1)
                root(base, i)

            for i in range(NT):
                act.wait_ge(x_tile_in[i], 16)
                if i > 0:
                    act.wait_ge(ss_done, i)
                run(junk[:, :], x[:, i, :], ACT.Square, accum_out=ss[:, i:i + 1]).then_inc(ss_done, 1)
                root(0, i)
                if i >= 1:
                    input_high("h1", i - 1)
            high(0)
            input_high("h1", NT - 1)
            for u in range(1, HI_UNITS):
                high(u)

            def dense(tile):
                kind, i = tile[0], tile[1]
                if kind in NATS and i == 0:
                    for k in range(3):
                        high(unit_of[(kind, k)] + HI_UNITS)
                        if kind == "vb" and k == 1:
                            head_root("qb")
                take(tile)
                if tile in unit_of and (kind not in NATS or i == 3):
                    high(unit_of[tile] + HI_UNITS)

            for tile in A1[:A1_DENSE]:
                dense(tile)
                if tile == ("qb", 2):
                    head_root("kb")
            def wo_high(m):
                n, c = m // 4, slice(UNIT * (m % 4), UNIT * (m % 4 + 1))
                arrived(act, f"wo{n}")
                run(wo_hi[n][:, c], wo_place[f"wo{n}"][:, c], ACT.Copy).then_inc(wo_hi_done, 1)

            for t in range(NS):
                exps(t, steps1, 0, den, logits1)
                if t + 1 in WO_LOW:
                    wo_high(WO_LOW[t + 1])
                if t in ROOT:
                    head_root(ROOT[t])
                takes(fill1, t)
                if t + 2 in LOW1:
                    high(LOW1[t + 2])
            for i in range(2):
                input_high("mx", i)
                for m in range(4 + 2 * i, 6 + 2 * i):
                    wo_high(m)
            for i in range(NT):
                if i < 2:
                    input_high("mx", i + 2)
                if i == 3:
                    high(U2)
                squares(NT, 0, i)
                if i >= 1:
                    input_high("h2", i - 1)
            high(U2 + 1)
            input_high("h2", NT - 1)
            high(U2 + 2)
            high(U2 + 3)
            for tile in A2[:A2_DENSE]:
                kind, i = tile
                if kind == "hidk":
                    act.wait_ge(zeroed, 1)
                if kind == "pm" and i == 0:
                    for n in range(2):
                        act.wait_ge(cl_done, n + 1)
                        run(ec_of[n], ec_of[n], ACT.Exp).then_inc(ce_done, 1)
                dense(tile)
            for t in range(NS):
                exps(t, steps2, NS, den2, logits2)
                takes(fill2, t)
                if t in GB_HIGH:
                    high(GB_HIGH[t])
                if t in BRANCH_HIGH:
                    branch_high(BRANCH_HIGH[t])
            for i in range(NT):
                act.wait_ge(t_full, TT[("at", i)] + 1)
                run(a_hi[:, :].rearrange("p (k s) -> p k s", k=4)[:, :, i * P:(i + 1) * P],
                    bank[4 + TT[("at", i)] % 2][:, :].rearrange("p (k s) -> p k s", k=4), ACT.Copy).then_inc(at_hi_done, 1)
            for e in range(KC):
                if e + 2 < KC:
                    branch_high(e + 2)
                n, c = e // 4, slice(UNIT * (e % 4), UNIT * (e % 4 + 1))
                if e % 4 == 0:
                    arrived(act, f"w2o{n}")
                run(w2o_hi[n][:, c], wring[:, SLOT * n:SLOT * (n + 1)][:, c], ACT.Copy).then_inc(w2o_hi_done, 1)
                act.wait_ge(mix_done, e + 1)
                run(m_hi[e][:, :], gaT[:, e, :], ACT.Copy).then_inc(m_hi_done, 1)
            NF = DFF // P

            def unit_raw(m):
                if m < NF:
                    return slot(f"f1_{m // 4}")[:, :, (m % 4) * P:(m % 4 + 1) * P], w_hi[ring3(m)][:, :].rearrange("p (k n) -> p k n", k=KC)
                k = m - NF
                return slot(f"f2_{k // 4}", D)[:, k % 4, :], w_hi[ring3(m)][:, :]

            def unit_hi(m):
                if m % 4 == 0:
                    arrived(act, f"f{1 + m // NF}_{m % NF // 4}")
                if 1 <= m <= 2:
                    act.wait_ge(t_full, TT[("h3", NT - 1, 1)] + 1)
                if m >= NF + 3:
                    act.wait_ge(unit_used, m - NF - 2)
                elif m >= 3:
                    act.wait_ge(a_full, AT[("ff", m - 3)] + 1)
                src, dst = unit_raw(m)
                run(dst, src, ACT.Copy).then_inc(w_hi_done, 1)

            for i in range(NT):
                squares(2 * NT, R_OUT2, i)
                if i >= 1:
                    input_high("h3", i - 1)
                if i == 2:
                    unit_hi(0)
            input_high("h3", NT - 1)

            for m in range(1, 3):
                unit_hi(m)
            def ff_high(k):
                run(ff_hi[k % 3][:, :], ffT[:, k, :], ACT.Copy).then_inc(ff_hi_done, 1)

            for c in range(NF):
                if c + 3 < NF + 1:
                    unit_hi(c + 3)
                if c == NF - 1:
                    ff_high(0)
                take(("ff", c))
            for k in range(NF):
                if k == 1:
                    act.wait_ge(a_full, A2_END + NF)
                if k >= 3:
                    act.wait_ge(unit_used, k - 2)
                if k > 0:
                    ff_high(k)
                if NF + k + 1 < 2 * NF:
                    unit_hi(NF + k + 1)
            for i in range(NT):
                act.wait_ge(ss_done, 3 * NT + i)
                act.wait_ge(r_free, R_FF + 2 * (i + 1))
                run(junk[:, :], x[:, i, :], ACT.Square, accum_out=ssf[:, i:i + 1]).then_inc(ss_done, 1)
                act.wait_ge(ms_done, 3 * NT + i + 1)
                run(rsf[:, i:i + 1], ssf[:, i:i + 1], ACT.Sqrt).then_inc(sq_done, 1)

        @block.vector
        def _(dve):
            v = nc.vector
            count = [0]

            def step(ins):
                count[0] += 1
                ins.then_inc(dve_step, 1)
                dve.wait_ge(dve_step, count[0])

            def norm(base, i, xn):
                dve.wait_ge(ss_done, base + i + 1)
                v.tensor_scalar(ss[:, base + i:base + i + 1], ss[:, base + i:base + i + 1], 1.0 / D, EPS, ALU.mult, ALU.add)\
                    .then_inc(ms_done, 1)
                dve.wait_ge(sq_done, base + i + 1)
                step(v.reciprocal(rs[:, base + i:base + i + 1], rs[:, base + i:base + i + 1]))
                v.tensor_scalar(xn[:, i, :], x[:, i, :], rs[:, base + i:base + i + 1], None, ALU.mult).then_inc(xn_done, 1)

            def take_sums(g):
                n = TT[("sum", g)]
                dve.wait_ge(t_full, n + 1)
                by = 1.0 / HD if g[0] == "k" else 1.0 / HD / SCALE ** 2
                v.tensor_scalar(inv[g], bank[4 + n % 2][0:NH, :], by, EPS * HD * by, ALU.mult, ALU.add).then_inc(t_free, 1)

            def invert(g, n):
                dve.wait_ge(inv_root, ORDER.index(g) + 1)
                part = inv[g][:, n * S // 2:(n + 1) * S // 2]
                v.reciprocal(part, part).then_inc(inv_done, 1)

            def scale_heads(g, c):
                n = TT[("spread", g, c)]
                gain = {"qb": V_QB, "kb": V_KB, "qa": V_QA, "ka": V_KA}[g]
                dve.wait_ge(t_full, n + 1)
                v.scalar_tensor_tensor(qkT[g][:, c, :], qkT[g][:, c, :], small[:, gain:gain + 1], bank[4 + n % 2][:, :], ALU.mult, ALU.mult)\
                    .then_inc(t_free, 1)

            def attention(t, steps, base, bias, finish, logits, probsT):
                if t < NS:
                    i, br, h = steps[t]
                    n = (i + 1) * P
                    b = bias(t)
                    dve.wait_ge(s_full, base + t + 1)
                    if t >= 3:
                        dve.wait_ge(t_full, TT[("pt", base + t - 3)] + 1)
                    v.tensor_tensor_reduce(logits[t % 3][:, 0:n], bank[2 + t % 2][:, 0:n], b, -1.0, BIG, ALU.add, ALU.min,
                                           negm[:, t:t + 1]).then_inc(l_done, 1)
                u = t - 2
                if 0 <= u < NS:
                    k = TT[("pt", base + u)]
                    n = (steps[u][0] + 1) * P
                    dve.wait_ge(t_full, k + 1)
                    if u >= 2:
                        dve.wait_ge(pv_done, base + u - 1)
                    v.tensor_copy(probsT[u % 2][:, 0:n], bank[4 + k % 2][:, 0:n]).then_inc(t_free, 1)
                if t >= 10 and (t - 3) % NH == NH - 1:
                    o = (t - 3) // NH
                    dve.wait_ge(pv_done, base + NH * (o + 1))
                    finish(o)

            dve.wait_ge(consts_in, 32)
            def low(u):
                dve.wait_ge(u_hi_done, u + 1)
                cols = unit_cols(u)
                v.tensor_tensor(u_lo[u % RAW_UNITS][:, 0:cols], raw_unit(u),
                                u_hi[u % HI_UNITS][:, 0:cols].bitcast(F32), ALU.subtract).then_inc(u_lo_done, 1)

            def branch_low(e):
                dve.wait_ge(br_hi_done, e + 1)
                v.tensor_tensor(br_lo[e % 3][:, :], wring[:, branch_at[e % 3]:branch_at[e % 3] + UNIT],
                                br_hi[e % 2][:, :].bitcast(F32), ALU.subtract).then_inc(br_lo_done, 1)

            def take_halves(name, i, factor, lo):
                tmps = [h_tmp[name][:, 512 * c:512 * c + 512].rearrange("p (k s) -> p k s", k=4) for c in range(2)]
                for c in range(2):
                    n = TT[(name, i, c)]
                    if i > 0:
                        dve.wait_ge(h_lo_done, halves(name, i, c) - 1)
                    dve.wait_ge(t_full, n + 1)
                    by = zT[:, 4 * c:4 * c + 4, i * P:(i + 1) * P] if factor is None else \
                        small[:, factor + 4 * c:factor + 4 * c + 4].unsqueeze(2).to_broadcast([P, 4, P])
                    v.tensor_tensor(tmps[c], bank[4 + n % 2][:, :].rearrange("p (k s) -> p k s", k=4), by, ALU.mult).then_inc(t_free, 1)
                for c in range(2):
                    m = halves(name, i, c)
                    dve.wait_ge(h_hi_done, m + 1)
                    part = lambda t: t[:, :].rearrange("p (k s) -> p k s", k=KC)[:, 4 * c:4 * c + 4, i * P:(i + 1) * P]
                    v.tensor_tensor(part(lo), tmps[c], part(h_hi).bitcast(F32), ALU.subtract).then_inc(h_lo_done, 1)

            def add_x(r0, i):
                for n in range(2):
                    r = r0 + 2 * i + n
                    dve.wait_ge(r_full, r + 1)
                    xs = x[:, i, n * 512:(n + 1) * 512]
                    v.tensor_tensor(xs, xs, bank[r % 4][:, :], ALU.add).then_inc(r_free, 1)

            for i in range(NT):
                norm(0, i, xn1)
                if i >= 1:
                    take_halves("h1", i - 1, V_G1, h_lo)
            low(0)
            take_halves("h1", NT - 1, V_G1, h_lo)
            dve.wait_ge(table_in, 48)
            dve.wait_ge(vec_full, 1)
            v.tensor_tensor(vec[:, 0:512], bank[6][0:2 * NH, 0:512], add_sb[:, 0:512], ALU.add)
            v.tensor_tensor(vec[:, 512:VEC], bank[7][0:2 * NH, 0:P], add_sb[:, 512:VEC], ALU.add).then_inc(vec_done, 1)
            for u in range(1, 8):
                low(u)
            dve.wait_ge(t_full, TT[("wi", 0)] + 1)
            v.tensor_copy(wi, bank[4 + TT[("wi", 0)] % 2][:, 0:NT * IDX_HEADS].rearrange("p (i h) -> p i h", i=NT)).then_inc(t_free, 1)
            dve.wait_ge(t_free, TT[("wi", 0)] + 1)

            dve.wait_ge(a_free, AT[("wi", 0)] + 1)
            for i in range(1, NT):
                n = (i + 1) * P
                s = score_of[i]
                for h in range(IDX_HEADS):
                    r = 4 * (i - 1) + h
                    dve.wait_ge(a_free, AT[("rel", i, h)] + 1)
                    if h == 0:
                        ins = v.tensor_scalar(s, rels[r % 2][:, 0:n], wi[:, i, 0:1], None, ALU.mult)
                    else:
                        ins = v.scalar_tensor_tensor(s, rels[r % 2][:, 0:n], wi[:, i, h:h + 1], s, ALU.mult, ALU.add)
                    ins.then_inc(rel_free, 1)
                    dve.wait_ge(rel_free, r + 1)
                step(v.tensor_tensor(s[:, i * P:n], s[:, i * P:n], consts[:, C_DIAG:C_DIAG + P], ALU.add))
            rounds = [i for i in range(1, NT) for _ in range(TOPK // 8)]

            def search(n0, n1):
                for i in rounds[n0:n1]:
                    step(v.max(top8, score_of[i]))
                    step(v.match_replace(score_of[i], top8, score_of[i], TAKEN))

            first = unit_of[("kb", 0)] + HI_UNITS
            per_unit = (4, 4, 4, 3, 3, 3, 3, 3, 3, 3, 2, 1)
            assert sum(per_unit) == EARLY_ROUNDS
            for m in range(12):
                if m == 5:
                    take_sums("kb")
                if m == 9:
                    take_sums("qb")
                if m >= 10:
                    for c in (2 * m - 20, 2 * m - 19):
                        scale_heads("kb", c)
                low(first + m)
                if m in (7, 8):
                    invert("kb", m - 7)
                search(sum(per_unit[:m]), sum(per_unit[:m + 1]))
            for m in range(3):
                if m == 2:
                    for c in range(2):
                        scale_heads("qb", c)
                low(first + 12 + m)
                if m < 2:
                    invert("qb", m)
            for c in range(2, 4):
                scale_heads("qb", c)

            combo_of = {t: c for c, t in enumerate(combos)}

            def bias1(t):
                i, br, h = steps1[t]
                if t in combo_of:
                    dve.wait_ge(combo_done, combo_of[t] + 1)
                    return combo[combo_of[t] % 2][:, 0:(i + 1) * P]
                return strips[:, (h if br == "a" else NH + h), (NT - 1 - i) * P:S]

            def finish1(o):
                i, br, _ = steps1[NH * o]
                dve.wait_ge(e_done, NH * (o + 1))
                step(v.reciprocal(gr, den[:, NH * o:NH * (o + 1)]))
                by_head = lambda a: a.rearrange("p (h d) -> p h d", h=NH)
                v.tensor_tensor(by_head(outs_of[br][:, i, :]), by_head(bank[6 + o % 2][:, :]), gr.unsqueeze(2).to_broadcast([P, NH, HD]), ALU.mult)\
                    .then_inc(o_free, 1)

            def wo_low(m):
                n, c = m // 4, slice(UNIT * (m % 4), UNIT * (m % 4 + 1))
                dve.wait_ge(wo_hi_done, m + 1)
                v.tensor_tensor(wo_lo[n][:, c], wo_place[f"wo{n}"][:, c], wo_hi[n][:, c].bitcast(F32), ALU.subtract).then_inc(wo_lo_done, 1)

            dve.wait_ge(strips_in, 16 * P // COPIES)
            for t in range(NS + 3):
                attention(t, steps1, 0, bias1, finish1, logits1, probsT1)
                if t in SUM:
                    take_sums(SUM[t])
                if t in INVERT:
                    invert(*INVERT[t])
                for part in SPREAD.get(t, []):
                    scale_heads(*part)
                if 1 <= t < MASKS:
                    search(EARLY_ROUNDS + t - 1, EARLY_ROUNDS + t)
                if t == MASKS:
                    for i in range(1, NT):
                        v.tensor_scalar(mask_of[i], score_of[i], TAKEN, NEG, ALU.not_equal, ALU.mult).then_inc(masks_done, 1)
                    dve.wait_ge(masks_done, NT - 1)
                if t in LOW1:
                    low(LOW1[t])
                if t in WO_LOW:
                    wo_low(WO_LOW[t])

            for i in range(2):
                take_halves("mx", i, None, h_lo)
                for m in range(4 + 2 * i, 6 + 2 * i):
                    wo_low(m)
            dve.wait_ge(x_in, 16 * NT)
            for i in range(NT):
                add_x(0, i)
                if i < 2:
                    take_halves("mx", i + 2, None, h_lo)
                if i == 3:
                    low(U2)
                norm(NT, i, xn2)
                if i >= 1 and i < NT - 1:
                    take_halves("h2", i - 1, V_G2, h_lo)
            take_halves("h2", NT - 2, V_G2, h_lo)
            low(U2 + 1)
            take_halves("h2", NT - 1, V_G2, h_lo)
            for u in range(2, 11):
                low(U2 + u)

            def rope(view, heads, cos, sin, n=P, tiles=NT):
                x1, x2 = view[:, :, :, 0:ROT], view[:, :, :, ROT:2 * ROT]
                size = tiles * heads * ROT
                tmp = [r[0:n, 0:size].rearrange("p (i h d) -> p i h d", i=tiles, h=heads) for r in rope_tmp]
                v.tensor_tensor(tmp[0], x1, cos, ALU.mult)
                v.tensor_tensor(tmp[1], x2, sin, ALU.mult)
                v.tensor_tensor(tmp[2], x2, cos, ALU.mult)
                step(v.tensor_tensor(tmp[3], x1, sin, ALU.mult))
                v.tensor_tensor(x1, tmp[0], tmp[1], ALU.subtract)
                return v.tensor_tensor(x2, tmp[2], tmp[3], ALU.add)

            def angles(at, heads):
                return consts[:, at:at + NT * ROT].rearrange("p (i d) -> p i d", i=NT).unsqueeze(2).to_broadcast([P, NT, heads, ROT])

            dve.wait_ge(a_free, AT[("kwvg", NT - 1)] + 1)
            for m in (2, 3):
                last = rope(dup[:, m, :, :, :, :].rearrange("p i g r d -> p i (g r) d"), 4, angles(C_COS, 4), angles(C_SIN, 4))
                if m == 2:
                    step(last)
            last.then_inc(rope_done, 1)
            dve.wait_ge(rope_done, 1)
            for u in range(11, 15):
                low(U2 + u)
            for m in range(2):
                pe_at = (V_PEK, V_PEV)[m]
                for g in range(G2):
                    n = TT[("kv", m, g)]
                    dve.wait_ge(t_full, n + 1)
                    for half in range(2):
                        rows = slice(half * HD, (half + 1) * HD)
                        src = bank[4 + n % 2][rows, 16 * half:16 * half + NC * 16].rearrange("p (c j) -> p c j", j=16)
                        pos = small[rows, pe_at:pe_at + 16].unsqueeze(1).to_broadcast([HD, NC, 16])
                        last = v.tensor_tensor(blk[m][rows, g, :, :], src, pos, ALU.add)
                        if half == 0:
                            step(last)
                    last.then_inc(t_free, 1)
            for m, br in ((2, "s"), (3, "w")):
                for g in range(G2):
                    n = TT[("kv", m, g)]
                    dve.wait_ge(t_full, n + 1)
                    v.tensor_copy(kT2[br][:, g, :], bank[4 + n % 2][:, :]).then_inc(t_free, 1)
            low(U2 + 15)
            dve.wait_ge(a_free, AT[("q2", NT - 1)] + 1)
            q2h = q2.rearrange("p (i h d) -> p i h d", i=NT, h=NH)
            rope(q2h, NH, angles(C_COS, NH), angles(C_SIN, NH)).then_inc(rope_done, 1)
            for u in range(16, 20):
                low(U2 + u)
            for c in range(4):
                n = TT[("q2", c)]
                dve.wait_ge(t_full, n + 1)
                v.tensor_scalar(q2T[:, c, :], bank[4 + n % 2][:, :], SCALE, None, ALU.mult).then_inc(t_free, 1)
            for u in range(20, 24):
                low(U2 + u)
            dve.wait_ge(a_free, AT[("kcmp", 0)] + 1)
            dve.wait_ge(rope_done, 2)
            pcos = consts[0:NC, C_PCOS:C_PCOS + ROT].unsqueeze(1).unsqueeze(1).to_broadcast([NC, 1, 4, ROT])
            psin = consts[0:NC, C_PSIN:C_PSIN + ROT].unsqueeze(1).unsqueeze(1).to_broadcast([NC, 1, 4, ROT])
            rope(kcn[0:NC, :, :, :].rearrange("p g r d -> p (g r) d").unsqueeze(1), 4, pcos, psin, NC, 1).then_inc(kcn_done, 1)
            for u in range(24, 27):
                low(U2 + u)
            n = TT[("kcT", 0)]
            dve.wait_ge(t_full, n + 1)
            dve.wait_ge(zeroed, 1)
            v.tensor_copy(kcT[:, :, 0:NC], bank[4 + n % 2][:, 0:G2 * NCP].rearrange("p (g c) -> p g c", g=G2)[:, :, 0:NC]).then_inc(t_free, 1)
            low(U2 + 27)
            quads = lambda a: a.rearrange("p (i m) c -> p i m c", i=NT)
            per_tile = lambda at: consts[:, at:at + NT * NCP].rearrange("p (i c) -> p i c", i=NT).unsqueeze(2).to_broadcast([P, NT, NH // 2, NCP])
            for n in range(2):
                e = ec_of[n]
                m = cm[:, 16 * n:16 * n + 16]
                dve.wait_ge(cs_full, n + 1)
                step(v.tensor_tensor(quads(e), bank[6 + n][:, :].rearrange("p (i m c) -> p i m c", i=NT, c=NCP), per_tile(C_CADD), ALU.add))
                step(v.tensor_reduce(m, e, AX.X, ALU.max))
                v.tensor_tensor(e, e, m.unsqueeze(2).to_broadcast([P, 16, NCP]), ALU.subtract).then_inc(cl_done, 1)
            for n in range(2):
                dve.wait_ge(ce_done, n + 1)
                v.tensor_tensor(quads(ec_of[n]), quads(ec_of[n]), per_tile(C_C01), ALU.mult).then_inc(cp_done, 1)
            dve.wait_ge(cp_done, 2)
            step(v.tensor_reduce(cden, ec.rearrange("p (m c) -> p m c", c=NCP), AX.X, ALU.add))
            step(v.tensor_scalar(cden, cden, 1e-30, None, ALU.max))
            step(v.reciprocal(cden, cden))
            cdh = cden.rearrange("p (i h) -> p i h", i=NT)
            step(v.tensor_tensor(cdh, cdh, gates[:, :, 0:NH], ALU.mult))
            for n in range(2):
                k = TT[("ec", n)]
                dve.wait_ge(t_full, k + 1)
                v.tensor_copy(ecT[:, 512 * n:512 * n + 512], bank[4 + k % 2][:, :]).then_inc(t_free, 1)
            heads = lambda a: a.rearrange("p (h d) -> p h d", h=NH)
            for i in range(NT):
                dve.wait_ge(co_full, i + 1)
                v.tensor_tensor(heads(attn[:, i, :]), heads(bank[6 + i % 2][:, :]),
                                cden[:, NH * i:NH * (i + 1)].unsqueeze(2).to_broadcast([P, NH, HD]), ALU.mult).then_inc(co_free, 1)

            def bias2(t):
                return strip0[:, (NT - 1 - steps2[t][0]) * P:S]

            def finish2(o):
                i, br, _ = steps2[NH * o]
                dve.wait_ge(e_done, NS + NH * (o + 1))
                at = NH if br == "s" else 2 * NH
                step(v.reciprocal(gr, den2[:, NH * o:NH * (o + 1)]))
                step(v.tensor_tensor(gr, gr, gates[:, i, at:at + NH], ALU.mult))
                part = heads(junk[:, 0:512])
                v.tensor_tensor(part, heads(bank[6 + o % 2][:, :]), gr.unsqueeze(2).to_broadcast([P, NH, HD]), ALU.mult).then_inc(o_free, 1)
                dve.wait_ge(o_free, NS // NH + o + 1)
                step(v.tensor_tensor(attn[:, i, :], attn[:, i, :], junk[:, 0:512], ALU.add))

            dve.wait_ge(co_free, NT)
            for t in range(NS + 3):
                attention(t, steps2, NS, bias2, finish2, logits2, probsT2)
                if t in (1, 2):
                    low(unit_of[("gb", 3 + t)])
                if 3 <= t < 7:
                    g = t - 3
                    dve.wait_ge(a_free, AT[("pm", g)] + 1)
                    v.tensor_tensor(pm_lo[:, g * S:(g + 1) * S], pmT[:, g, :], pm_hi[:, g * S:(g + 1) * S].bitcast(F32), ALU.subtract)\
                        .then_inc(pm_lo_done, 1)
                if t - 3 in GB_HIGH:
                    low(GB_HIGH[t - 3])
                if t - 3 in BRANCH_HIGH:
                    branch_low(BRANCH_HIGH[t - 3])
            for i in range(NT):
                n = TT[("at", i)]
                dve.wait_ge(at_hi_done, i + 1)
                part = lambda a: a[:, :].rearrange("p (k s) -> p k s", k=4)
                v.tensor_tensor(part(a_lo)[:, :, i * P:(i + 1) * P], part(bank[4 + n % 2]),
                                part(a_hi)[:, :, i * P:(i + 1) * P].bitcast(F32), ALU.subtract).then_inc(t_free, 1)
            R = 2 * NT
            for e in range(KC):
                for n, g in enumerate((gaT, gbT)):
                    r = R + 2 * e + n
                    dve.wait_ge(r_full, r + 1)
                    v.tensor_tensor(g[:, e, :], g[:, e, :], bank[r % 4][:, :], ALU.mult).then_inc(r_free, 1)
                dve.wait_ge(r_free, R + 2 * e + 2)
                v.tensor_tensor(gaT[:, e, :], gaT[:, e, :], gbT[:, e, :], ALU.add).then_inc(mix_done, 1)
                if e + 2 < KC:
                    branch_low(e + 2)
                n, c = e // 4, slice(UNIT * (e % 4), UNIT * (e % 4 + 1))
                dve.wait_ge(w2o_hi_done, e + 1)
                v.tensor_tensor(w2o_lo[n][:, c], wring[:, SLOT * n:SLOT * (n + 1)][:, c], w2o_hi[n][:, c].bitcast(F32), ALU.subtract)\
                    .then_inc(w2o_lo_done, 1)
                dve.wait_ge(m_hi_done, e + 1)
                v.tensor_tensor(m_lo[e][:, :], gaT[:, e, :], m_hi[e][:, :].bitcast(F32), ALU.subtract).then_inc(m_lo_done, 1)
            R += 2 * KC

            NF = DFF // P

            def unit_lo(m):
                dve.wait_ge(w_hi_done, m + 1)
                if m < NF:
                    src, cut = slot(f"f1_{m // 4}")[:, :, (m % 4) * P:(m % 4 + 1) * P], lambda t: t[:, :].rearrange("p (k n) -> p k n", k=KC)
                else:
                    src, cut = slot(f"f2_{(m - NF) // 4}", D)[:, (m - NF) % 4, :], lambda t: t[:, :]
                v.tensor_tensor(cut(w_lo[ring3(m)]), src, cut(w_hi[ring3(m)]).bitcast(F32), ALU.subtract).then_inc(w_lo_done, 1)

            for i in range(NT):
                add_x(R, i)
                norm(2 * NT, i, xn3)
                if i >= 1:
                    take_halves("h3", i - 1, V_G3, h3_lo)
                if i == 2:
                    unit_lo(0)
            take_halves("h3", NT - 1, V_G3, h3_lo)
            R += 2 * NT

            for m in range(1, NF):
                unit_lo(m)
            for k in range(NF):
                if k == 0:
                    unit_lo(NF)
                dve.wait_ge(ff_hi_done, k + 1)
                v.tensor_tensor(ff_lo[k % 3][:, :], ffT[:, k, :], ff_hi[k % 3][:, :].bitcast(F32), ALU.subtract).then_inc(ff_lo_done, 1)
                if NF + k + 1 < 2 * NF:
                    unit_lo(NF + k + 1)
            for i in range(NT):
                for n in range(2):
                    r = R + 2 * i + n
                    dve.wait_ge(r_full, r + 1)
                    xs = x[:, i, n * 512:(n + 1) * 512]
                    v.tensor_tensor(xs, xs, bank[2 * i + n][:, :], ALU.add).then_inc(r_free, 1)
            dve.wait_ge(gfin_in, 16)
            for i in range(NT):
                dve.wait_ge(ss_done, 3 * NT + i + 1)
                v.tensor_scalar(ssf[:, i:i + 1], ssf[:, i:i + 1], 1.0 / D, EPS, ALU.mult, ALU.add).then_inc(ms_done, 1)
                dve.wait_ge(sq_done, 3 * NT + i + 1)
                step(v.reciprocal(rsf[:, i:i + 1], rsf[:, i:i + 1]))
                v.scalar_tensor_tensor(x[:, i, :], x[:, i, :], rsf[:, i:i + 1], gfin, ALU.mult, ALU.mult).then_inc(y_done, 1)

        @block.gpsimd
        def _(pool):
            g = nc.gpsimd
            pool.wait_ge(vec_done, 1)
            pool.dma_start(copies.rearrange("m h x -> h m x"), vec.unsqueeze(1).to_broadcast([2 * NH, COPIES, VEC]))\
                .then_inc(vec_out, 16)
            pool.wait_ge(vec_out, 16)
            pitch = 2 * NH * VEC
            for p in range(0, P, COPIES):
                diagonal = bass.AP(copies.tensor, P - 1 - p, [[pitch - 1, COPIES], [VEC, 2 * NH], [1, S]])
                pool.dma_start(strips[p:p + COPIES, :, :], diagonal).then_inc(strips_in, 16)
            pool.wait_ge(strips_in, 16 * P // COPIES)
            pool.wait_ge(masks_done, NT - 1)
            pool.wait_ge(t_free, TT[("spread", "qa", 3)] + 1)
            for c, t in enumerate(combos):
                i, _, h = steps1[t]
                if c >= 2:
                    pool.wait_ge(l_done, combos[c - 2] + 1)
                g.tensor_tensor(combo[c % 2][:, 0:(i + 1) * P], strips[:, h, (NT - 1 - i) * P:S], mask_of[i], ALU.add)\
                    .then_inc(combo_done, 1)
            pool.wait_ge(xn_done, 2 * NT)
            pool.wait_ge(r_full, R_BRANCH)
            pool.wait_ge(t_free, TT[("mx", NT - 1, 1)] + 1)
            for z in (hidk, hidv, kcT):
                g.memset(z, 0.0)
            g.memset(vdiag, 0.0).then_inc(zeroed, 1)
            chain = [0]

            def link(ins):
                chain[0] += 1
                ins.then_inc(pool_chain, 1)
                pool.wait_ge(pool_chain, chain[0])

            for n, width in enumerate(POOL_WINDOWS):
                pool.wait_ge(a_free, AT[("pool", n)] + 1)
                src, shift, k = uT[:, n, :], 1, 0
                while shift < width:
                    dst = ptmp[k % 2]
                    g.tensor_copy(dst[:, 0:shift], src[:, 0:shift])
                    link(g.tensor_tensor(dst[:, shift:S], src[:, shift:S], src[:, 0:S - shift], ALU.add))
                    src, shift, k = dst, 2 * shift, k + 1
                g.tensor_tensor(src[:, 0:16], src[:, 0:16], consts[:, C_INV + 16 * n:C_INV + 16 * n + 16], ALU.mult)
                link(g.tensor_scalar(src[:, 16:S], src[:, 16:S], 1.0 / width, None, ALU.mult))
                g.tensor_tensor(uT[:, n, :], src, uT[:, n, :], ALU.subtract).then_inc(pooled, 1)
                pool.wait_ge(pooled, n + 1)


_CONSTANTS = ("consts", "onehot", "vec_add", "spread")
_DIRECT = ("x", "rel_bias", "w_in", "w_out", "w_in_2", "cmp_k_w1_2", "cmp_k_w2_2", "cmp_v_w1_2", "cmp_v_w2_2",
           "w_branch_attn_2", "pool_w_2", "w_branch_pool_2", "w_out_2", "w_ff1_2", "w_ff2_2")


def kernel(**inputs):
    from concourse import bacc
    from concourse.bass_utils import run_bass_kernel_spmd

    a = {k: np.asarray(v) for k, v in inputs.items()}
    arrays = dict(zip(_CONSTANTS, shape_constants()))
    for name in _DIRECT:
        arr = a[name]
        arrays[name] = np.ascontiguousarray(arr if name in ("x", "rel_bias") else arr[0])
    arrays["norm_final_2"] = np.ascontiguousarray(a["norm_final_2"].reshape(1, D))
    per_chunk = lambda g: g.reshape(-1, P).T
    per_head = lambda g: np.concatenate([g[0], g[0]])[:, None]
    blocks = lambda pe: pe[0].reshape(2, 16, HD).transpose(0, 2, 1).reshape(P, 16)
    arrays["small"] = np.ascontiguousarray(np.concatenate(
        [per_chunk(a["norm_gain"][0]), per_chunk(a["norm_mix_2"][0]), per_chunk(a["norm_mlp_2"][0]),
         per_head(a["q_norm_b"]), per_head(a["k_norm_b"]), per_head(a["q_norm_a"]), per_head(a["k_norm_a"]),
         per_chunk(a["pool_scale_2"][0]), blocks(a["cmp_pe_k_2"]), blocks(a["cmp_pe_v_2"])], axis=1))
    nc = bacc.Bacc("TRN2", target_bir_lowering=False, num_devices=1)
    w = {n: nc.dram_tensor(f"in_{n}", v.shape, F32, kind="ExternalInput").ap() for n, v in arrays.items()}
    out = nc.dram_tensor("out", (1, S, D), F32, kind="ExternalOutput").ap()
    build(nc, w, out)
    r = run_bass_kernel_spmd(nc, [{f"in_{n}": v for n, v in arrays.items()}], core_ids=[0])
    return r.results[0]["out"]
```
